# Optimizing a Trainium2 kernel written in Bass

```python
import math
import jax
import jax.numpy as jnp
from jax import lax
import numpy as np

D_MODEL = 1024
BATCH = 1
SEQ = 256
DEPTH = 1

CHUNK = 64
Q_BLOCK = 128
MEM_LEN = 256
MEM_HEADS = 4
MEM_DIM = D_MODEL // MEM_HEADS

FOX_DIM = 64
FOX_W = D_MODEL // 4
FOX_HEADS = FOX_W // FOX_DIM
DIFF_QK_DIM = 32
DIFF_V_DIM = 2 * DIFF_QK_DIM
DIFF_W = D_MODEL // 4
DIFF_HEADS = DIFF_W // DIFF_V_DIM
HGRN_DIM = 128
HGRN_W = D_MODEL - FOX_W - DIFF_W
HGRN_HEADS = HGRN_W // HGRN_DIM

MIX_W = FOX_W + DIFF_W + HGRN_W
IN_SIZES = (FOX_W, FOX_W, FOX_W, FOX_HEADS, DIFF_W, DIFF_W, DIFF_W, HGRN_W, HGRN_W, HGRN_W, HGRN_W)
IN_W = sum(IN_SIZES)

N_EXPERTS = 16
N_GROUPS = 4
EXPERTS_PER_GROUP = N_EXPERTS // N_GROUPS
TOP_K = 2
EXPERT_FF = D_MODEL // 2

ALPHA = (2 * DEPTH) ** 0.25
BETA = (8 * DEPTH) ** -0.25
LN_EPS = 1e-5


def _layer_norm(x, g, b):
    xf = x.astype(jnp.float32)
    mu = jnp.mean(xf, axis=-1, keepdims=True)
    var = jnp.mean(jnp.square(xf - mu), axis=-1, keepdims=True)
    y = (xf - mu) * lax.rsqrt(var + LN_EPS) * g.astype(jnp.float32) + b.astype(jnp.float32)
    return y.astype(x.dtype)

def _rms_norm(x, g):
    xf = x.astype(jnp.float32)
    y = xf * lax.rsqrt(jnp.mean(xf * xf, axis=-1, keepdims=True) + LN_EPS) * g.astype(jnp.float32)
    return y.astype(x.dtype)

def _split_heads(t, n_heads):
    b, s, _ = t.shape
    return t.reshape(b, s, n_heads, -1).transpose(0, 2, 1, 3)

def _merge_heads(t):
    b, h, s, d = t.shape
    return t.transpose(0, 2, 1, 3).reshape(b, s, h * d)

def _to_blocks(t):
    b, h, s = t.shape[:3]
    t = t.reshape((b, h, s // Q_BLOCK, Q_BLOCK) + t.shape[3:])
    return jnp.moveaxis(t, 2, 0)

def _from_blocks(t):
    nb, b, h, q, d = t.shape
    return t.transpose(1, 2, 0, 3, 4).reshape(b, h, nb * q, d)

def _split_columns(proj):
    parts, start = [], 0
    for width in IN_SIZES:
        parts.append(proj[..., start:start + width])
        start += width
    return parts

def _forgetting_attention(q, k, v, log_f):
    s = q.shape[2]
    cum = jnp.cumsum(log_f, axis=-1)
    key_pos = jnp.arange(s)
    query_pos = key_pos.reshape(s // Q_BLOCK, Q_BLOCK)
    scale = FOX_DIM ** -0.5

    def block(args):
        q_blk, c_blk, q_pos = args
        logits = jnp.einsum('bhqd,bhkd->bhqk', q_blk, k).astype(jnp.float32) * scale
        logits = logits + c_blk[..., :, None] - cum[..., None, :]
        logits = jnp.where(key_pos[None, :] <= q_pos[:, None], logits, -jnp.inf)
        p = jax.nn.softmax(logits, axis=-1).astype(v.dtype)
        return jnp.einsum('bhqk,bhkd->bhqd', p, v)

    out = lax.map(block, (_to_blocks(q), _to_blocks(cum), query_pos))
    return _from_blocks(out)

def _differential_attention(q1, q2, k1, k2, v, lam):
    s = q1.shape[2]
    key_chunk = jnp.arange(s) // CHUNK
    query_chunk = key_chunk.reshape(s // Q_BLOCK, Q_BLOCK)
    scale = DIFF_QK_DIM ** -0.5

    def block(args):
        q1b, q2b, qc = args
        visible = key_chunk[None, :] <= qc[:, None]

        def attn_map(qb, kk):
            logits = jnp.einsum('bhqd,bhkd->bhqk', qb, kk).astype(jnp.float32) * scale
            return jax.nn.softmax(jnp.where(visible, logits, -jnp.inf), axis=-1)

        p = attn_map(q1b, k1) - lam * attn_map(q2b, k2)
        return jnp.einsum('bhqk,bhkd->bhqd', p.astype(v.dtype), v)

    out = lax.map(block, (_to_blocks(q1), _to_blocks(q2), query_chunk))
    return _from_blocks(out)

def _hgrn2_recurrence(q, k, log_f, v):
    b, h, s, dk = q.shape
    dv = v.shape[-1]
    n = s // CHUNK

    def chunks(t):
        t = t.astype(jnp.float32)
        return t.reshape(b, h, n, CHUNK, t.shape[-1]).transpose(2, 0, 1, 3, 4)

    pos = jnp.arange(CHUNK)
    causal = (pos[:, None] >= pos[None, :])[None, None, :, :, None]

    def step(state, inp):
        qc, kc, gc, vc = inp
        bc = jnp.cumsum(gc, axis=2)
        rel = jnp.where(causal, bc[:, :, :, None, :] - bc[:, :, None, :, :], -jnp.inf)
        scores = jnp.einsum('bhtd,bhsd,bhtsd->bhts', qc, kc, jnp.exp(rel))
        o = (jnp.einsum('bhts,bhsv->bhtv', scores, vc)
             + jnp.einsum('bhtd,bhdv->bhtv', qc * jnp.exp(bc), state))
        b_last = bc[:, :, -1, :]
        k_dec = kc * jnp.exp(b_last[:, :, None, :] - bc)
        state = jnp.exp(b_last)[..., None] * state + jnp.einsum('bhsd,bhsv->bhdv', k_dec, vc)
        return state, o

    state0 = jnp.zeros((b, h, dk, dv), jnp.float32)
    _, o = lax.scan(step, state0, (chunks(q), chunks(k), chunks(log_f), chunks(v)))
    return o.transpose(1, 2, 0, 3, 4).reshape(b, h, s, dv)

def _hybrid_mixer(x, w_in, fox_fb, lam_q1, lam_k1, lam_q2, lam_k2, lam_init,
                  diff_norm_g, lower_bound, hgrn_norm_g, w_out):
    proj = x @ w_in
    fq, fk, fv, ff, dq, dk, dv, hq, hf, hi, hg = _split_columns(proj)

    log_f = jax.nn.log_sigmoid(ff.astype(jnp.float32) + fox_fb.astype(jnp.float32))
    y_fox = _forgetting_attention(_split_heads(fq, FOX_HEADS), _split_heads(fk, FOX_HEADS),
                                  _split_heads(fv, FOX_HEADS), log_f.transpose(0, 2, 1))

    dq_h = _split_heads(dq, DIFF_HEADS)
    dk_h = _split_heads(dk, DIFF_HEADS)
    lam = (jnp.exp(jnp.sum(lam_q1.astype(jnp.float32) * lam_k1.astype(jnp.float32)))
           - jnp.exp(jnp.sum(lam_q2.astype(jnp.float32) * lam_k2.astype(jnp.float32)))
           + lam_init)
    y_diff = _differential_attention(dq_h[..., :DIFF_QK_DIM], dq_h[..., DIFF_QK_DIM:],
                                     dk_h[..., :DIFF_QK_DIM], dk_h[..., DIFF_QK_DIM:],
                                     _split_heads(dv, DIFF_HEADS), lam)
    y_diff = _rms_norm(y_diff, diff_norm_g) * (1.0 - lam_init)

    f_logit = hf.astype(jnp.float32)
    lb = lower_bound.astype(jnp.float32)
    log_f_h = jnp.logaddexp(jnp.log(lb), jnp.log1p(-lb) + jax.nn.log_sigmoid(f_logit))
    k_h = (1.0 - lb) * jax.nn.sigmoid(-f_logit)
    o = _hgrn2_recurrence(_split_heads(jax.nn.silu(hq), HGRN_HEADS), _split_heads(k_h, HGRN_HEADS),
                          _split_heads(log_f_h, HGRN_HEADS), _split_heads(hi, HGRN_HEADS))
    y_hgrn = _rms_norm(o, hgrn_norm_g) * jax.nn.silu(_split_heads(hg, HGRN_HEADS).astype(jnp.float32))

    y = jnp.concatenate([_merge_heads(y_fox).astype(x.dtype), _merge_heads(y_diff).astype(x.dtype),
                         _merge_heads(y_hgrn).astype(x.dtype)], axis=-1)
    return y @ w_out

def _memory_attention(x, mem, w_q, w_k, w_v, w_o):
    q = _split_heads(x @ w_q, MEM_HEADS)
    k = _split_heads(mem @ w_k, MEM_HEADS)
    v = _split_heads(mem @ w_v, MEM_HEADS)
    logits = jnp.einsum('bhqd,bhkd->bhqk', q, k).astype(jnp.float32) * MEM_DIM ** -0.5
    p = jax.nn.softmax(logits, axis=-1).astype(v.dtype)
    return _merge_heads(jnp.einsum('bhqk,bhkd->bhqd', p, v)) @ w_o

def _grouped_moe(x, router_w, router_b, w1, w3, w2):
    b, s, d = x.shape
    xt = x.reshape(b * s, d)
    n = xt.shape[0]
    scores = jax.nn.sigmoid((xt @ router_w).astype(jnp.float32))
    biased = scores + router_b.astype(jnp.float32)
    grouped = biased.reshape(n, N_GROUPS, EXPERTS_PER_GROUP)
    group_score = jnp.sum(lax.top_k(grouped, TOP_K)[0], axis=-1)
    group_sel = jnp.argmax(group_score, axis=-1)
    in_group = jnp.arange(N_GROUPS)[None, :] == group_sel[:, None]
    masked = jnp.where(in_group[:, :, None], grouped, -jnp.inf).reshape(n, N_EXPERTS)
    _, expert_idx = lax.top_k(masked, TOP_K)
    sel = jnp.take_along_axis(scores, expert_idx, axis=-1)
    gates = sel / jnp.sum(sel, axis=-1, keepdims=True)
    gate_dense = jnp.sum(jax.nn.one_hot(expert_idx, N_EXPERTS, dtype=jnp.float32) * gates[..., None], axis=1)
    out = jnp.zeros_like(xt)
    for e in range(N_EXPERTS):
        hid = jax.nn.silu(xt @ w1[e]) * (xt @ w3[e])
        out = out + gate_dense[:, e, None].astype(xt.dtype) * (hid @ w2[e])
    return out.reshape(b, s, d)

def first_inputs(seed: int = 0) -> dict:
    key = jax.random.key(seed)
    ks = jax.random.split(key, 26)
    f32 = jnp.float32

    def nrm(k, shape, scale):
        return jax.random.normal(k, shape, f32) * scale

    d = D_MODEL
    return {
        'x': nrm(ks[0], (BATCH, SEQ, d), 1.0),
        'mem': nrm(ks[1], (BATCH, MEM_LEN, d), 1.0),
        'ln_in_g': 1.0 + nrm(ks[2], (d,), 0.02),
        'ln_in_b': nrm(ks[3], (d,), 0.02),
        'w_in': nrm(ks[4], (DEPTH, d, IN_W), d ** -0.5),
        'fox_fb': jax.random.uniform(ks[5], (DEPTH, FOX_HEADS), f32, 1.0, 3.0),
        'lam_q1': nrm(ks[6], (DEPTH, DIFF_QK_DIM), 0.1),
        'lam_k1': nrm(ks[7], (DEPTH, DIFF_QK_DIM), 0.1),
        'lam_q2': nrm(ks[8], (DEPTH, DIFF_QK_DIM), 0.1),
        'lam_k2': nrm(ks[9], (DEPTH, DIFF_QK_DIM), 0.1),
        'diff_norm_g': 1.0 + nrm(ks[10], (DEPTH, DIFF_V_DIM), 0.02),
        'hgrn_lb': nrm(ks[11], (DEPTH, HGRN_W), 0.1),
        'hgrn_norm_g': 1.0 + nrm(ks[12], (DEPTH, HGRN_DIM), 0.02),
        'w_out': nrm(ks[13], (DEPTH, MIX_W, d), BETA * MIX_W ** -0.5),
        'mem_wq': nrm(ks[14], (DEPTH, d, d), d ** -0.5),
        'mem_wk': nrm(ks[15], (DEPTH, d, d), d ** -0.5),
        'mem_wv': nrm(ks[16], (DEPTH, d, d), d ** -0.5),
        'mem_wo': nrm(ks[17], (DEPTH, d, d), BETA * d ** -0.5),
        'router_w': nrm(ks[18], (d, N_EXPERTS), d ** -0.5),
        'router_b': nrm(ks[19], (N_EXPERTS,), 0.01),
        'w1': nrm(ks[20], (DEPTH, N_EXPERTS, d, EXPERT_FF), d ** -0.5),
        'w3': nrm(ks[21], (DEPTH, N_EXPERTS, d, EXPERT_FF), d ** -0.5),
        'w2': nrm(ks[22], (DEPTH, N_EXPERTS, EXPERT_FF, d), BETA * EXPERT_FF ** -0.5),
        'ln_g': 1.0 + nrm(ks[23], (DEPTH, 3, d), 0.02),
        'ln_b': nrm(ks[24], (DEPTH, 3, d), 0.02),
    }

def first_block(x, mem, ln_in_g, ln_in_b, w_in, fox_fb, lam_q1, lam_k1, lam_q2, lam_k2,
              diff_norm_g, hgrn_lb, hgrn_norm_g, w_out, mem_wq, mem_wk, mem_wv, mem_wo,
              router_w, router_b, w1, w3, w2, ln_g, ln_b):
    lbs = jax.nn.softmax(hgrn_lb.astype(jnp.float32), axis=0)
    lbs = jnp.cumsum(lbs, axis=0) - lbs[0]
    h = _layer_norm(x, ln_in_g, ln_in_b)
    for i in range(DEPTH):
        lam_init = 0.8 - 0.6 * math.exp(-0.3 * i)
        y = _hybrid_mixer(h, w_in[i], fox_fb[i], lam_q1[i], lam_k1[i], lam_q2[i], lam_k2[i],
                          lam_init, diff_norm_g[i], jnp.maximum(lbs[i], 0.0), hgrn_norm_g[i], w_out[i])
        h = _layer_norm(ALPHA * h + y, ln_g[i, 0], ln_b[i, 0])
        y = _memory_attention(h, mem, mem_wq[i], mem_wk[i], mem_wv[i], mem_wo[i])
        h = _layer_norm(ALPHA * h + y, ln_g[i, 1], ln_b[i, 1])
        y = _grouped_moe(h, router_w, router_b, w1[i], w3[i], w2[i])
        h = _layer_norm(ALPHA * h + y, ln_g[i, 2], ln_b[i, 2])
    return h


DEPTH_2 = 2

HEAD_DIM = 64
N_SLOTS = D_MODEL // HEAD_DIM
A_HEADS = 8
A_LATENT = 128
IDX_HEADS = 8
IDX_DIM = 64
A_TOPK_MAX = 256
B_HEADS = 8
B_KV_HEADS = 2
B_WINDOW = 128
C_HEADS = 16
C_KV_HEADS = 2
CMP_BLOCK = 32
CMP_STRIDE = 16
CMP_HIDDEN = 128
SLC_BLOCK = 64
SLC_COUNT = 8
C_WINDOW = 512
X_HEADS = 4
X_HEAD_DIM = 128
D_FF = 2816
N_EXPERTS_2 = 8
D_FF_EXPERT = 3584
REL_BUCKETS = 32
REL_MAX_DIST = 128
SLC_Q_BLOCK = 32
NEG_INF = -1e30
FORCE_BONUS = 1e6
ALPHA_2 = (2 * DEPTH_2) ** 0.25
BETA_2 = (8 * DEPTH_2) ** -0.25
N_EVEN = (DEPTH_2 + 1) // 2
N_ODD = DEPTH_2 // 2
EVEN_WIDTHS = (A_HEADS * HEAD_DIM, A_LATENT, IDX_HEADS * IDX_DIM, IDX_DIM, IDX_HEADS,
               B_HEADS * HEAD_DIM, B_KV_HEADS * HEAD_DIM, B_KV_HEADS * HEAD_DIM)
EVEN_COLS = sum(EVEN_WIDTHS)
ODD_WIDTHS = (C_HEADS * HEAD_DIM,) + (C_KV_HEADS * HEAD_DIM,) * 6 + (3 * C_HEADS,)
ODD_COLS = sum(ODD_WIDTHS)


def split_cols(a, widths):
    cuts = [int(c) for c in np.cumsum(widths)[:-1]]
    return jnp.split(a, cuts, axis=-1)

def layer_norm(x, g, b):
    xf = x.astype(jnp.float32)
    mu = jnp.mean(xf, -1, keepdims=True)
    var = jnp.mean(jnp.square(xf - mu), -1, keepdims=True)
    return ((xf - mu) * lax.rsqrt(var + LN_EPS)).astype(x.dtype) * g + b

def rms_norm(x, g):
    xf = x.astype(jnp.float32)
    y = xf * lax.rsqrt(jnp.mean(jnp.square(xf), -1, keepdims=True) + LN_EPS)
    return y.astype(x.dtype) * g

def rel_bucket(dist):
    n = jnp.maximum(dist, 0)
    max_exact = REL_BUCKETS // 2
    nf = jnp.maximum(n, 1).astype(jnp.float32)
    log_b = max_exact + (jnp.log(nf / max_exact) / math.log(REL_MAX_DIST / max_exact)
                         * (REL_BUCKETS - max_exact)).astype(jnp.int32)
    return jnp.where(n < max_exact, n, jnp.minimum(log_b, REL_BUCKETS - 1))

def banded_attention(q, k, v, rel_tbl, window, sinks=None):
    B, S, H, D = q.shape
    kvh = k.shape[2]
    g = H // kvh
    pad = -(-window // Q_BLOCK) * Q_BLOCK
    span = pad + Q_BLOCK
    kp = jnp.pad(k, ((0, 0), (pad, 0), (0, 0), (0, 0)))
    vp = jnp.pad(v, ((0, 0), (pad, 0), (0, 0), (0, 0)))
    dist = np.arange(Q_BLOCK)[:, None] + pad - np.arange(span)[None, :]
    band = jnp.asarray((dist >= 0) & (dist < window))
    bias = rel_tbl.astype(jnp.float32)[rel_bucket(jnp.asarray(dist))]
    bias = bias.transpose(2, 0, 1).reshape(kvh, g, Q_BLOCK, span)
    key_off = jnp.arange(span) - pad

    def block(n):
        t0 = n * Q_BLOCK
        qb = lax.dynamic_slice_in_dim(q, t0, Q_BLOCK, 1).reshape(B, Q_BLOCK, kvh, g, D)
        kb = lax.dynamic_slice_in_dim(kp, t0, span, 1)
        vb = lax.dynamic_slice_in_dim(vp, t0, span, 1)
        logits = jnp.einsum('bqkgd,bskd->bkgqs', qb, kb).astype(jnp.float32) * D ** -0.5 + bias
        ok = band & (t0 + key_off >= 0)[None, :]
        logits = jnp.where(ok, logits, NEG_INF)
        if sinks is None:
            p = jax.nn.softmax(logits, axis=-1)
        else:
            s = sinks.astype(jnp.float32).reshape(kvh, g, 1, 1)
            m = jnp.maximum(jnp.max(logits, -1, keepdims=True), s)
            e = jnp.exp(logits - m)
            p = e / (jnp.sum(e, -1, keepdims=True) + jnp.exp(s - m))
        o = jnp.einsum('bkgqs,bskd->bqkgd', p.astype(v.dtype), vb)
        return o.reshape(B, Q_BLOCK, H, D)

    out = lax.map(block, jnp.arange(S // Q_BLOCK))
    return jnp.moveaxis(out, 0, 1).reshape(B, S, H, D)

def dsa_attention(q_a, c_kv, q_i, k_i, w_i, ckv_gain, w_uk, w_uv, rel_tbl):
    B, S, _ = q_a.shape
    topk = min(A_TOPK_MAX, S // 4)
    q_lat = jnp.einsum('bshd,hdc->bshc', q_a.reshape(B, S, A_HEADS, HEAD_DIM), w_uk)
    c = rms_norm(c_kv, ckv_gain)
    qi = q_i.reshape(B, S, IDX_HEADS, IDX_DIM)
    wi = w_i * IDX_HEADS ** -0.5
    tbl = rel_tbl.astype(jnp.float32)
    kpos = jnp.arange(S)

    def block(n):
        t0 = n * Q_BLOCK
        qpos = t0 + jnp.arange(Q_BLOCK)
        qi_b = lax.dynamic_slice_in_dim(qi, t0, Q_BLOCK, 1)
        wi_b = lax.dynamic_slice_in_dim(wi, t0, Q_BLOCK, 1)
        ql_b = lax.dynamic_slice_in_dim(q_lat, t0, Q_BLOCK, 1)
        act = jax.nn.relu(jnp.einsum('bqhd,bsd->bqhs', qi_b, k_i) * IDX_DIM ** -0.5)
        score = jnp.einsum('bqh,bqhs->bqs', wi_b, act).astype(jnp.float32)
        score = jnp.where(kpos[None, :] <= qpos[:, None], score, NEG_INF)
        _, sel = lax.top_k(score, topk)
        c_sel = jax.vmap(lambda cb, sb: cb[sb])(c, sel)
        dist = qpos[None, :, None] - sel
        bias = tbl[rel_bucket(dist)].transpose(0, 1, 3, 2)
        lg = jnp.einsum('bqhc,bqkc->bqhk', ql_b, c_sel).astype(jnp.float32) * HEAD_DIM ** -0.5 + bias
        lg = jnp.where((dist >= 0)[:, :, None, :], lg, NEG_INF)
        p = jax.nn.softmax(lg, axis=-1).astype(c.dtype)
        o_lat = jnp.einsum('bqhk,bqkc->bqhc', p, c_sel)
        return jnp.einsum('bqhc,hcd->bqhd', o_lat, w_uv)

    out = lax.map(block, jnp.arange(S // Q_BLOCK))
    return jnp.moveaxis(out, 0, 1).reshape(B, S, A_HEADS, HEAD_DIM)

def compress_blocks(kv, pe, w1, w2):
    B, S, G, D = kv.shape
    n_cmp = (S - CMP_BLOCK) // CMP_STRIDE + 1
    idx = np.arange(n_cmp)[:, None] * CMP_STRIDE + np.arange(CMP_BLOCK)[None, :]
    blk = kv[:, idx] + pe[None, None, :, None, :]
    blk = blk.transpose(0, 1, 3, 2, 4).reshape(B, n_cmp, G, CMP_BLOCK * D)
    return jax.nn.gelu(blk @ w1) @ w2

def nsa_attention(q, k_cmp, v_cmp, k_slc, v_slc, k_win, v_win, gate_logits,
                  pe_k, w1_k, w2_k, pe_v, w1_v, w2_v, rel_tbl):
    B, S, H, D = q.shape
    G = C_KV_HEADS
    hpg = H // G
    qg = q.reshape(B, S, G, hpg, D)
    scale = D ** -0.5
    tbl = rel_tbl.astype(jnp.float32)
    pos = np.arange(S)

    n_cmp = (S - CMP_BLOCK) // CMP_STRIDE + 1
    kc = compress_blocks(k_cmp, pe_k, w1_k, w2_k)
    vc = compress_blocks(v_cmp, pe_v, w1_v, w2_v)
    cmp_end = np.arange(n_cmp) * CMP_STRIDE + CMP_BLOCK - 1
    dist_c = pos[:, None] - cmp_end[None, :]
    valid_c = jnp.asarray(dist_c >= 0)
    bias_c = tbl[rel_bucket(jnp.asarray(dist_c))].transpose(2, 0, 1).reshape(G, hpg, S, n_cmp)
    lg = jnp.einsum('bsghd,bngd->bghsn', qg, kc).astype(jnp.float32) * scale + bias_c
    p_cmp = jax.nn.softmax(jnp.where(valid_c, lg, NEG_INF), axis=-1) * valid_c
    o_cmp = jnp.einsum('bghsn,bngd->bsghd', p_cmp.astype(vc.dtype), vc).reshape(B, S, H, D)

    n_slc = S // SLC_BLOCK
    n_sel = min(SLC_COUNT, n_slc)
    cs = np.arange(n_cmp)[:, None] * CMP_STRIDE
    ss = np.arange(n_slc)[None, :] * SLC_BLOCK
    overlap = jnp.asarray(((cs < ss + SLC_BLOCK) & (cs + CMP_BLOCK > ss)).astype(np.float32))
    p_slc = jnp.einsum('bghsn,nj->bgsj', p_cmp, overlap)
    blk = pos // SLC_BLOCK
    jj = np.arange(n_slc)
    forced = (jj[None, :] == 0) | (jj[None, :] == blk[:, None]) | (jj[None, :] == blk[:, None] - 1)
    admissible = jj[None, :] * SLC_BLOCK <= pos[:, None]
    score = jnp.where(jnp.asarray(admissible),
                      p_slc + FORCE_BONUS * jnp.asarray(forced.astype(np.float32)), NEG_INF)
    _, sel = lax.top_k(score, n_sel)

    kb = k_slc.reshape(B, n_slc, SLC_BLOCK, G, D).transpose(0, 3, 1, 2, 4)
    vb = v_slc.reshape(B, n_slc, SLC_BLOCK, G, D).transpose(0, 3, 1, 2, 4)
    bi = jnp.arange(B)[:, None, None, None]
    gi = jnp.arange(G)[None, :, None, None]
    tbl_g = tbl.reshape(REL_BUCKETS, G, hpg).transpose(1, 0, 2)
    in_blk = jnp.arange(SLC_BLOCK)
    n_keys = n_sel * SLC_BLOCK

    def slc_block(n):
        t0 = n * SLC_Q_BLOCK
        qpos = t0 + jnp.arange(SLC_Q_BLOCK)
        qb = lax.dynamic_slice_in_dim(qg, t0, SLC_Q_BLOCK, 1)
        sb = lax.dynamic_slice_in_dim(sel, t0, SLC_Q_BLOCK, 2)
        ks = kb[bi, gi, sb].reshape(B, G, SLC_Q_BLOCK, n_keys, D)
        vs = vb[bi, gi, sb].reshape(B, G, SLC_Q_BLOCK, n_keys, D)
        kpos = (sb[..., None] * SLC_BLOCK + in_blk).reshape(B, G, SLC_Q_BLOCK, n_keys)
        dist = qpos[None, None, :, None] - kpos
        bias = tbl_g[gi, rel_bucket(dist)].transpose(0, 1, 4, 2, 3)
        lg2 = jnp.einsum('bqghd,bgqsd->bghqs', qb, ks).astype(jnp.float32) * scale + bias
        lg2 = jnp.where((dist >= 0)[:, :, None], lg2, NEG_INF)
        p = jax.nn.softmax(lg2, axis=-1).astype(vs.dtype)
        o = jnp.einsum('bghqs,bgqsd->bqghd', p, vs)
        return o.reshape(B, SLC_Q_BLOCK, H, D)

    o_slc = lax.map(slc_block, jnp.arange(S // SLC_Q_BLOCK))
    o_slc = jnp.moveaxis(o_slc, 0, 1).reshape(B, S, H, D)

    o_win = banded_attention(q, k_win, v_win, rel_tbl, C_WINDOW)

    gt = jax.nn.sigmoid(gate_logits).reshape(B, S, H, 3)
    return gt[..., 0:1] * o_cmp + gt[..., 1:2] * o_slc + gt[..., 2:3] * o_win

def even_mixer(x, w_in, ckv_gain, w_uk, w_uv, sinks, w_out, rel_table):
    B, S, _ = x.shape
    q_a, c_kv, q_i, k_i, w_i, q_b, k_b, v_b = split_cols(x @ w_in, EVEN_WIDTHS)
    o_a = dsa_attention(q_a, c_kv, q_i, k_i, w_i, ckv_gain, w_uk, w_uv, rel_table[:, :A_HEADS])
    o_b = banded_attention(q_b.reshape(B, S, B_HEADS, HEAD_DIM),
                           k_b.reshape(B, S, B_KV_HEADS, HEAD_DIM),
                           v_b.reshape(B, S, B_KV_HEADS, HEAD_DIM),
                           rel_table[:, A_HEADS:A_HEADS + B_HEADS], B_WINDOW, sinks)
    o = jnp.concatenate([o_a.reshape(B, S, -1), o_b.reshape(B, S, -1)], axis=-1)
    return o @ w_out

def odd_mixer(x, w_in, pe_k, w1_k, w2_k, pe_v, w1_v, w2_v, w_out, rel_table):
    B, S, _ = x.shape
    q, kc, vc, ks, vs, kw, vw, gl = split_cols(x @ w_in, ODD_WIDTHS)
    r = lambda a, h: a.reshape(B, S, h, HEAD_DIM)
    o = nsa_attention(r(q, C_HEADS), r(kc, C_KV_HEADS), r(vc, C_KV_HEADS), r(ks, C_KV_HEADS),
                      r(vs, C_KV_HEADS), r(kw, C_KV_HEADS), r(vw, C_KV_HEADS), gl,
                      pe_k, w1_k, w2_k, pe_v, w1_v, w2_v, rel_table[:, :C_HEADS])
    return o.reshape(B, S, C_HEADS * HEAD_DIM) @ w_out

def cross_attention(x, mem, w_q, w_k, w_v, w_o):
    B, S, _ = x.shape
    M = mem.shape[1]
    q = (x @ w_q).reshape(B, S, X_HEADS, X_HEAD_DIM)
    k = (mem @ w_k).reshape(B, M, X_HEADS, X_HEAD_DIM)
    v = (mem @ w_v).reshape(B, M, X_HEADS, X_HEAD_DIM)
    lg = jnp.einsum('bshd,bmhd->bhsm', q, k).astype(jnp.float32) * X_HEAD_DIM ** -0.5
    p = jax.nn.softmax(lg, axis=-1).astype(v.dtype)
    o = jnp.einsum('bhsm,bmhd->bshd', p, v).reshape(B, S, X_HEADS * X_HEAD_DIM)
    return o @ w_o

def dense_swiglu(x, w_gate, w_up, w_down):
    return (jax.nn.silu(x @ w_gate) * (x @ w_up)) @ w_down

def moe_swiglu(x, w_router, w_gate, w_up, w_down):
    logits = (x @ w_router).astype(jnp.float32)
    top_val, top_idx = lax.top_k(logits, TOP_K)
    top_w = jax.nn.softmax(top_val, axis=-1)
    gate = jnp.einsum('bsk,bske->bse', top_w,
                      jax.nn.one_hot(top_idx, N_EXPERTS_2, dtype=jnp.float32)).astype(x.dtype)
    y = jnp.zeros_like(x)
    for e in range(N_EXPERTS_2):
        h = jax.nn.silu(x @ w_gate[e]) * (x @ w_up[e])
        y = y + gate[..., e:e + 1] * (h @ w_down[e])
    return y

def second_inputs(seed: int = 0) -> dict:
    key = jax.random.key(seed)
    ks = iter(jax.random.split(key, 32))

    def nrm(shape, scale):
        return jax.random.normal(next(ks), shape, jnp.float32) * scale

    D = D_MODEL
    XW = X_HEADS * X_HEAD_DIM
    CW = CMP_BLOCK * HEAD_DIM
    return {
        'x': nrm((BATCH, SEQ, D), 1.0),
        'mem': nrm((BATCH, MEM_LEN, D), 1.0),
        'rel_table': nrm((REL_BUCKETS, N_SLOTS), 0.2),
        'ev_w_in': nrm((N_EVEN, D, EVEN_COLS), D ** -0.5),
        'ev_ckv_gain': 1.0 + nrm((N_EVEN, A_LATENT), 0.02),
        'ev_w_uk': nrm((N_EVEN, A_HEADS, HEAD_DIM, A_LATENT), HEAD_DIM ** -0.5),
        'ev_w_uv': nrm((N_EVEN, A_HEADS, A_LATENT, HEAD_DIM), A_LATENT ** -0.5),
        'ev_sinks': nrm((N_EVEN, B_HEADS), 0.5),
        'ev_w_out': nrm((N_EVEN, N_SLOTS * HEAD_DIM, D), BETA_2 * (N_SLOTS * HEAD_DIM) ** -0.5),
        'od_w_in': nrm((N_ODD, D, ODD_COLS), D ** -0.5),
        'od_pe_k': nrm((N_ODD, CMP_BLOCK, HEAD_DIM), 0.1),
        'od_w1_k': nrm((N_ODD, CW, CMP_HIDDEN), CW ** -0.5),
        'od_w2_k': nrm((N_ODD, CMP_HIDDEN, HEAD_DIM), CMP_HIDDEN ** -0.5),
        'od_pe_v': nrm((N_ODD, CMP_BLOCK, HEAD_DIM), 0.1),
        'od_w1_v': nrm((N_ODD, CW, CMP_HIDDEN), CW ** -0.5),
        'od_w2_v': nrm((N_ODD, CMP_HIDDEN, HEAD_DIM), CMP_HIDDEN ** -0.5),
        'od_w_out': nrm((N_ODD, C_HEADS * HEAD_DIM, D), BETA_2 * (C_HEADS * HEAD_DIM) ** -0.5),
        'xa_w_q': nrm((DEPTH_2, D, XW), D ** -0.5),
        'xa_w_k': nrm((DEPTH_2, D, XW), D ** -0.5),
        'xa_w_v': nrm((DEPTH_2, D, XW), D ** -0.5),
        'xa_w_o': nrm((DEPTH_2, XW, D), BETA_2 * XW ** -0.5),
        'ff_w_gate': nrm((N_EVEN, D, D_FF), D ** -0.5),
        'ff_w_up': nrm((N_EVEN, D, D_FF), D ** -0.5),
        'ff_w_down': nrm((N_EVEN, D_FF, D), BETA_2 * D_FF ** -0.5),
        'moe_w_router': nrm((N_ODD, D, N_EXPERTS_2), D ** -0.5),
        'moe_w_gate': nrm((N_ODD, N_EXPERTS_2, D, D_FF_EXPERT), D ** -0.5),
        'moe_w_up': nrm((N_ODD, N_EXPERTS_2, D, D_FF_EXPERT), D ** -0.5),
        'moe_w_down': nrm((N_ODD, N_EXPERTS_2, D_FF_EXPERT, D), BETA_2 * D_FF_EXPERT ** -0.5),
        'ln_g': 1.0 + nrm((DEPTH_2, 3, D), 0.02),
        'ln_b': nrm((DEPTH_2, 3, D), 0.02),
    }

def second_block(x, mem, rel_table, ev_w_in, ev_ckv_gain, ev_w_uk, ev_w_uv, ev_sinks, ev_w_out,
              od_w_in, od_pe_k, od_w1_k, od_w2_k, od_pe_v, od_w1_v, od_w2_v, od_w_out,
              xa_w_q, xa_w_k, xa_w_v, xa_w_o, ff_w_gate, ff_w_up, ff_w_down,
              moe_w_router, moe_w_gate, moe_w_up, moe_w_down, ln_g, ln_b):
    h = x
    for i in range(DEPTH_2):
        j = i // 2
        if i % 2 == 0:
            mix = even_mixer(h, ev_w_in[j], ev_ckv_gain[j], ev_w_uk[j], ev_w_uv[j], ev_sinks[j],
                             ev_w_out[j], rel_table)
        else:
            mix = odd_mixer(h, od_w_in[j], od_pe_k[j], od_w1_k[j], od_w2_k[j], od_pe_v[j],
                            od_w1_v[j], od_w2_v[j], od_w_out[j], rel_table)
        h = layer_norm(ALPHA_2 * h + mix, ln_g[i, 0], ln_b[i, 0])
        xa = cross_attention(h, mem, xa_w_q[i], xa_w_k[i], xa_w_v[i], xa_w_o[i])
        h = layer_norm(ALPHA_2 * h + xa, ln_g[i, 1], ln_b[i, 1])
        if i % 2 == 0:
            ff = dense_swiglu(h, ff_w_gate[j], ff_w_up[j], ff_w_down[j])
        else:
            ff = moe_swiglu(h, moe_w_router[j], moe_w_gate[j], moe_w_up[j], moe_w_down[j])
        h = layer_norm(ALPHA_2 * h + ff, ln_g[i, 2], ln_b[i, 2])
    return h


def setup_inputs(seed=0):
    out = dict(first_inputs(seed))
    for name, value in second_inputs(seed + 1).items():
        if name != "x":
            out[name + "_2"] = value
    return out


def reference(
    x, mem, ln_in_g, ln_in_b, w_in, fox_fb, lam_q1, lam_k1, lam_q2, lam_k2, diff_norm_g,
    hgrn_lb, hgrn_norm_g, w_out, mem_wq, mem_wk, mem_wv, mem_wo, router_w, router_b, w1, w3, w2,
    ln_g, ln_b, mem_2, rel_table_2, ev_w_in_2, ev_ckv_gain_2, ev_w_uk_2, ev_w_uv_2, ev_sinks_2,
    ev_w_out_2, od_w_in_2, od_pe_k_2, od_w1_k_2, od_w2_k_2, od_pe_v_2, od_w1_v_2, od_w2_v_2,
    od_w_out_2, xa_w_q_2, xa_w_k_2, xa_w_v_2, xa_w_o_2, ff_w_gate_2, ff_w_up_2, ff_w_down_2,
    moe_w_router_2, moe_w_gate_2, moe_w_up_2, moe_w_down_2, ln_g_2, ln_b_2,
):
    x = first_block(
        x, mem, ln_in_g, ln_in_b, w_in, fox_fb, lam_q1, lam_k1, lam_q2, lam_k2, diff_norm_g,
        hgrn_lb, hgrn_norm_g, w_out, mem_wq, mem_wk, mem_wv, mem_wo, router_w, router_b, w1, w3,
        w2, ln_g, ln_b,
    )
    return second_block(
        x, mem_2, rel_table_2, ev_w_in_2, ev_ckv_gain_2, ev_w_uk_2, ev_w_uv_2, ev_sinks_2,
        ev_w_out_2, od_w_in_2, od_pe_k_2, od_w1_k_2, od_w2_k_2, od_pe_v_2, od_w1_v_2, od_w2_v_2,
        od_w_out_2, xa_w_q_2, xa_w_k_2, xa_w_v_2, xa_w_o_2, ff_w_gate_2, ff_w_up_2, ff_w_down_2,
        moe_w_router_2, moe_w_gate_2, moe_w_up_2, moe_w_down_2, ln_g_2, ln_b_2,
    )


_drawn_inputs = setup_inputs


def setup_inputs(seed=0):
    import zlib

    import numpy as np

    out = dict(_drawn_inputs(seed))
    spreads = {}
    factors = {'lam_k2': 8.0,
     'diff_norm_g': 2.829,
     'hgrn_norm_g': 3.123,
     'ev_ckv_gain_2': 8.0,
     'ev_sinks_2': 64.0,
     'od_pe_k_2': 27.071,
     'od_pe_v_2': 4.287}
    for name, (base, spread) in spreads.items():
        noise = np.random.default_rng([zlib.crc32(name.encode()), seed]).standard_normal(out[name].shape)
        drawn = base * np.exp(spread * noise) if base else spread * noise
        out[name] = jnp.asarray(drawn.astype(out[name].dtype))
    for name, factor in factors.items():
        out[name] = (out[name] * factor).astype(out[name].dtype)
    return out
```

```python
import math
from contextlib import ExitStack

import numpy as np

import concourse.bass as bass
from concourse import mybir

ALU = mybir.AluOpType
ACT = mybir.ActivationFunctionType
AX = mybir.AxisListType
F32 = mybir.dt.float32

P = 128
T = 256
TT = T // P
D = 1024
KT = D // P
COLS = 256
RING = 6
SLOT = KT * COLS
EPS = 1e-5
NEG = -1e30
TAKEN = -3e38

ALPHA1 = 2.0 ** 0.25
ALPHA2 = 4.0 ** 0.25
FOX_H, DIFF_H, HGRN_H, MEM_H = 4, 4, 4, 4
LAM_INIT = 0.8 - 0.6 * math.exp(0.0)
E1, FF1 = 16, 512
E2, FF2 = 8, 3584
FF_DENSE = 2816
TOPK = T // 4
N_CMP = 15
BUCKETS = 32
LEVELS = [128, 64, 32, 16, 8, 4, 2, 1]
BIAS_W = 384
ROW_W = 512


def shape_constants():
    p = np.arange(P)
    q = np.arange(T)
    eye = np.eye(P)
    flip = np.eye(P)[::-1]
    tri = np.stack([(p[:, None] + P * t <= q[None, :]) for t in range(TT)], 1).reshape(P, -1)
    causal = np.stack([np.where(q[None, :] <= p[:, None] + P * t, 0.0, NEG) for t in range(TT)], 1).reshape(P, -1)
    chunk = np.stack([np.where(q[None, :] // 64 <= (p[:, None] + P * t) // 64, 0.0, NEG) for t in range(TT)],
                     1).reshape(P, -1)
    levels = []
    for b in LEVELS[1:]:
        s, t = p[:, None], p[None, :]
        levels.append((s // (2 * b) == t // (2 * b)) & (s % (2 * b) < b) & (t % (2 * b) >= b))
    levels.append(p[:, None] == p[None, :])
    levels = np.stack(levels, 1).reshape(P, -1)
    halves = (p[:, None] // 64 == p[None, :] // 64)
    ends = 16 * np.arange(N_CMP) + 31
    valid = np.stack([(p[:, None] + P * t >= ends[None, :]) for t in range(TT)], 1).reshape(P, -1)
    lower = lambda n: np.broadcast_to((np.arange(n)[None, :] < np.arange(n)[:, None]).reshape(1, -1), (P, n * n))
    parts = [("eye", eye), ("flip", flip), ("tri", tri), ("causal", causal), ("chunk", chunk), ("levels", levels),
             ("halves", halves), ("valid", valid), ("lower4", lower(4)), ("lower8", lower(8))]
    at, off = {}, 0
    for name, a in parts:
        at[name] = (off, a.shape[1])
        off += a.shape[1]
    wide = np.concatenate([np.asarray(a, np.float32) for _, a in parts], 1)

    def bucket(dist):
        n = np.maximum(dist, 1)
        log_b = 16 + (np.log(n / 16.0) / math.log(8.0) * 16).astype(np.int64)
        return np.where(dist < 16, np.maximum(dist, 0), np.minimum(log_b, BUCKETS - 1))

    def onehot(dist, ok):
        m = np.zeros((BUCKETS + 1, len(dist)))
        m[bucket(dist), np.arange(len(dist))] = ok
        m[BUCKETS] = ~ok
        return m
    j = np.arange(ROW_W)
    dist = 255 - j
    fwd = j - 255
    rows = np.stack([onehot(dist, dist >= 0), onehot(dist, (dist >= 0) & (dist < 128)), onehot(fwd, fwd >= 0)], 1)
    return at, np.ascontiguousarray(wide), rows.reshape(BUCKETS + 1, -1).astype(np.float32)


CONST_AT, CONST_WIDE, CONST_ROWS = shape_constants()


class Tally:

    def __init__(self, eng, sem):
        self.eng, self.sem, self.n = eng, sem, 0

    def did(self, ins):
        ins.then_inc(self.sem, 1)
        self.n += 1

    def wait(self):
        self.eng.wait_ge(self.sem, self.n)


def two_block_kernel(nc, I, out):
    ctx = ExitStack()
    with ctx:
        def sb(name, shape):
            return ctx.enter_context(nc.sbuf_tensor(name, shape, F32))[tuple(slice(None) for _ in shape)]

        def sem(name):
            return ctx.enter_context(nc.semaphore(name))

        ring = sb("ring", [P, RING, SLOT])
        h = sb("h", [P, TT, D])
        hT = sb("hT", [P, KT, T])
        yT = sb("yT", [P, KT, T])
        memT = sb("memT", [P, KT, T])
        mkT = sb("mkT", [P, KT, T])
        mv = sb("mv", [P, TT, D])
        gb = sb("gb", [P, 2, D])
        cw = sb("cw", [P, CONST_WIDE.shape[1]])
        NS = 3
        S = sb("S", [P, NS, TT, T])
        PT = sb("PT", [P, 2, TT, T])
        small = sb("small", [P, 1500])
        arena = sb("arena", [P, 15872])

        def const(name):
            o, n = CONST_AT[name]
            return cw[:, o:o + n]
        eye, flip, halves = const("eye"), const("flip"), const("halves")
        tri = const("tri").rearrange("p (a k) -> p a k", a=TT)
        causal = const("causal").rearrange("p (a k) -> p a k", a=TT)
        chunkmask = const("chunk").rearrange("p (a k) -> p a k", a=TT)
        levelmask = const("levels").rearrange("p (a k) -> p a k", a=len(LEVELS))
        valid = const("valid").rearrange("p (t n) -> p t n", t=TT)

        small_used = [0]

        def tiny(*shape):
            n = int(np.prod(shape))
            o = small_used[0]
            small_used[0] += n
            assert small_used[0] <= 1500, small_used
            v = small[:, o:o + n]
            names = " ".join("abcd"[:len(shape)])
            return v if len(shape) == 1 else v.rearrange(f"p ({names}) -> p {names}",
                                                         **{c: s for c, s in zip("abcd", shape)})

        class Region:

            def __init__(self, start=0):
                self.at = start

            def get(self, *shape):
                n = int(np.prod(shape))
                v = arena[:, self.at:self.at + n]
                self.at += n
                assert self.at <= 15872, self.at
                names = " ".join("abcd"[:len(shape)])
                return v if len(shape) == 1 else v.rearrange(f"p ({names}) -> p {names}",
                                                             **{c: s for c, s in zip("abcd", shape)})

        r = Region()
        fqT, fkT, fv = r.get(2, T), r.get(2, T), r.get(TT, 256)
        dqT, dkT, dv = r.get(2, T), r.get(2, T), r.get(TT, 256)
        hqT, hfT, hi, hgT = r.get(4, T), r.get(4, T), r.get(TT, 512), r.get(4, T)
        hkT, bcT = r.get(4, T), r.get(4, T)
        decay = r.get(2, 4, T)
        Wlv = r.get(2, 4, T)
        SM = r.get(3, 512)
        oT, sqT = hqT, hfT
        dsq, drs = r.get(2, T), r.get(2, T)
        mem_tok = Region(1536).get(TT, D)
        hankel = Region(3584).get(16, BIAS_W)
        mqT = Region().get(KT, T)
        r = Region()
        sg = r.get(2, T)
        hid = r.get(4, T)
        biasT = Region(15872 - 16 * BIAS_W).get(16, BIAS_W)
        r = Region()
        qaT, qiT, qbT = r.get(4, T), r.get(4, T), r.get(4, T)
        kiT, kbT, vb = r.get(T), r.get(2, T), r.get(TT, P)
        ckv, cT, qlatT = r.get(TT, P), r.get(T), r.get(8, T)
        olatT = qlatT
        idx_act = r.get(2, TT, T)
        score = r.get(TT, T)
        work = r.get(TT, T)
        assert r.at <= 15872 - 16 * BIAS_W, r.at
        r = Region()
        qcT = r.get(8, T)
        kvcT = r.get(2, T)
        ksT, vs, kwT, vw = r.get(2, T), r.get(TT, P), r.get(2, T), r.get(TT, P)
        Pc = r.get(2, TT, 8, 32)
        bcmp = r.get(2, TT, 8, 16)
        pcT = r.get(2, 2, T)
        geluT = r.get(2, 2, 32)
        kcT = r.get(2, 32)
        vc4 = r.get(2, 64)
        assert r.at <= 15872 - 16 * BIAS_W, r.at

        wff = tiny(KT, FOX_H)
        foxb = tiny(FOX_H)
        lamv = tiny(4, 32)
        dng, hng = tiny(1), tiny(1)
        rw1, rb1, rw2 = tiny(KT, E1), tiny(E1), tiny(KT, E2)
        ckvg = tiny(P)
        sinks = tiny(8)
        peT = tiny(2, 32)
        stats, mvar, veps, std, rstd = tiny(TT, 2, 6), tiny(TT, 2), tiny(TT), tiny(TT), tiny(TT)
        ffx = tiny(TT, FOX_H)
        ffa, ffe, nlogf, cumq = tiny(TT, FOX_H), tiny(TT, FOX_H), tiny(TT, FOX_H), tiny(TT, FOX_H)
        lamp, lams, lame, neglam = tiny(2, 32), tiny(2), tiny(2), tiny(2)
        nmx, ssum, rsum, esink = tiny(NS, TT), tiny(NS, TT), tiny(NS, TT), tiny(NS, TT)
        nsinks = tiny(8)
        wi = tiny(TT, 8)
        css, cstd, crstd = tiny(TT), tiny(TT), tiny(TT)
        m8 = tiny(TT, 8)
        pbias = tiny(5)
        csum, cmx = tiny(32), tiny(32)

        wuk, wuv, w2kv = sb("wuk", [P, 4, P]), sb("wuv", [P, 8, 64]), sb("w2kv", [P, 2, 64])
        tab = sb("tab", [BUCKETS + 1, 16])
        ohot = sb("ohot", [BUCKETS + 1, 3, ROW_W])
        rowbuf = PT[0:16].rearrange("p a b c -> p a (b c)")
        rows_dram = nc.dram_tensor("bias_rows", (16, 2, ROW_W), F32, kind="Internal").ap()
        ones = sb("ones", [P, T])
        route = S[:].rearrange("p a b c -> p (a b c)")[:, 0:1000]
        step_gate = sb("step_gate", [P, TT, 112])
        g3 = sb("g3", [P, TT, 48])

        F = [ctx.enter_context(nc.psum_tensor(f"psF{i}", [P, 512], F32)) for i in range(4)]
        B = [ctx.enter_context(nc.psum_tensor(f"psB{i}", [P, 512], F32)) for i in range(4)]

        def pair(bank, w=T):
            return bank[:, 0:2 * w].rearrange("p (a b) -> p a b", a=2)

        x_in, mem_in, mem2_in = sem("x_in"), sem("mem_in"), sem("mem2_in")
        consts_in, params_in, table_in = sem("consts_in"), sem("params_in"), sem("table_in")
        gb_in = sem("gb_in")
        w_in = [sem(f"weights_in{i}") for i in range(RING)]
        out_stored = sem("out_stored")
        rows_out, rows_back = sem("bias_rows_out"), sem("bias_rows_back")
        set_up = sem("set_up")
        ln_done, var_ready, std_ready = sem("ln_done"), sem("var_ready"), sem("std_ready")
        proj_ready, proj_saved = sem("proj_ready"), sem("proj_saved")
        res_ready, res_added = sem("res_ready"), sem("res_added")
        logits_ready, scored, max_ready = sem("logits_ready"), sem("scored"), sem("max_ready")
        exp_ready, probs_ready = sem("exp_ready"), sem("probs_ready")
        pt_ready, pt_saved, pv_done, o_saved = sem("pt_ready"), sem("pt_saved"), sem("pv_done"), sem("o_saved")
        dve_step, act_step, pool_step = sem("dve_step"), sem("act_step"), sem("pool_step")
        gu_ready, sg_ready, hid_ready = sem("gate_up_ready"), sem("silu_ready"), sem("hidden_ready")
        y_ready, y_added = sem("y_ready"), sem("y_added")
        to_act, from_act = sem("dve_to_act"), sem("act_to_dve")
        logf_ready = sem("log_forget_ready")
        squares_ready, y_normed = sem("squares_ready"), sem("y_normed")
        latents_ready, penalty_ready = sem("latents_ready"), sem("penalty_ready")
        cmp_cleared, cmp_ready = sem("compressed_cleared"), sem("compressed_probs_ready")
        idx_used = sem("indexer_product_used")
        hg_arg, hg_exp, hg_w = sem("level_argument"), sem("level_decay"), sem("level_operands")
        hg_scores, hg_masked, hg_pv = sem("level_scores"), sem("level_masked"), sem("level_pv")

        chunks = []
        freed = {}
        landed = [0] * RING
        ready_at = {}

        def chunk(src, kt=KT, w=COLS):
            c = len(chunks)
            pieces = src if isinstance(src, list) else [(0, P, src)]
            chunks.append((pieces, kt, w))
            landed[c % RING] += 16 * len(pieces)
            ready_at[c] = landed[c % RING]
            return c

        def wview(c, kt, w):
            return ring[:, c % RING, 0:kt * w].rearrange("p (a n) -> p a n", a=kt)

        def kxn(ap):
            return ap.rearrange("(a p) n -> p a n", p=P)

        units = []
        adds = []

        def unit(stage, kind, args, dest, func=ACT.Copy, scale=1.0):
            units.append((stage, kind, args, dest, func, scale))
            if kind in ("T", "tok", "dup") and args[1] is not None:
                freed[args[1]] = (proj_ready, len(units))
            if kind == "hidden":
                for c in args[2]:
                    freed[c] = (proj_ready, len(units))

        def span(stage):
            n = [i for i, u in enumerate(units) if u[0] == stage]
            return n[0], n[-1] + 1

        def add_span(stage):
            n = [i for i, u in enumerate(adds) if u[0] == stage]
            return n[0], n[-1] + 1

        def transposes(stage, src, dst, blocks=KT):
            for j in range(0, blocks, 2):
                unit(stage, "tr", (src, j), dst[:, j:j + 2, :])

        def project(stage, kind, x, src, dest, c0, n, func=ACT.Copy, scale=1.0, dstT=True):
            for j in range(n):
                c = chunk(kxn(src)[:, :, c0 + j * COLS:c0 + (j + 1) * COLS])
                d = dest[:, 2 * j:2 * j + 2, :] if kind == "T" else dest[:, :, j * COLS:(j + 1) * COLS]
                unit(stage, kind, (x, c, KT, COLS, 0, COLS), d, func, scale)

        def residual(stage, src, kt=KT):
            for j in range(D // COLS):
                c = chunk(kxn(src)[:, :, j * COLS:(j + 1) * COLS], kt)
                adds.append((stage, c, kt, j))
                freed[c] = (res_ready, len(adds))

        phases = {}
        steps_before = [0]

        def experts(name, steps):
            phases[name] = (len(chunks), steps, steps_before[0])
            for s in range(steps):
                g = steps_before[0] + s
                for part in range(3):
                    c = len(chunks)
                    chunks.append((None, 0, 0))
                    landed[c % RING] += 16
                    ready_at[c] = landed[c % RING]
                    freed[c] = (gu_ready, 2 * g + 2) if part < 2 else (y_ready, 4 * g + 4)
            steps_before[0] += steps

        transposes("mem1 transposed", mem_tok, memT)
        project("mem1 keys", "T", memT, I["mem_wk"][0], mkT, 0, 4)
        project("mem1 values", "tok", memT, I["mem_wv"][0], mv, 0, 4)
        for a in range(2):
            unit("bias rows", "row", (a,), rowbuf[:, a, :])
        transposes("ln0 transposed", h, hT)
        w = I["w_in"][0]
        project("mix1", "T", hT, w, hfT, 2052, 2)
        unit("mix1", "tok", (hT, None, KT, FOX_H, 0, FOX_H), ffx)
        project("mix1", "T", hT, w, fqT, 0, 1, scale=0.125)
        project("mix1", "T", hT, w, fkT, 256, 1)
        project("mix1", "tok", hT, w, fv, 512, 1)
        project("mix1", "T", hT, w, dqT, 772, 1, scale=32.0 ** -0.5)
        project("mix1", "T", hT, w, dkT, 1028, 1)
        project("mix1", "tok", hT, w, dv, 1284, 1)
        project("mix1", "tok", hT, w, hi, 2564, 2)
        project("mix1", "T", hT, w, hqT, 1540, 2, func=ACT.Silu)
        project("mix1", "T", hT, w, hgT, 3076, 2, func=ACT.Silu)
        unit("forget sums", "cum", (), cumq, ACT.Copy, -1.0)
        unit("mean squares", "sumsq", (halves, dsq, 1.0 / 64), drs)
        for a in range(2):
            unit("mean squares", "sumsq", (ones[:, 0:P], sqT[:, 2 * a:2 * a + 2, :], 1.0 / P),
                 decay[:, 0, 2 * a:2 * a + 2, :])
        residual("out1", I["w_out"][0])
        transposes("ln1 transposed", h, hT)
        project("mem1 queries", "T", hT, I["mem_wq"][0], mqT, 0, 4, scale=1.0 / 16)
        residual("mem1 out", I["mem_wo"][0])
        transposes("ln2 transposed", h, hT)
        route_in = route[:, 0:TT * E1].rearrange("p (a b) -> p a b", a=TT)
        unit("router1", "tok", (hT, None, KT, E1, 0, E1), route_in, ACT.Sigmoid)
        experts("moe1", E1 * FF1 // COLS)
        for j in range(16):
            unit("bias tiles 0", "flip", (j,), biasT[:, j, :])
        transposes("mem2 transposed", mem_tok, memT)
        for i in range(2):
            project(f"xa{i} keys", "T", memT, I["xa_w_k_2"][i], mkT, 0, 2)
            project(f"xa{i} values", "tok", memT, I["xa_w_v_2"][i], mv, 0, 2)
            transposes(f"ln{3 * i + 3} transposed", h, hT)
            if i == 0:
                w = I["ev_w_in_2"][0]
                c = chunk(kxn(w)[:, :, 512:640], w=128)
                unit("mix2", "tok", (hT, c, KT, 128, 0, 128), ckv)
                c = chunk(kxn(w)[:, :, 1152:1224], w=72)
                unit("mix2", "dup", (hT, c, KT, 72, 0, 1), kiT)
                unit("mix2", "tok", (hT, c, KT, 72, 64, 8), wi, ACT.Copy, 8.0 ** -0.5)
                project("mix2", "T", hT, w, qiT, 640, 2)
                for j in range(8):
                    unit("indexer", "idx", (j,), idx_act[:, j % 2], ACT.Relu, 0.125)
                project("mix2b", "T", hT, w, qaT, 0, 2)
                project("mix2b", "T", hT, w, qbT, 1224, 2, scale=0.125)
                c = chunk(kxn(w)[:, :, 1736:1992])
                unit("mix2b", "dup", (hT, c, KT, 256, 0, 2), kbT)
                unit("mix2b", "tok", (hT, c, KT, 256, 128, 128), vb)
                for j in (0, 4, 1, 5):
                    unit("latent queries", "uk", (j,), qlatT[:, j:j + 3:2, :], ACT.Copy, 0.125)
                unit("latent keys", "ctr", (), cT)
                for j in range(4):
                    unit("latent out", "uv", (j,), yT[:, j, :])
                residual("out2", I["ev_w_out_2"][0])
            else:
                w = I["od_w_in_2"][0]
                project("mix3", "T", hT, w, kvcT, 1024, 1)
                project("mix3", "T", hT, w, qcT, 0, 4, scale=0.125)
                for c0, kd, vd in ((1280, ksT, vs), (1536, kwT, vw)):
                    c = chunk(kxn(w)[:, :, c0:c0 + 256])
                    unit("mix3", "dup", (hT, c, KT, 256, 0, 2), kd)
                    unit("mix3", "tok", (hT, c, KT, 256, 128, 128), vd)
                c = chunk(kxn(w)[:, :, 1792:1840], w=48)
                unit("mix3", "tok", (hT, c, KT, 48, 0, 48), g3, ACT.Sigmoid)
                unit("compressed bias", "cb", (), bcmp)
                for br, name in enumerate(("od_w1_k_2", "od_w1_v_2")):
                    v = I[name][0].rearrange("(j d) c -> d j c", d=64)
                    cs = [chunk([(0, 64, v[:, 16 * a:16 * a + 16, :]), (64, 64, v[:, 16 * a:16 * a + 16, :])], 16, 128)
                          for a in range(2)]
                    for g in range(2):
                        unit("compress hidden", "hidden", (br, g, cs), geluT[:, br, g, 0:N_CMP])
                unit("compress out", "kc", (), kcT)
                unit("compress out", "vc", (), vc4)
                for par in range(2):
                    adds.append(("compressed logits", None, par, None))
                for par in range(2):
                    unit("compressed probs", "pctr", (par,), pcT[:, par])
                residual("out3", I["od_w_out_2"][0])
            transposes(f"ln{3 * i + 4} transposed", h, hT)
            project(f"xa{i} queries", "T", hT, I["xa_w_q_2"][i], mqT, 0, 2, scale=128.0 ** -0.5)
            residual(f"xa{i} out", I["xa_w_o_2"][i], 4)
            transposes(f"ln{3 * i + 5} transposed", h, hT)
            if i == 0:
                experts("dense", FF_DENSE // COLS)
                for j in range(8, 16):
                    unit("bias tiles 1", "flip", (j,), biasT[:, j, :])
            else:
                unit("router2", "tok", (hT, None, KT, E2, 0, E2), route[:, 0:TT * E2].rearrange(
                    "p (a b) -> p a b", a=TT))
                experts("moe2", E2 * FF2 // COLS)

        maps, groups, map_span = [], [], {}

        def attention(stage, items):
            m0, g0 = len(maps), len(groups)
            for members, dest in items:
                for n, mp in enumerate(members):
                    base = mp.setdefault("base", 0)
                    same = [i for i, o in enumerate(members) if o.get("base", 0) == base]
                    mp.update(group=len(groups), new=(n == 0), first=(n == same[0]), last=(n == same[-1]),
                              end=(n == len(members) - 1))
                    maps.append(mp)
                groups.append((len(maps) - 1, dest))
            map_span[stage] = (m0, len(maps), g0, len(groups))

        def half(j):
            return slice(64 * (j % 2), 64 * (j % 2) + 64)

        fox = [([dict(qk=[(fqT[half(j), j // 2, :], fkT[half(j), j // 2, :])], mask=causal, fox=j,
                      v=fv[:, :, 64 * j:64 * j + 64], base=64 * (j % 2)) for j in (2 * a, 2 * a + 1)],
                yT[:, a, :]) for a in range(2)]

        def diff_map(j, c):
            rows = slice(32 * (2 * (j % 2) + c), 32 * (2 * (j % 2) + c) + 32)
            return dict(qk=[(dqT[rows, j // 2, :], dkT[rows, j // 2, :])], mask=chunkmask,
                        coef=neglam if c else None, v=dv[:, :, 64 * j:64 * j + 64], base=64 * (j % 2))
        diff = [([diff_map(j, c) for j in (2 * a, 2 * a + 1) for c in range(2)], yT[:, 2 + a, :]) for a in range(2)]
        attention("mix1", fox + diff)
        attention("mem1", [([dict(qk=[(mqT[:, 2 * j + a, :], mkT[:, 2 * j + a, :]) for a in range(2)],
                                  v=mv[:, :, 256 * j:256 * j + 256])], yT[:, 2 * j:2 * j + 2, :]) for j in range(4)])

        def bias_of(j):
            v = biasT[:, j, P:P + T]
            return bass.AP(tensor=v.tensor, offset=v.offset, ap=[v.ap[0], [-P, TT], [1, T]])
        lat = [([dict(qk=[(qlatT[:, j, :], cT)], mask=bias_of(j), extra=work, v=ckv[:, :, 0:P])],
                olatT[:, j, :]) for j in range(8)]
        win = [([dict(qk=[(qbT[half(j), j // 2, :], kbT[half(j), j // 4, :])], mask=bias_of(8 + j), sink=j,
                      v=vb[:, :, 64 * (j // 4):64 * (j // 4) + 64], base=64 * (j % 2)) for j in (2 * a, 2 * a + 1)],
                yT[:, 4 + a, :]) for a in range(4)]
        attention("mix2", win + lat)
        cross = [([dict(qk=[(mqT[:, j, :], mkT[:, j, :])], v=mv[:, :, P * j:P * j + P])], yT[:, j, :])
                 for j in range(4)]
        attention("xa0", cross)

        def nsa_maps(j):
            g = j // 8
            out = []
            for branch, (k, v) in enumerate(((ksT, vs), (kwT, vw))):
                out.append(dict(qk=[(qcT[half(j), j // 2, :], k[half(j), g, :])], mask=bias_of(j),
                                coef=g3[:, :, 3 * j + 1 + branch], v=v[:, :, 64 * g:64 * g + 64], base=64 * (j % 2),
                                compressed=j if branch == 0 else None))
            return out
        attention("mix3", [(nsa_maps(2 * a) + nsa_maps(2 * a + 1), yT[:, a, :]) for a in range(8)])
        attention("xa1", [([dict(mp) for mp in members], dest) for members, dest in cross])

        def saved(stage):
            return span(stage)[1]

        def maps_end(stage):
            return map_span[stage][1]

        def groups_end(stage):
            return map_span[stage][3]

        N_PARAMS = len(SMALL_LOADS) + 4
        CREDIT = 4
        n_steps = steps_before[0]
        block = ctx.enter_context(nc.Block())

        @block.sync
        def _(sp):
            sp.dma_start(h[:], I["x"][0].rearrange("(t p) d -> p t d", p=P)).then_inc(x_in, 16)
            sp.dma_start(mem_tok, I["mem"][0].rearrange("(t p) d -> p t d", p=P)).then_inc(mem_in, 16)

            def load(c):
                pieces, kt, w = chunks[c]
                if c >= RING:
                    sp.wait_ge(*freed[c - RING])
                for row, n, src in pieces:
                    sp.dma_start(ring[row:row + n, c % RING, 0:kt * w].rearrange("p (a n) -> p a n", a=kt),
                                 src).then_inc(w_in[c % RING], 16)

            def load_experts(wg, wu, wd, n_exp, ff, name):
                first, steps, before = phases[name]
                per = ff // COLS
                gate = wg.rearrange("e (a p) (c n) -> e c p a n", p=P, n=COLS)
                up = wu.rearrange("e (a p) (c n) -> e c p a n", p=P, n=COLS)
                down = wd.rearrange("e (c f p) n -> e c p f n", p=P, f=2)

                def step(e, c, par, g, peeled):
                    for part, w in enumerate((gate, up, down)):
                        slot = (first + 3 * par + part) % RING
                        if peeled:
                            k = first + 3 * par + part - RING
                            if k >= 0:
                                sp.wait_ge(*freed[k])
                        elif part < 2:
                            sp.wait_ge(gu_ready, g * 2 - 2)
                        else:
                            sp.wait_ge(y_ready, g * 4 - 4)
                        kt = KT if part < 2 else 2
                        sp.dma_start(ring[:, slot, :].rearrange("p (a n) -> p a n", a=kt),
                                     w[bass.ds(e, 1), bass.ds(c, 1)].rearrange("e c p a n -> p (e c a) n"))\
                            .then_inc(w_in[slot], 16)

                for s in range(2):
                    step(0, s, s, before + s, True)
                if per > 3:
                    with nc.sync.Fori(1, per // 2) as b:
                        for s in range(2):
                            step(0, b * 2 + s, s, b * 2 + (before + s), False)
                if per % 2:
                    step(0, per - 1, 0, before + per - 1, False)
                if n_exp > 1:
                    with nc.sync.Fori(1, n_exp) as e:
                        if per == 2:
                            for s in range(2):
                                step(e, s, s, e * 2 + (before + s), False)
                        else:
                            with nc.sync.Fori(0, per // 2) as b:
                                for s in range(2):
                                    step(e, b * 2 + s, s, e * per + b * 2 + (before + s), False)

            order = [("moe1", ("w1", "w3", "w2"), E1, FF1, True), ("dense", ("ff_w_gate_2", "ff_w_up_2", "ff_w_down_2"), 1,
                     FF_DENSE, False), ("moe2", ("moe_w_gate_2", "moe_w_up_2", "moe_w_down_2"), E2, FF2, True)]
            at = 0
            for name, ws, n_exp, ff, experts_dim in order:
                first, steps, _ = phases[name]
                for c in range(at, first):
                    load(c)
                wg, wu, wd = [I[x][0] if experts_dim else I[x] for x in ws]
                load_experts(wg, wu, wd, n_exp, ff, name)
                at = first + 3 * steps
            assert at == len(chunks)
            sp.wait_ge(ln_done, 10)
            sp.dma_start(out[0].rearrange("(t p) d -> p t d", p=P), h[:]).then_inc(out_stored, 16)
            sp.wait_ge(out_stored, 16)

        @block.gpsimd
        def _(pool):
            pool.dma_start(cw[:], I["const_wide"]).then_inc(consts_in, 16)
            pool.dma_start(ohot[:].rearrange("p a b -> p (a b)"), I["const_rows"]).then_inc(table_in, 16)
            pool.dma_start(tab[0:BUCKETS, :], I["rel_table_2"]).then_inc(table_in, 16)
            nc.gpsimd.memset(tab[BUCKETS:BUCKETS + 1, :], NEG).then_inc(set_up, 1)

            ln_params = [(I["ln_in_g"], I["ln_in_b"])] + [(I["ln_g"][0, i], I["ln_b"][0, i]) for i in range(3)] + \
                [(I["ln_g_2"][a, i], I["ln_b_2"][a, i]) for a in range(2) for i in range(3)]

            def load_gb(n):
                if n:
                    pool.wait_ge(ln_done, n)
                for k in range(2):
                    pool.dma_start(gb[:, k, :], across(ln_params[n][k])).then_inc(gb_in, 16)

            def across(row):
                return bass.AP(tensor=row.tensor, offset=row.offset, ap=[[0, P]] + list(row.ap))

            load_gb(0)
            small_loads = {
                "wff": (wff, kxn(I["w_in"][0])[:, :, 768:772]), "foxb": (foxb, across(I["fox_fb"][0])),
                "lam0": (lamv[:, 0], across(I["lam_q1"][0])), "lam1": (lamv[:, 1], across(I["lam_k1"][0])),
                "lam2": (lamv[:, 2], across(I["lam_q2"][0])), "lam3": (lamv[:, 3], across(I["lam_k2"][0])),
                "dng": (dng[0:64], I["diff_norm_g"][0].rearrange("(p a) -> p a", a=1)),
                "dng2": (dng[64:128], I["diff_norm_g"][0].rearrange("(p a) -> p a", a=1)),
                "hng": (hng, I["hgrn_norm_g"][0].rearrange("(p a) -> p a", a=1)),
                "rw1": (rw1, kxn(I["router_w"])), "rb1": (rb1, across(I["router_b"])),
                "rw2": (rw2, kxn(I["moe_w_router_2"][0])), "ckvg": (ckvg, across(I["ev_ckv_gain_2"][0])),
                "sinks": (sinks, across(I["ev_sinks_2"][0])),
                "wuk": (wuk[:], I["ev_w_uk_2"][0].rearrange("(a b) d c -> (b d) a c", b=2)),
                "wuv": (wuv[:], I["ev_w_uv_2"][0].rearrange("h c d -> c h d")),
                "w2k": (w2kv[:, 0], I["od_w2_k_2"][0]), "w2v": (w2kv[:, 1], I["od_w2_v_2"][0]),
            }
            assert list(small_loads) == SMALL_LOADS
            for dst, src in small_loads.values():
                pool.dma_start(dst, src, allow_slow_non_contiguous=True).then_inc(params_in, 16)
            for b in range(2):
                for k, name in enumerate(("od_pe_k_2", "od_pe_v_2")):
                    pool.dma_start(peT[64 * b:64 * b + 64, k], I[name][0].rearrange("j d -> d j"),
                                   allow_slow_non_contiguous=True).then_inc(params_in, 16)

            pool.wait_ge(proj_saved, saved("bias rows"))
            pool.dma_start(rows_dram, rowbuf).then_inc(rows_out, 16)

            def hankel_rows(heads, variant):
                src = bass.AP(tensor=rows_dram.tensor, offset=heads[0] * 2 * ROW_W + variant * ROW_W,
                              ap=[[1, P], [2 * ROW_W, len(heads)], [1, BIAS_W]])
                pool.dma_start(hankel[:, heads[0]:heads[0] + len(heads), :], src).then_inc(rows_back, 16)

            load_gb(1)
            for lv, b in enumerate(LEVELS):
                pool.wait_ge(hg_exp, lv + 1)
                if lv >= 2:
                    pool.wait_ge(hg_scores, 2 * (lv - 1) - 1)
                for side, src in enumerate((hkT, hqT)):
                    def view(x):
                        return x.rearrange("p h t -> p (h t)").rearrange("p (n a b) -> p n a b", a=2, b=b)[:, :, side, :]
                    ins = nc.gpsimd.tensor_tensor(view(Wlv[:, lv % 2]), view(decay[:, lv % 2]), view(src), ALU.mult)
                ins.then_inc(hg_w, 1)
            load_gb(2)
            load_gb(3)
            pool.dma_start(mem_tok, I["mem_2"][0].rearrange("(t p) d -> p t d", p=P)).then_inc(mem2_in, 16)
            pool.wait_ge(rows_out, 16)
            hankel_rows(list(range(8)), 0)
            hankel_rows(list(range(8, 16)), 1)
            for n in range(4, 7):
                load_gb(n)
            hankel_rows(list(range(8, 16)), 0)
            for n in range(7, 10):
                load_gb(n)

        def per_step_pair(fori, steps, head, tail):
            head(0, 0)
            with fori(0, (steps - 1) // 2) as i:
                head(i, 1)
                tail(i, 0)
                head(i + 1, 0)
                tail(i, 1)
            n = (steps - 1) // 2
            if steps % 2 == 0:
                head(n, 1)
            tail(n, 0)
            if steps % 2 == 0:
                tail(n, 1)

        @block.tensor
        def _(pe):
            mm = nc.tensor.matmul

            def weights(c):
                pe.wait_ge(w_in[c % RING], ready_at[c])
                _, kt, w = chunks[c]
                return wview(c, kt, w)

            def emit(u):
                stage, kind, args, dest, _, _ = units[u]
                bank = B[2 + u % 2]
                if u >= 2:
                    pe.wait_ge(proj_saved, u - 1)
                if kind == "T":
                    x, c, kt, w, _, _ = args
                    wt = weights(c)
                    for j in range(2):
                        for k in range(kt):
                            last = mm(bank[:, T * j:T * j + T], wt[:, k, P * j:P * j + P], x[:, k, :],
                                      start=(k == 0), stop=(k == kt - 1))
                elif kind == "tok":
                    x, c, kt, w, c0, n = args
                    wt = weights(c) if c is not None else {"mix1": wff, "router1": rw1, "router2": rw2}[stage]
                    for t in range(TT):
                        for k in range(kt):
                            last = mm(bank[:, n * t:n * t + n], x[:, k, P * t:P * t + P], wt[:, k, c0:c0 + n],
                                      start=(k == 0), stop=(k == kt - 1))
                elif kind == "dup":
                    x, c, kt, w, c0, groups_ = args
                    wt = weights(c)
                    for g in range(groups_):
                        for b in range(2):
                            for k in range(kt):
                                last = mm(bank[64 * b:64 * b + 64, T * g:T * g + T], wt[:, k, 64 * g:64 * g + 64],
                                          x[:, k, :], start=(k == 0), stop=(k == kt - 1))
                elif kind == "tr":
                    src, j0 = args
                    for j in range(2):
                        for t in range(TT):
                            last = nc.tensor.transpose(bank[:, T * j + P * t:T * j + P * t + P],
                                                       src[:, t, P * (j0 + j):P * (j0 + j) + P], eye)
                elif kind == "ctr":
                    for t in range(TT):
                        last = nc.tensor.transpose(bank[:, P * t:P * t + P], ckv[:, t, :], eye)
                elif kind == "pctr":
                    for a in range(2):
                        for t in range(TT):
                            blk = Pc[:, args[0], t, 4 * a:4 * a + 4, :].rearrange("p a b -> p (a b)")
                            last = nc.tensor.transpose(bank[:, T * a + P * t:T * a + P * t + P], blk, eye)
                elif kind == "row":
                    last = mm(bank[0:16, :], tab[:], ohot[:, args[0], :], start=True, stop=True)
                elif kind == "flip":
                    last = mm(bank[:, 0:BIAS_W], flip, hankel[:, args[0], :], start=True, stop=True)
                elif kind == "cum":
                    for t in range(TT):
                        for st in range(TT):
                            last = mm(bank[:, FOX_H * t:FOX_H * t + FOX_H], tri[:, st, P * t:P * t + P],
                                      nlogf[:, st, :], start=(st == 0), stop=(st == TT - 1))
                elif kind == "sumsq":
                    lhs, sq, _ = args
                    last = mm(bank[:, :], lhs, sq.rearrange("p a b -> p (a b)"), start=True, stop=True)
                elif kind == "uk":
                    for a in range(2):
                        j = args[0] + 2 * a
                        last = mm(bank[:, T * a:T * a + T], wuk[half(j), j // 2, :], qaT[half(j), j // 2, :],
                                  start=True, stop=True)
                elif kind == "idx":
                    j = args[0]
                    for t in range(TT):
                        last = mm(bank[:, T * t:T * t + T], qiT[half(j), j // 2, P * t:P * t + P], kiT[half(j), :],
                                  start=True, stop=True)
                elif kind == "uv":
                    for a in range(2):
                        last = mm(bank[64 * a:64 * a + 64, 0:T], wuv[:, 2 * args[0] + a, :],
                                  olatT[:, 2 * args[0] + a, :], start=True, stop=True)
                elif kind == "cb":
                    for t in range(TT):
                        for n in range(N_CMP):
                            o = 255 + P * t - 16 * n - 31
                            last = mm(bank[:, 16 * (N_CMP * t + n):16 * (N_CMP * t + n) + 16], ohot[:, 2, o:o + P],
                                      tab[:], start=True, stop=True)
                elif kind == "hidden":
                    br, g, cs = args
                    rows = slice(64 * g, 64 * g + 64)
                    for j in range(32):
                        wt = weights(cs[j // 16]) if j % 16 == 0 else wt
                        last = mm(bank[:, 0:N_CMP], wt[rows, j % 16, :], kvcT[rows, br, j:j + 16 * (N_CMP - 1) + 1:16],
                                  start=(j == 0), stop=(j == 31))
                    for j in range(32):
                        wt = wview(cs[j // 16], 16, 128)
                        last = mm(bank[:, 16:17], wt[rows, j % 16, :], peT[rows, br, j:j + 1],
                                  start=(j == 0), stop=(j == 31))
                elif kind == "kc":
                    for g in range(2):
                        for b in range(2):
                            last = mm(bank[64 * b:64 * b + 64, 32 * g:32 * g + 32], w2kv[:, 0, :], geluT[:, 0, g, :],
                                      start=True, stop=True)
                elif kind == "vc":
                    for g in range(2):
                        for b in range(4):
                            last = mm(bank[32 * b:32 * b + 32, 64 * g:64 * g + 64], geluT[:, 1, g, :], w2kv[:, 1, :],
                                      start=True, stop=True)
                last.then_inc(proj_ready, 1)

            def run(stage):
                for u in range(*span(stage)):
                    emit(u)

            def add(stage, kt=KT):
                for a in range(*add_span(stage)):
                    _, c, kt, j = adds[a]
                    bank = F[a % 4]
                    if a >= 4:
                        pe.wait_ge(res_added, a - 3)
                    wt = weights(c)
                    for t in range(TT):
                        for k in range(kt):
                            last = mm(bank[:, COLS * t:COLS * t + COLS], yT[:, k, P * t:P * t + P], wt[:, k, :],
                                      start=(k == 0), stop=(k == kt - 1))
                    last.then_inc(res_ready, 1)

            def logits(m):
                mp, bank = maps[m], F[m % 2]
                if m >= 2:
                    pe.wait_ge(scored, m - 1)
                for t in range(TT):
                    n = len(mp["qk"]) + (TT if "fox" in mp else 0)
                    for i, (q, k) in enumerate(mp["qk"]):
                        last = mm(bank[:, T * t:T * t + T], q[:, P * t:P * t + P], k, start=(i == 0), stop=(i == n - 1))
                    if "fox" in mp:
                        for st in range(TT):
                            g = nlogf[:, st, mp["fox"]:mp["fox"] + 1].broadcast_to([P, P])
                            last = mm(bank[:, T * t:T * t + T], g, tri[:, st, :], start=False, stop=(st == TT - 1))
                last.then_inc(logits_ready, 1)

            def transpose_probs(m):
                pe.wait_ge(probs_ready, m + 1)
                if m >= 2:
                    pe.wait_ge(pt_saved, m - 1)
                for k in range(TT):
                    for t in range(TT):
                        last = nc.tensor.transpose(F[2 + m % 2][:, T * k + P * t:T * k + P * t + P],
                                                   S[:, m % NS, t, P * k:P * k + P], eye)
                last.then_inc(pt_ready, 1)

            def values(m):
                mp = maps[m]
                g = mp["group"]
                bank = B[g % 2]
                if mp["new"] and g >= 2:
                    pe.wait_ge(o_saved, g - 1)
                base, width = mp["base"], mp["v"].shape[2]
                first = mp["first"]
                if mp.get("compressed") is not None:
                    j = mp["compressed"]
                    rows = slice(32 * (j // 2 % 4), 32 * (j // 2 % 4) + N_CMP)
                    mm(bank[base:base + 64, 0:T], vc4[rows, j // 8, :], pcT[rows, j % 2, j // 8, :], start=True,
                       stop=False)
                    first = False
                pe.wait_ge(pt_saved, m + 1)
                for piece in range(0, width, P):
                    w = min(P, width - piece)
                    for k in range(TT):
                        last = mm(bank[base:base + w, 2 * piece:2 * piece + T], mp["v"][:, k, piece:piece + w],
                                  PT[:, m % 2, k, :], start=(first and k == 0), stop=(mp["last"] and k == TT - 1))
                last.then_inc(pv_done, 1)

            def attend(stage):
                m0, m1, _, _ = map_span[stage]
                for i in range(m0, m1 + 3):
                    if i < m1:
                        logits(i)
                    if m0 <= i - 2 < m1:
                        transpose_probs(i - 2)
                    if m0 <= i - 3:
                        values(i - 3)
                pe.wait_ge(o_saved, groups_end(stage))

            def hgrn():
                pend = []

                def level_values():
                    j, lv, hp = pend.pop(0)
                    pe.wait_ge(hg_masked, j + 1)
                    for n in range(4):
                        head = n if lv == 0 else 2 * hp + n // 2
                        i = 1 if lv == 0 else n % 2
                        s = 0 if lv == 0 else i
                        last = mm(B[head // 2][:, T * (head % 2) + P * i:T * (head % 2) + P * i + P],
                                  hi[:, s, P * head:P * head + P], SM[:, j % 3, P * n:P * n + P],
                                  start=(lv == 0 and n % 2 == 0), stop=(lv == len(LEVELS)), skip_group_check=True)
                    last.then_inc(hg_pv, 1)

                j = 0
                for lv in range(len(LEVELS) + 1):
                    if lv < len(LEVELS):
                        pe.wait_ge(hg_w, lv + 1)
                    key = Wlv[:, lv % 2] if lv < len(LEVELS) else hkT
                    query = Wlv[:, lv % 2] if lv < len(LEVELS) else hqT
                    for hp in range(1 if lv == 0 else 2):
                        if j >= 4:
                            pe.wait_ge(hg_masked, j - 3)
                        for n in range(4):
                            if lv == 0:
                                a, b = key[:, n, 0:P], query[:, n, P:T]
                            else:
                                head, i = 2 * hp + n // 2, n % 2
                                a, b = key[:, head, P * i:P * i + P], query[:, head, P * i:P * i + P]
                            last = mm(F[j % 4][:, P * n:P * n + P], a, b, start=True, stop=True)
                        last.then_inc(hg_scores, 1)
                        pend.append((j, lv, hp))
                        if len(pend) > 1:
                            level_values()
                        j += 1
                level_values()

            def expert_steps(name):
                first, steps, before = phases[name]

                def landed_(i, par, part):
                    c = first + 3 * par + part
                    pe.wait_ge(w_in[c % RING], i * 16 + ready_at[c])
                    return wview(c, KT if part < 2 else 2, COLS if part < 2 else D)

                def gate_up(i, par):
                    for f in range(2):
                        n = 2 * (before + par) + f
                        pe.wait_ge(hid_ready, i * 4 + (n + 1))
                        for part in range(2):
                            wt = landed_(i, par, part)
                            for k in range(KT):
                                last = mm(F[n % 4][:, T * part:T * part + T], wt[:, k, P * f:P * f + P], hT[:, k, :],
                                          start=(k == 0), stop=(k == KT - 1))
                        last.then_inc(gu_ready, 1)

                def down(i, par):
                    s = before + par
                    pe.wait_ge(hid_ready, i * 4 + (2 * s + 2 + CREDIT))
                    wt = landed_(i, par, 2)
                    for j in range(4):
                        t, c = j // 2, j % 2
                        pe.wait_ge(y_added, i * 8 + (4 * s + j + 1))
                        for f in range(2):
                            last = mm(B[j][:, :], hid[:, (2 * s + f) % 4, P * t:P * t + P],
                                      wt[:, f, 512 * c:512 * c + 512], start=(f == 0), stop=(f == 1))
                        last.then_inc(y_ready, 1)

                per_step_pair(nc.tensor.Fori, steps, gate_up, down)
                pe.wait_ge(y_added, 4 * (before + steps) + CREDIT)

            pe.wait_ge(consts_in, 16)
            pe.wait_ge(mem_in, 16)
            run("mem1 transposed")
            pe.wait_ge(proj_saved, saved("mem1 transposed"))
            run("mem1 keys")
            run("mem1 values")
            pe.wait_ge(table_in, 32)
            pe.wait_ge(set_up, 1)
            run("bias rows")
            pe.wait_ge(ln_done, 1)
            run("ln0 transposed")
            pe.wait_ge(proj_saved, saved("ln0 transposed"))
            pe.wait_ge(params_in, 16 * N_PARAMS)
            run("mix1")
            pe.wait_ge(logf_ready, 1)
            run("forget sums")
            pe.wait_ge(proj_saved, saved("forget sums"))
            attend("mix1")
            hgrn()
            pe.wait_ge(squares_ready, 2)
            run("mean squares")
            pe.wait_ge(y_normed, 2)
            add("out1")
            pe.wait_ge(ln_done, 2)
            run("ln1 transposed")
            pe.wait_ge(proj_saved, saved("ln1 transposed"))
            run("mem1 queries")
            pe.wait_ge(proj_saved, saved("mem1 queries"))
            attend("mem1")
            add("mem1 out")
            pe.wait_ge(ln_done, 3)
            run("ln2 transposed")
            pe.wait_ge(proj_saved, saved("ln2 transposed"))
            run("router1")
            pe.wait_ge(proj_saved, saved("router1"))
            expert_steps("moe1")
            pe.wait_ge(rows_back, 32)
            run("bias tiles 0")
            pe.wait_ge(mem2_in, 16)
            run("mem2 transposed")
            pe.wait_ge(proj_saved, saved("mem2 transposed"))
            for i in range(2):
                if i == 1:
                    pe.wait_ge(rows_back, 48)
                    run("bias tiles 1")
                run(f"xa{i} keys")
                run(f"xa{i} values")
                pe.wait_ge(ln_done, 3 * i + 4)
                run(f"ln{3 * i + 3} transposed")
                pe.wait_ge(proj_saved, saved(f"ln{3 * i + 3} transposed"))
                if i == 0:
                    run("mix2")
                    pe.wait_ge(proj_saved, saved("mix2"))
                    run("indexer")
                    run("mix2b")
                    pe.wait_ge(proj_saved, saved("mix2b"))
                    run("latent queries")
                    pe.wait_ge(latents_ready, 1)
                    run("latent keys")
                    pe.wait_ge(proj_saved, saved("latent keys"))
                    attend("mix2")
                    run("latent out")
                    pe.wait_ge(proj_saved, saved("latent out"))
                    add("out2")
                else:
                    run("mix3")
                    run("compressed bias")
                    pe.wait_ge(proj_saved, saved("mix3"))
                    run("compress hidden")
                    pe.wait_ge(proj_saved, saved("compress hidden"))
                    run("compress out")
                    pe.wait_ge(proj_saved, saved("compress out"))
                    for par in range(2):
                        a = add_span("compressed logits")[0] + par
                        pe.wait_ge(res_added, a - 3)
                        for t in range(TT):
                            for jj in range(8):
                                j = 2 * jj + par
                                o = 256 * t + 32 * jj
                                last = mm(F[a % 4][:, o:o + N_CMP], qcT[half(j), j // 2, P * t:P * t + P],
                                          kcT[half(j), j // 8, 0:N_CMP], start=True, stop=True)
                        last.then_inc(res_ready, 1)
                    pe.wait_ge(cmp_ready, 1)
                    run("compressed probs")
                    pe.wait_ge(proj_saved, saved("compressed probs"))
                    attend("mix3")
                    add("out3")
                pe.wait_ge(ln_done, 3 * i + 5)
                run(f"ln{3 * i + 4} transposed")
                pe.wait_ge(proj_saved, saved(f"ln{3 * i + 4} transposed"))
                run(f"xa{i} queries")
                pe.wait_ge(proj_saved, saved(f"xa{i} queries"))
                attend(f"xa{i}")
                add(f"xa{i} out")
                pe.wait_ge(ln_done, 3 * i + 6)
                run(f"ln{3 * i + 5} transposed")
                pe.wait_ge(proj_saved, saved(f"ln{3 * i + 5} transposed"))
                if i == 1:
                    run("router2")
                    pe.wait_ge(proj_saved, saved("router2"))
                expert_steps("dense" if i == 0 else "moe2")

        @block.scalar
        def _(act):
            step = Tally(act, act_step)
            asked = [0]
            ap_ = nc.scalar.activation

            def request():
                asked[0] += 1
                act.wait_ge(to_act, asked[0])

            def answer(ins):
                ins.then_inc(from_act, 1)

            def root():
                request()
                answer(ap_(std, veps, ACT.Sqrt))

            def save(stage):
                for u in range(*span(stage)):
                    _, kind, args, dest, func, scale = units[u]
                    bank = B[2 + u % 2]
                    act.wait_ge(proj_ready, u + 1)
                    if kind in ("T", "tr", "pctr", "uk"):
                        ins = ap_(dest, pair(bank), func, scale=scale)
                    elif kind == "tok":
                        ins = ap_(dest, pair(bank, args[5]), func, scale=scale)
                    elif kind == "dup":
                        ins = ap_(dest, pair(bank) if args[5] == 2 else bank[:, 0:T], func, scale=scale)
                    elif kind in ("ctr", "uv"):
                        ins = ap_(dest, bank[:, 0:T], func)
                    elif kind == "idx":
                        if args[0] >= 2:
                            act.wait_ge(idx_used, args[0] - 1)
                        ins = ap_(dest, pair(bank), func, scale=scale)
                    elif kind == "row":
                        ins = ap_(dest, bank[0:16, :], func)
                    elif kind == "flip":
                        ins = ap_(dest, bank[:, 0:BIAS_W], func)
                    elif kind == "cum":
                        ins = ap_(dest, bank[:, 0:TT * FOX_H].rearrange("p (a b) -> p a b", a=TT), func, scale=scale)
                    elif kind == "sumsq":
                        step.did(ap_(dest, pair(bank), ACT.Ln, bias=pbias[:, 0:1], scale=args[2]))
                        step.wait()
                        ins = ap_(dest, dest, ACT.Exp, scale=-0.5)
                    elif kind == "cb":
                        for par in range(2):
                            for t in range(TT):
                                src = bank[:, 240 * t:240 * t + 240].rearrange("p (n j r) -> p r j n", r=2, j=8)[:, par]
                                ins = ap_(bcmp[:, par, t, :, 0:N_CMP], src, func)
                    elif kind == "hidden":
                        pe_col = pbias[:, 1 + 2 * args[0] + args[1]:2 + 2 * args[0] + args[1]]
                        step.did(ap_(pe_col, bank[:, 16:17], ACT.Copy))
                        step.wait()
                        ins = ap_(dest, bank[:, 0:N_CMP], ACT.Gelu_apprx_tanh, bias=pe_col)
                    elif kind == "kc":
                        ins = ap_(dest, bank[:, 0:64].rearrange("p (a b) -> p a b", a=2), func)
                    elif kind == "vc":
                        ins = ap_(dest, bank[:, 0:128].rearrange("p (a b) -> p a b", a=2), func)
                    ins.then_inc(proj_saved, 1)

            def exps(m):
                mp, s = maps[m], m % NS
                act.wait_ge(max_ready, m + 1)
                if "sink" in mp:
                    j = mp["sink"]
                    ap_(esink[:, s], nmx[:, s], ACT.Exp, bias=sinks[:, j:j + 1])
                for t in range(TT):
                    ins = ap_(S[:, s, t], S[:, s, t], ACT.Exp, bias=nmx[:, s, t:t + 1], accum_out=ssum[:, s, t:t + 1])
                ins.then_inc(exp_ready, 1)

            def save_probs(m):
                act.wait_ge(pt_ready, m + 1)
                if m >= 2:
                    act.wait_ge(pv_done, m - 1)
                ap_(PT[:, m % 2], pair(F[2 + m % 2]), ACT.Copy).then_inc(pt_saved, 1)

            def save_group(g):
                last, dest = groups[g]
                act.wait_ge(pv_done, last + 1)
                bank = B[g % 2]
                src = pair(bank) if len(dest.shape) == 3 else bank[:, 0:T]
                ap_(dest, src, ACT.Copy).then_inc(o_saved, 1)

            def attend(stage):
                m0, m1, _, _ = map_span[stage]
                for i in range(m0, m1 + 3):
                    if i < m1:
                        exps(i)
                    if m0 <= i - 2 < m1:
                        save_probs(i - 2)
                    if m0 <= i - 3 and maps[i - 3]["end"]:
                        save_group(maps[i - 3]["group"])

            def expert_steps(name):
                first, steps, before = phases[name]

                def one(i, par):
                    for f in range(2):
                        n = 2 * (before + par) + f
                        act.wait_ge(gu_ready, i * 4 + (n + 1))
                        act.wait_ge(hid_ready, i * 4 + (n - 1 + CREDIT))
                        ap_(sg[:, n % 2], F[n % 4][:, 0:T], ACT.Silu).then_inc(sg_ready, 1)
                with nc.scalar.Fori(0, steps // 2) as i:
                    one(i, 0)
                    one(i, 1)
                if steps % 2:
                    one(steps // 2, 0)

            root()
            request()
            answer(ap_(lame, lams, ACT.Exp))
            save("mem1 transposed")
            save("mem1 keys")
            save("mem1 values")
            save("bias rows")
            save("ln0 transposed")
            save("mix1")
            request()
            step.did(ap_(ffe, ffa, ACT.Exp, scale=-1.0))
            step.wait()
            answer(ap_(ffe, ffe, ACT.Ln, bias=1.0))
            request()
            step.did(ap_(hkT, bcT, ACT.Exp, scale=-1.0))
            step.wait()
            step.did(ap_(bcT, hkT, ACT.Ln, bias=1.0))
            step.wait()
            answer(ap_(hkT, hfT, ACT.Sigmoid, scale=-1.0))
            save("forget sums")
            act.wait_ge(rows_out, 16)
            attend("mix1")
            for lv in range(len(LEVELS)):
                act.wait_ge(hg_arg, lv + 1)
                ap_(decay[:, lv % 2], decay[:, lv % 2], ACT.Exp).then_inc(hg_exp, 1)
            act.wait_ge(hg_pv, 2 * len(LEVELS) + 1)
            for a in range(2):
                ins = ap_(oT[:, 2 * a:2 * a + 2, :], pair(B[a]), ACT.Copy)
            answer(ins)
            save("mean squares")
            root()
            save("ln1 transposed")
            save("mem1 queries")
            attend("mem1")
            root()
            save("ln2 transposed")
            save("router1")
            expert_steps("moe1")
            root()
            save("bias tiles 0")
            save("mem2 transposed")
            for i in range(2):
                if i == 1:
                    root()
                    save("bias tiles 1")
                save(f"xa{i} keys")
                save(f"xa{i} values")
                save(f"ln{3 * i + 3} transposed")
                if i == 0:
                    save("mix2")
                    request()
                    answer(ap_(cstd, css, ACT.Sqrt))
                    save("indexer")
                    save("mix2b")
                    save("latent queries")
                    save("latent keys")
                    attend("mix2")
                    save("latent out")
                else:
                    save("mix3")
                    save("compressed bias")
                    act.wait_ge(cmp_cleared, 1)
                    save("compress hidden")
                    save("compress out")
                    request()
                    pc = Pc.rearrange("p r t j n -> p (r t j) n")[:, :, 0:N_CMP]
                    answer(ap_(pc, pc, ACT.Exp))
                    save("compressed probs")
                    attend("mix3")
                root()
                save(f"ln{3 * i + 4} transposed")
                save(f"xa{i} queries")
                attend(f"xa{i}")
                root()
                save(f"ln{3 * i + 5} transposed")
                if i == 1:
                    save("router2")
                    request()
                    e = route[:, 16:32]
                    answer(ap_(e, e, ACT.Exp))
                expert_steps("dense" if i == 0 else "moe2")
            root()

        @block.vector
        def _(dve):
            V = nc.vector
            step = Tally(dve, dve_step)
            answered = [0]

            def ask(ins):
                ins.then_inc(to_act, 1)
                answered[0] += 1

            def answer():
                dve.wait_ge(from_act, answered[0])

            def do(ins):
                step.did(ins)
                step.wait()

            norms = [0]

            def layer_norm():
                n = norms[0]
                norms[0] += 1
                for t in range(TT):
                    for a in range(2):
                        ins = V.bn_stats(stats[:, t, a, :], h[:, t, 512 * a:512 * a + 512])
                do(ins)
                for t in range(TT):
                    ins = V.bn_aggr(mvar[:, t, :], stats[:, t])
                do(ins)
                ask(V.tensor_scalar(veps, mvar[:, :, 1], EPS, None, ALU.add))
                answer()
                do(V.reciprocal(rstd, std))
                for t in range(TT):
                    ins = V.tensor_scalar(h[:, t], h[:, t], mvar[:, t, 0:1], rstd[:, t:t + 1], ALU.subtract, ALU.mult)
                do(ins)
                dve.wait_ge(gb_in, 32 * (n + 1))
                for t in range(TT):
                    ins = V.tensor_tensor(h[:, t], h[:, t], gb[:, 0], ALU.mult)
                do(ins)
                for t in range(TT):
                    ins = V.tensor_tensor(h[:, t], h[:, t], gb[:, 1], ALU.add)
                ins.then_inc(ln_done, 1)
                dve.wait_ge(ln_done, n + 1)

            def add(stage, alpha):
                for a in range(*add_span(stage)):
                    j = adds[a][3]
                    hs = h[:, :, COLS * j:COLS * j + COLS]
                    dve.wait_ge(res_ready, a + 1)
                    V.scalar_tensor_tensor(out=hs, in0=hs, scalar=alpha, in1=pair(F[a % 4]), op0=ALU.mult,
                                           op1=ALU.add).then_inc(res_added, 1)
                dve.wait_ge(res_added, add_span(stage)[1])

            def score_map(m):
                mp, s = maps[m], m % NS
                bank = pair(F[m % 2])
                dve.wait_ge(logits_ready, m + 1)
                if m >= NS:
                    dve.wait_ge(pt_ready, m - NS + 1)
                if "fox" in mp:
                    j = mp["fox"]
                    for t in range(TT):
                        ins = V.scalar_tensor_tensor(out=S[:, s, t], in0=bank[:, t], scalar=cumq[:, t, j:j + 1],
                                                     in1=mp["mask"][:, t], op0=ALU.add, op1=ALU.add)
                elif "mask" in mp:
                    ins = V.tensor_tensor(S[:, s], bank, mp["mask"], ALU.add)
                else:
                    ins = V.tensor_copy(S[:, s], bank)
                ins.then_inc(scored, 1)
                dve.wait_ge(scored, m + 1)
                if "extra" in mp:
                    do(V.tensor_tensor(S[:, s], S[:, s], mp["extra"], ALU.add))
                ins = V.tensor_reduce(nmx[:, s], S[:, s], AX.X, ALU.max, negate=True)
                if "sink" in mp:
                    do(ins)
                    j = mp["sink"]
                    ins = V.tensor_scalar(nmx[:, s], nmx[:, s], nsinks[:, j:j + 1], None, ALU.min)
                ins.then_inc(max_ready, 1)

            def normalise(m):
                mp, s = maps[m], m % NS
                dve.wait_ge(exp_ready, m + 1)
                if "sink" in mp:
                    do(V.tensor_tensor(ssum[:, s], ssum[:, s], esink[:, s], ALU.add))
                do(V.reciprocal(rsum[:, s], ssum[:, s]))
                if mp.get("coef") is not None:
                    do(V.tensor_tensor(rsum[:, s], rsum[:, s], mp["coef"], ALU.mult))
                for t in range(TT):
                    ins = V.tensor_scalar(S[:, s, t], S[:, s, t], rsum[:, s, t:t + 1], None, ALU.mult)
                ins.then_inc(probs_ready, 1)

            def attend(stage):
                m0, m1, _, _ = map_span[stage]
                for i in range(m0, m1 + 1):
                    if i < m1:
                        score_map(i)
                    if m0 <= i - 1:
                        normalise(i - 1)

            def chosen(src, groups_, n, k, lower, rank, sel):
                shape = [P, groups_, n, n]
                gt = route[:, 400:400 + groups_ * n * n].rearrange("p (g j i) -> p g j i", j=n, i=n)
                ge = route[:, 600:600 + groups_ * n * n].rearrange("p (g j i) -> p g j i", j=n, i=n)
                low = lower.rearrange("p (j i) -> p j i", j=n)
                other = src.unsqueeze(2).broadcast_to(shape)
                own = src.unsqueeze(3).broadcast_to(shape)
                V.tensor_tensor(gt, other, own, ALU.is_gt)
                do(V.tensor_tensor(ge, other, own, ALU.is_ge))
                for g in range(groups_):
                    ins = V.tensor_tensor(ge[:, g], ge[:, g], low, ALU.mult)
                do(ins)
                do(V.tensor_tensor(gt, gt, ge, ALU.max))
                do(V.tensor_reduce(rank, gt, AX.X, ALU.add))
                do(V.tensor_scalar(sel, rank, k - 0.5, None, ALU.is_lt))

            def spread_gates(gates, n_exp, per):
                do(V.tensor_copy(step_gate[:, :, 0:n_exp * per].rearrange("p t (e s) -> p t e s", s=per),
                                 gates.unsqueeze(3).broadcast_to([P, TT, n_exp, per])))

            def route1():
                r_ = Slots(route, TT * E1)
                sc = route[:, 0:32].rearrange("p (a b) -> p a b", a=TT)
                biased, sel, gates, rank = (r_.get(32) for _ in range(4))
                gs, grank, gsel, tot = r_.get(8), r_.get(8), r_.get(8), r_.get(2)
                dve.wait_ge(proj_saved, saved("router1"))
                v3 = lambda x: x.rearrange("p (a b) -> p a b", a=TT)
                v8 = lambda x: x.rearrange("p (g n) -> p g n", n=4)
                do(V.tensor_tensor(v3(biased), sc, rb1.unsqueeze(1).broadcast_to([P, TT, E1]), ALU.add))
                chosen(v8(biased), 8, 4, 2, const("lower4"), v8(rank), v8(sel))
                do(V.tensor_tensor(gates, biased, sel, ALU.mult))
                do(V.tensor_reduce(gs, v8(gates), AX.X, ALU.add))
                g2 = lambda x: x.rearrange("p (a b) -> p a b", a=TT)
                chosen(g2(gs), 2, 4, 1, const("lower4"), g2(grank), g2(gsel))
                do(V.tensor_tensor(v8(sel), v8(sel), gsel.unsqueeze(2).broadcast_to([P, 8, 4]), ALU.mult))
                do(V.tensor_tensor(gates, route[:, 0:32], sel, ALU.mult))
                do(V.tensor_reduce(tot, v3(gates), AX.X, ALU.add))
                do(V.reciprocal(tot, tot))
                do(V.tensor_tensor(v3(gates), v3(gates), tot.unsqueeze(2).broadcast_to([P, TT, E1]), ALU.mult))
                spread_gates(v3(gates), E1, FF1 // COLS)

            def route2():
                lg = route[:, 0:16]
                e = route[:, 16:32]
                r_ = Slots(route, 32)
                sel, rank, mx, tot = r_.get(16), r_.get(16), r_.get(2), r_.get(2)
                v3 = lambda x: x.rearrange("p (a b) -> p a b", a=TT)
                dve.wait_ge(proj_saved, saved("router2"))
                chosen(v3(lg), 2, 8, 2, const("lower8"), v3(rank), v3(sel))
                do(V.tensor_reduce(mx, v3(lg), AX.X, ALU.max))
                ask(V.tensor_tensor(v3(e), v3(lg), mx.unsqueeze(2).broadcast_to([P, TT, E2]), ALU.subtract))
                answer()
                do(V.tensor_tensor(e, e, sel, ALU.mult))
                do(V.tensor_reduce(tot, v3(e), AX.X, ALU.add))
                do(V.reciprocal(tot, tot))
                do(V.tensor_tensor(v3(e), v3(e), tot.unsqueeze(2).broadcast_to([P, TT, E2]), ALU.mult))
                spread_gates(v3(e), E2, FF2 // COLS)

            def expert_steps(name, alpha):
                first, steps, before = phases[name]
                do(V.tensor_scalar(h[:], h[:], alpha, None, ALU.mult))

                def hidden(i, par):
                    for f in range(2):
                        n = 2 * (before + par) + f
                        dve.wait_ge(sg_ready, i * 4 + (n + 1))
                        V.tensor_tensor(hid[:, n % 4], sg[:, n % 2], F[n % 4][:, T:2 * T], ALU.mult)\
                            .then_inc(hid_ready, 1)

                def gather(i, par):
                    s = before + par
                    for j in range(4):
                        t, c = j // 2, j % 2
                        dve.wait_ge(y_ready, i * 8 + (4 * s + j + 1))
                        dve.wait_ge(y_added, i * 8 + (4 * s + j + 1))
                        hs = h[:, t, 512 * c:512 * c + 512]
                        V.scalar_tensor_tensor(out=hs, in0=B[j][:, :], scalar=step_gate[:, t, bass.ds(i * 2 + par, 1)],
                                               in1=hs, op0=ALU.mult, op1=ALU.add).then_inc(y_added, 1)

                per_step_pair(nc.vector.Fori, steps, hidden, gather)
                dve.wait_ge(y_added, 4 * (before + steps) + CREDIT)

            V.memset(ones[:], 1.0).then_inc(hid_ready, CREDIT)
            V.memset(step_gate[:], 1.0).then_inc(y_added, CREDIT)
            V.memset(pbias[:, 0:1], EPS)
            dve.wait_ge(x_in, 16)
            layer_norm()
            dve.wait_ge(params_in, 16 * N_PARAMS)
            for a in range(2):
                ins = V.tensor_tensor(lamp[:, a], lamv[:, 2 * a], lamv[:, 2 * a + 1], ALU.mult)
            do(ins)
            ask(V.tensor_reduce(lams, lamp, AX.X, ALU.add))
            answer()
            for a in range(2):
                ins = V.tensor_scalar(neglam[:, a:a + 1], lame[:, 1:2], lame[:, 0:1], -LAM_INIT, ALU.subtract, ALU.add)
            V.tensor_scalar(dng, dng, 1.0 - LAM_INIT, None, ALU.mult)
            do(V.tensor_scalar(nsinks, sinks, -1.0, None, ALU.mult))
            dve.wait_ge(proj_saved, saved("mix1"))
            do(V.tensor_tensor(ffx, ffx, foxb.unsqueeze(1).broadcast_to([P, TT, FOX_H]), ALU.add))
            flat = lambda x: x.rearrange("p a b -> p (a b)")
            ask(V.scalar_tensor_tensor(out=flat(ffa), in0=flat(ffx), scalar=-1.0, in1=flat(ffx), op0=ALU.mult,
                                       op1=ALU.max))
            ask(V.scalar_tensor_tensor(out=flat(bcT), in0=flat(hfT), scalar=-1.0, in1=flat(hfT), op0=ALU.mult,
                                       op1=ALU.max))
            answer()
            do(V.scalar_tensor_tensor(out=flat(ffx), in0=flat(ffx), scalar=0.0, in1=flat(ffe), op0=ALU.min,
                                      op1=ALU.subtract))
            V.tensor_scalar(nlogf, ffx, -1.0, None, ALU.mult).then_inc(logf_ready, 1)
            do(V.scalar_tensor_tensor(out=flat(bcT), in0=flat(hfT), scalar=0.0, in1=flat(bcT), op0=ALU.min,
                                      op1=ALU.subtract))
            for j in range(HGRN_H):
                ins = V.tensor_tensor_scan(hfT[:, j], ones[:], bcT[:, j], 0.0, ALU.mult, ALU.add)
            do(ins)
            dve.wait_ge(proj_saved, saved("forget sums"))
            attend("mix1")
            dve.wait_ge(o_saved, groups_end("mix1"))
            V.tensor_tensor(dsq, yT[:, 2:4], yT[:, 2:4], ALU.mult).then_inc(squares_ready, 1)

            def level_argument(lv):
                b = LEVELS[lv]
                cut = lambda x: x.rearrange("p h t -> p (h t)").rearrange("p (n a b) -> p n a b", a=2, b=b)
                src, dst = cut(hfT), cut(decay[:, lv % 2])
                ref = src[:, :, 0, b - 1:b].broadcast_to([P, HGRN_H * T // (2 * b), b])
                if lv >= 2:
                    dve.wait_ge(hg_w, lv - 1)
                V.tensor_tensor(dst[:, :, 0, :], ref, src[:, :, 0, :], ALU.subtract)
                V.tensor_tensor(dst[:, :, 1, :], src[:, :, 1, :], ref, ALU.subtract).then_inc(hg_arg, 1)

            j = 0
            level_argument(0)
            for lv in range(len(LEVELS) + 1):
                if lv + 1 < len(LEVELS):
                    level_argument(lv + 1)
                for hp in range(1 if lv == 0 else 2):
                    dve.wait_ge(hg_scores, j + 1)
                    if j >= 3:
                        dve.wait_ge(hg_pv, j - 2)
                    if lv == 0:
                        ins = V.tensor_copy(SM[:, j % 3], F[j % 4][:, :])
                    else:
                        ins = V.tensor_tensor(SM[:, j % 3].rearrange("p (a b) -> p a b", a=4),
                                              F[j % 4][:, :].rearrange("p (a b) -> p a b", a=4),
                                              levelmask[:, lv - 1:lv, :].broadcast_to([P, 4, P]), ALU.mult)
                    ins.then_inc(hg_masked, 1)
                    j += 1
            answered[0] += 1
            answer()
            V.tensor_tensor(sqT, oT, oT, ALU.mult).then_inc(squares_ready, 1)
            dve.wait_ge(proj_saved, saved("mean squares"))
            V.scalar_tensor_tensor(out=yT[:, 2:4], in0=yT[:, 2:4], scalar=dng[:, 0:1], in1=drs, op0=ALU.mult,
                                   op1=ALU.mult).then_inc(y_normed, 1)
            do(V.scalar_tensor_tensor(out=oT, in0=oT, scalar=hng[:, 0:1], in1=decay[:, 0], op0=ALU.mult, op1=ALU.mult))
            V.tensor_tensor(yT[:, 4:8], oT, hgT, ALU.mult).then_inc(y_normed, 1)
            add("out1", ALPHA1)
            layer_norm()
            attend("mem1")
            add("mem1 out", ALPHA1)
            layer_norm()
            route1()
            expert_steps("moe1", ALPHA1)
            layer_norm()
            for i in range(2):
                if i == 0:
                    dve.wait_ge(proj_saved, saved("mix2"))
                    for t in range(TT):
                        do(V.tensor_tensor_reduce(out=work[:, t, 0:P], in0=ckv[:, t], in1=ckv[:, t], scale=1.0,
                                                  scalar=0.0, op0=ALU.mult, op1=ALU.add, accum_out=css[:, t:t + 1]))
                    ask(V.tensor_scalar(css, css, 1.0 / P, EPS, ALU.mult, ALU.add))
                    answer()
                    do(V.reciprocal(crstd, cstd))
                    for t in range(TT):
                        ins = V.scalar_tensor_tensor(out=ckv[:, t], in0=ckv[:, t], scalar=crstd[:, t:t + 1],
                                                     in1=ckvg, op0=ALU.mult, op1=ALU.mult)
                    ins.then_inc(latents_ready, 1)
                    for j in range(8):
                        dve.wait_ge(proj_saved, span("indexer")[0] + j + 1)
                        for t in range(TT):
                            ins = V.scalar_tensor_tensor(out=score[:, t], in0=idx_act[:, j % 2, t],
                                                         scalar=wi[:, t, j:j + 1],
                                                         in1=causal[:, t] if j == 0 else score[:, t],
                                                         op0=ALU.mult, op1=ALU.add)
                        ins.then_inc(idx_used, 1)
                        dve.wait_ge(idx_used, j + 1)
                    for rnd in range(TOPK // 8):
                        src = score if rnd == 0 else work
                        for t in range(TT):
                            ins = V.max(m8[:, t], src[:, t])
                        do(ins)
                        for t in range(TT):
                            ins = V.match_replace(work[:, t], m8[:, t], src[:, t], TAKEN)
                        do(ins)
                    do(V.tensor_scalar(work, work, TAKEN / 2, NEG, ALU.is_gt, ALU.mult))
                    attend("mix2")
                    add("out2", ALPHA2)
                else:
                    dve.wait_ge(proj_saved, saved("mix3"))
                    V.memset(Pc, 0.0)
                    V.memset(geluT, 0.0).then_inc(cmp_cleared, 1)
                    dve.wait_ge(cmp_cleared, 1)
                    dve.wait_ge(proj_saved, saved("compressed bias"))
                    pc = Pc.rearrange("p r t j n -> p (r t j) n")
                    for par in range(2):
                        a = add_span("compressed logits")[0] + par
                        dve.wait_ge(res_ready, a + 1)
                        V.tensor_tensor(pc[:, 16 * par:16 * par + 16, 0:N_CMP],
                                        F[a % 4][:, :].rearrange("p (a n) -> p a n", n=32)[:, :, 0:N_CMP],
                                        bcmp[:, par].rearrange("p t j n -> p (t j) n")[:, :, 0:N_CMP],
                                        ALU.add).then_inc(res_added, 1)
                    dve.wait_ge(res_added, add_span("compressed logits")[1])
                    pn = pc[:, :, 0:N_CMP]
                    do(V.tensor_reduce(cmx, pn, AX.X, ALU.max, negate=True))
                    ask(V.tensor_tensor(pn, pn, cmx.unsqueeze(2).broadcast_to([P, 32, N_CMP]), ALU.add))
                    answer()
                    do(V.tensor_reduce(csum, pn, AX.X, ALU.add))
                    do(V.reciprocal(csum, csum))
                    for par in range(2):
                        c2 = csum[:, 16 * par:16 * par + 16].rearrange("p (t j) -> p t j", t=TT)
                        gate = g3[:].rearrange("p t (j r c) -> p r c t j", r=2, c=3)[:, par, 0]
                        ins = V.tensor_tensor(c2, c2, gate, ALU.mult)
                    do(ins)
                    do(V.tensor_tensor(pn, pn, csum.unsqueeze(2).broadcast_to([P, 32, N_CMP]), ALU.mult))
                    for par in range(2):
                        for t in range(TT):
                            x = Pc[:, par, t, :, 0:N_CMP]
                            ins = V.tensor_tensor(x, x, valid[:, t:t + 1, :].broadcast_to([P, 8, N_CMP]), ALU.mult)
                    ins.then_inc(cmp_ready, 1)
                    attend("mix3")
                    add("out3", ALPHA2)
                layer_norm()
                attend(f"xa{i}")
                add(f"xa{i} out", ALPHA2)
                layer_norm()
                if i == 1:
                    route2()
                else:
                    dve.wait_ge(proj_saved, saved("ln5 transposed"))
                    do(V.memset(step_gate[:, :, 0:FF_DENSE // COLS], 1.0))
                expert_steps("dense" if i == 0 else "moe2", ALPHA2)
                layer_norm()


SMALL_LOADS = ["wff", "foxb", "lam0", "lam1", "lam2", "lam3", "dng", "dng2", "hng", "rw1", "rb1", "rw2", "ckvg", "sinks",
               "wuk", "wuv", "w2k", "w2v"]


class Slots:

    def __init__(self, tensor, at):
        self.tensor, self.at = tensor, at

    def get(self, n):
        self.at += n
        assert self.at <= 400
        return self.tensor[:, self.at - n:self.at]


def kernel(**inputs):
    import concourse.bacc as _bacc
    from concourse.bass_utils import run_bass_kernel_spmd as _run

    nc = _bacc.Bacc("TRN2", target_bir_lowering=False, num_devices=1)
    arrays, args = {}, {}
    named = dict(inputs)
    named["const_wide"], named["const_rows"] = CONST_WIDE, CONST_ROWS
    for name, a in named.items():
        a = np.ascontiguousarray(a)
        arrays[f"in_{name}_dram"] = a
        args[name] = nc.dram_tensor(f"in_{name}_dram", a.shape, mybir.dt.from_np(a.dtype), kind="ExternalInput").ap()
    out = nc.dram_tensor("out_0_dram", (1, T, D), F32, kind="ExternalOutput").ap()
    two_block_kernel(nc, args, out)
    r = _run(nc, [arrays], core_ids=[0])
    return r.results[0]["out_0_dram"]
```

```python
import math
from contextlib import ExitStack

import numpy as np

import concourse.bass as bass
from concourse import mybir

ALU = mybir.AluOpType
ACT = mybir.ActivationFunctionType
AX = mybir.AxisListType
F32 = mybir.dt.float32

P = 128
T = 256
TT = T // P
D = 1024
KT = D // P
COLS = 256
RING = 6
SLOT = KT * COLS
CROWD = 128
SLOTS = 128
EPS = 1e-5
NEG = -1e30
TAKEN = -3e38

ALPHA1 = 2.0 ** 0.25
ALPHA2 = 4.0 ** 0.25
FOX_H, DIFF_H, HGRN_H, MEM_H = 4, 4, 4, 4
LAM_INIT = 0.8 - 0.6 * math.exp(0.0)
E1, FF1 = 16, 512
E2, FF2 = 8, 3584
FF_DENSE = 2816
TOPK = T // 4
N_CMP = 15
BUCKETS = 32
LEVELS = [128, 64, 32, 16, 8, 4, 2, 1]
BIAS_W = 384
ROW_W = 512


def shape_constants():
    p = np.arange(P)
    q = np.arange(T)
    eye = np.eye(P)
    flip = np.eye(P)[::-1]
    tri = np.stack([(p[:, None] + P * t <= q[None, :]) for t in range(TT)], 1).reshape(P, -1)
    causal = np.stack([np.where(q[None, :] <= p[:, None] + P * t, 0.0, NEG) for t in range(TT)], 1).reshape(P, -1)
    chunk = np.stack([np.where(q[None, :] // 64 <= (p[:, None] + P * t) // 64, 0.0, NEG) for t in range(TT)],
                     1).reshape(P, -1)
    levels = []
    for b in LEVELS[1:]:
        s, t = p[:, None], p[None, :]
        levels.append((s // (2 * b) == t // (2 * b)) & (s % (2 * b) < b) & (t % (2 * b) >= b))
    levels.append(p[:, None] == p[None, :])
    levels = np.stack(levels, 1).reshape(P, -1)
    halves = (p[:, None] // 64 == p[None, :] // 64)
    ends = 16 * np.arange(N_CMP) + 31
    valid = np.stack([(p[:, None] + P * t >= ends[None, :]) for t in range(TT)], 1).reshape(P, -1)
    lower = lambda n: np.broadcast_to((np.arange(n)[None, :] < np.arange(n)[:, None]).reshape(1, -1), (P, n * n))
    iota = np.broadcast_to(np.arange(SLOTS)[None, :], (P, SLOTS))
    parts = [("iota", iota), ("eye", eye), ("flip", flip), ("tri", tri), ("causal", causal), ("chunk", chunk), ("levels", levels),
             ("halves", halves), ("valid", valid), ("lower4", lower(4)), ("lower8", lower(8))]
    at, off = {}, 0
    for name, a in parts:
        at[name] = (off, a.shape[1])
        off += a.shape[1]
    wide = np.concatenate([np.asarray(a, np.float32) for _, a in parts], 1)

    def bucket(dist):
        n = np.maximum(dist, 1)
        log_b = 16 + (np.log(n / 16.0) / math.log(8.0) * 16).astype(np.int64)
        return np.where(dist < 16, np.maximum(dist, 0), np.minimum(log_b, BUCKETS - 1))

    def onehot(dist, ok):
        m = np.zeros((BUCKETS + 1, len(dist)))
        m[bucket(dist), np.arange(len(dist))] = ok
        m[BUCKETS] = ~ok
        return m
    j = np.arange(ROW_W)
    dist = 255 - j
    fwd = j - 255
    rows = np.stack([onehot(dist, dist >= 0), onehot(dist, (dist >= 0) & (dist < 128)), onehot(fwd, fwd >= 0)], 1)
    return at, np.ascontiguousarray(wide), rows.reshape(BUCKETS + 1, -1).astype(np.float32)


CONST_AT, CONST_WIDE, CONST_ROWS = shape_constants()


class Tally:

    def __init__(self, eng, sem):
        self.eng, self.sem, self.n = eng, sem, 0

    def did(self, ins):
        ins.then_inc(self.sem, 1)
        self.n += 1

    def wait(self):
        self.eng.wait_ge(self.sem, self.n)


def two_block_kernel(nc, I, out):
    ctx = ExitStack()
    with ctx:
        def sb(name, shape):
            return ctx.enter_context(nc.sbuf_tensor(name, shape, F32))[tuple(slice(None) for _ in shape)]

        def sem(name):
            return ctx.enter_context(nc.semaphore(name))

        ring = sb("ring", [P, RING, SLOT])
        h = sb("h", [P, TT, D])
        hT = sb("hT", [P, KT, T])
        yT = sb("yT", [P, KT, T])
        memT = sb("memT", [P, KT, T])
        mkT = sb("mkT", [P, KT, T])
        mv = sb("mv", [P, TT, D])
        gb = sb("gb", [P, 2, D])
        cw = sb("cw", [P, CONST_WIDE.shape[1]])
        NS = 3
        S = sb("S", [P, NS, TT, T])
        PT = sb("PT", [P, 2, TT, T])
        small = sb("small", [P, 1500])
        arena = sb("arena", [P, 15872])

        def const(name):
            o, n = CONST_AT[name]
            return cw[:, o:o + n]
        eye, flip, halves = const("eye"), const("flip"), const("halves")
        tri = const("tri").rearrange("p (a k) -> p a k", a=TT)
        causal = const("causal").rearrange("p (a k) -> p a k", a=TT)
        chunkmask = const("chunk").rearrange("p (a k) -> p a k", a=TT)
        levelmask = const("levels").rearrange("p (a k) -> p a k", a=len(LEVELS))
        valid = const("valid").rearrange("p (t n) -> p t n", t=TT)

        small_used = [0]

        def tiny(*shape):
            n = int(np.prod(shape))
            o = small_used[0]
            small_used[0] += n
            assert small_used[0] <= 1500, small_used
            v = small[:, o:o + n]
            names = " ".join("abcd"[:len(shape)])
            return v if len(shape) == 1 else v.rearrange(f"p ({names}) -> p {names}",
                                                         **{c: s for c, s in zip("abcd", shape)})

        class Region:

            def __init__(self, start=0):
                self.at = start

            def get(self, *shape):
                n = int(np.prod(shape))
                v = arena[:, self.at:self.at + n]
                self.at += n
                assert self.at <= 15872, self.at
                names = " ".join("abcd"[:len(shape)])
                return v if len(shape) == 1 else v.rearrange(f"p ({names}) -> p {names}",
                                                             **{c: s for c, s in zip("abcd", shape)})

        r = Region()
        fqT, fkT, fv = r.get(2, T), r.get(2, T), r.get(TT, 256)
        dqT, dkT, dv = r.get(2, T), r.get(2, T), r.get(TT, 256)
        hqT, hfT, hi, hgT = r.get(4, T), r.get(4, T), r.get(TT, 512), r.get(4, T)
        hkT, bcT = r.get(4, T), r.get(4, T)
        decay = r.get(2, 4, T)
        Wlv = r.get(2, 4, T)
        SM = r.get(3, 512)
        oT, sqT = hqT, hfT
        dsq, drs = r.get(2, T), r.get(2, T)
        r = Region()
        hidden_sg = r.get(2, COLS)
        hidden_tok = r.get(2, COLS)
        hidden_T = r.get(2, 2, SLOTS)
        assert r.at <= 1536
        r = Region(9728)
        acc = r.get(TT, D)
        xgT = r.get(KT, SLOTS)
        y_slots = r.get(D)
        pick, gated = r.get(TT, SLOTS), r.get(TT, SLOTS)
        gatedT = r.get(TT, P)
        mem_tok = Region(1536).get(TT, D)
        hankel = Region(3584).get(16, BIAS_W)
        mqT = Region().get(KT, T)
        r = Region()
        sg = r.get(2, T)
        hid = r.get(4, T)
        biasT = Region(15872 - 16 * BIAS_W).get(16, BIAS_W)
        r = Region()
        qaT, qiT, qbT = r.get(4, T), r.get(4, T), r.get(4, T)
        kiT, kbT, vb = r.get(T), r.get(2, T), r.get(TT, P)
        ckv, cT, qlatT = r.get(TT, P), r.get(T), r.get(8, T)
        olatT = qlatT
        idx_act = r.get(2, TT, T)
        score = r.get(TT, T)
        work = r.get(TT, T)
        assert r.at <= 15872 - 16 * BIAS_W, r.at
        r = Region()
        qcT = r.get(8, T)
        kvcT = r.get(2, T)
        ksT, vs, kwT, vw = r.get(2, T), r.get(TT, P), r.get(2, T), r.get(TT, P)
        Pc = r.get(2, TT, 8, 32)
        bcmp = r.get(2, TT, 8, 16)
        pcT = r.get(2, 2, T)
        geluT = r.get(2, 2, 32)
        kcT = r.get(2, 32)
        vc4 = r.get(2, 64)
        assert r.at <= 15872 - 16 * BIAS_W, r.at

        wff = tiny(KT, FOX_H)
        foxb = tiny(FOX_H)
        lamv = tiny(4, 32)
        dng, hng = tiny(1), tiny(1)
        rw1, rb1, rw2 = tiny(KT, E1), tiny(E1), tiny(KT, E2)
        ckvg = tiny(P)
        sinks = tiny(8)
        peT = tiny(2, 32)
        stats, mvar, veps, std, rstd = tiny(TT, 2, 6), tiny(TT, 2), tiny(TT), tiny(TT), tiny(TT)
        ffx = tiny(TT, FOX_H)
        ffa, ffe, nlogf, cumq = tiny(TT, FOX_H), tiny(TT, FOX_H), tiny(TT, FOX_H), tiny(TT, FOX_H)
        lamp, lams, lame, neglam = tiny(2, 32), tiny(2), tiny(2), tiny(2)
        nmx, ssum, rsum, esink = tiny(NS, TT), tiny(NS, TT), tiny(NS, TT), tiny(NS, TT)
        nsinks = tiny(8)
        wi = tiny(TT, 8)
        css, cstd, crstd = tiny(TT), tiny(TT), tiny(TT)
        m8 = tiny(TT, 8)
        pbias = tiny(5)
        csum, cmx = tiny(32), tiny(32)

        wuk, wuv, w2kv = sb("wuk", [P, 4, P]), sb("wuv", [P, 8, 64]), sb("w2kv", [P, 2, 64])
        tab = sb("tab", [BUCKETS + 1, 16])
        ohot = sb("ohot", [BUCKETS + 1, 3, ROW_W])
        rowbuf = PT[0:16].rearrange("p a b c -> p a (b c)")
        rows_dram = nc.dram_tensor("bias_rows", (16, 2, ROW_W), F32, kind="Internal").ap()
        ones = sb("ones", [P, T])
        route = S[:].rearrange("p a b c -> p (a b c)")[:, 0:1000]
        route_slot, route_gate = tiny(TT, E1 + 1), tiny(TT, E1 + 1)
        route_count = tiny(TT, E1)
        crowded = ctx.enter_context(nc.sbuf_tensor("crowded", [P, 2], mybir.dt.int32))
        g3 = sb("g3", [P, TT, 48])

        F = [ctx.enter_context(nc.psum_tensor(f"psF{i}", [P, 512], F32)) for i in range(4)]
        B = [ctx.enter_context(nc.psum_tensor(f"psB{i}", [P, 512], F32)) for i in range(4)]

        def pair(bank, w=T):
            return bank[:, 0:2 * w].rearrange("p (a b) -> p a b", a=2)

        x_in, mem_in, mem2_in = sem("x_in"), sem("mem_in"), sem("mem2_in")
        consts_in, params_in, table_in = sem("consts_in"), sem("params_in"), sem("table_in")
        gb_in = sem("gb_in")
        w_in = [sem(f"weights_in{i}") for i in range(RING)]
        out_stored = sem("out_stored")
        rows_out, rows_back = sem("bias_rows_out"), sem("bias_rows_back")
        set_up = sem("set_up")
        ln_done, var_ready, std_ready = sem("ln_done"), sem("var_ready"), sem("std_ready")
        proj_ready, proj_saved = sem("proj_ready"), sem("proj_saved")
        res_ready, res_added = sem("res_ready"), sem("res_added")
        logits_ready, scored, max_ready = sem("logits_ready"), sem("scored"), sem("max_ready")
        exp_ready, probs_ready = sem("exp_ready"), sem("probs_ready")
        pt_ready, pt_saved, pv_done, o_saved = sem("pt_ready"), sem("pt_saved"), sem("pv_done"), sem("o_saved")
        dve_step, act_step, pool_step = sem("dve_step"), sem("act_step"), sem("pool_step")
        gu_ready, sg_ready, hid_ready = sem("gate_up_ready"), sem("silu_ready"), sem("hidden_ready")
        y_ready, y_added = sem("y_ready"), sem("y_added")
        to_act, from_act = sem("dve_to_act"), sem("act_to_dve")
        logf_ready = sem("log_forget_ready")
        squares_ready, y_normed = sem("squares_ready"), sem("y_normed")
        latents_ready, penalty_ready = sem("latents_ready"), sem("penalty_ready")
        cmp_cleared, cmp_ready = sem("compressed_cleared"), sem("compressed_probs_ready")
        idx_used = sem("indexer_product_used")
        hg_arg, hg_exp, hg_w = sem("level_argument"), sem("level_decay"), sem("level_operands")
        hg_scores, hg_masked, hg_pv = sem("level_scores"), sem("level_masked"), sem("level_pv")

        def pass_sems(name, ring_too):
            d = {k: sem(f"{name}_{k}") for k in ("slots", "z_ready", "z_saved", "gu", "sg", "hid", "y_ready", "y_added")}
            if ring_too:
                d["w_in"] = [sem(f"{name}_weights_in{i}") for i in range(RING)]
            return d
        rounds = {name: [pass_sems(name, False), pass_sems(name + "_rest", True)] for name in ("moe1", "moe2")}
        chosen_ready, counted = sem("experts_chosen"), sem("experts_counted")

        chunks = []
        freed = {}
        landed = [0] * RING
        ready_at = {}

        def chunk(src, kt=KT, w=COLS):
            c = len(chunks)
            pieces = src if isinstance(src, list) else [(0, P, src)]
            chunks.append((pieces, kt, w))
            landed[c % RING] += 16 * len(pieces)
            ready_at[c] = landed[c % RING]
            return c

        def wview(c, kt, w):
            return ring[:, c % RING, 0:kt * w].rearrange("p (a n) -> p a n", a=kt)

        def kxn(ap):
            return ap.rearrange("(a p) n -> p a n", p=P)

        units = []
        adds = []

        def unit(stage, kind, args, dest, func=ACT.Copy, scale=1.0):
            units.append((stage, kind, args, dest, func, scale))
            if kind in ("T", "tok", "dup") and args[1] is not None:
                freed[args[1]] = (proj_ready, len(units))
            if kind == "hidden":
                for c in args[2]:
                    freed[c] = (proj_ready, len(units))

        def span(stage):
            n = [i for i, u in enumerate(units) if u[0] == stage]
            return n[0], n[-1] + 1

        def add_span(stage):
            n = [i for i, u in enumerate(adds) if u[0] == stage]
            return n[0], n[-1] + 1

        def transposes(stage, src, dst, blocks=KT):
            for j in range(0, blocks, 2):
                unit(stage, "tr", (src, j), dst[:, j:j + 2, :])

        def project(stage, kind, x, src, dest, c0, n, func=ACT.Copy, scale=1.0, dstT=True):
            for j in range(n):
                c = chunk(kxn(src)[:, :, c0 + j * COLS:c0 + (j + 1) * COLS])
                d = dest[:, 2 * j:2 * j + 2, :] if kind == "T" else dest[:, :, j * COLS:(j + 1) * COLS]
                unit(stage, kind, (x, c, KT, COLS, 0, COLS), d, func, scale)

        def residual(stage, src, kt=KT):
            for j in range(D // COLS):
                c = chunk(kxn(src)[:, :, j * COLS:(j + 1) * COLS], kt)
                adds.append((stage, c, kt, j))
                freed[c] = (res_ready, len(adds))

        phases = {}
        steps_before = [0]

        def experts(name, steps):
            phases[name] = (len(chunks), steps, steps_before[0])
            for s in range(steps):
                g = steps_before[0] + s
                for part in range(3):
                    c = len(chunks)
                    chunks.append((None, 0, 0))
                    landed[c % RING] += 16
                    ready_at[c] = landed[c % RING]
                    freed[c] = (gu_ready, 2 * g + 2) if part < 2 else (y_ready, 4 * g + 4)
            steps_before[0] += steps

        def routed(name, n_exp, per):
            q = rounds[name][0]
            phases[name] = (len(chunks), per, n_exp)
            for e in range(n_exp):
                for s in range(per):
                    for part in range(3):
                        c = len(chunks)
                        chunks.append((None, 0, 0))
                        landed[c % RING] += 16
                        ready_at[c] = landed[c % RING]
                        freed[c] = (q["gu"], e * per + s + 1) if part < 2 else (q["y_ready"], e * (per + 2) + s + 1)

        transposes("mem1 transposed", mem_tok, memT)
        project("mem1 keys", "T", memT, I["mem_wk"][0], mkT, 0, 4)
        project("mem1 values", "tok", memT, I["mem_wv"][0], mv, 0, 4)
        for a in range(2):
            unit("bias rows", "row", (a,), rowbuf[:, a, :])
        transposes("ln0 transposed", h, hT)
        w = I["w_in"][0]
        project("mix1", "T", hT, w, hfT, 2052, 2)
        unit("mix1", "tok", (hT, None, KT, FOX_H, 0, FOX_H), ffx)
        project("mix1", "T", hT, w, fqT, 0, 1, scale=0.125)
        project("mix1", "T", hT, w, fkT, 256, 1)
        project("mix1", "tok", hT, w, fv, 512, 1)
        project("mix1", "T", hT, w, dqT, 772, 1, scale=32.0 ** -0.5)
        project("mix1", "T", hT, w, dkT, 1028, 1)
        project("mix1", "tok", hT, w, dv, 1284, 1)
        project("mix1", "tok", hT, w, hi, 2564, 2)
        project("mix1", "T", hT, w, hqT, 1540, 2, func=ACT.Silu)
        project("mix1", "T", hT, w, hgT, 3076, 2, func=ACT.Silu)
        unit("forget sums", "cum", (nlogf, FOX_H), cumq, ACT.Copy, -1.0)
        unit("mean squares", "sumsq", (halves, dsq, 1.0 / 64), drs)
        for a in range(2):
            unit("mean squares", "sumsq", (ones[:, 0:P], sqT[:, 2 * a:2 * a + 2, :], 1.0 / P),
                 decay[:, 0, 2 * a:2 * a + 2, :])
        residual("out1", I["w_out"][0])
        transposes("ln1 transposed", h, hT)
        project("mem1 queries", "T", hT, I["mem_wq"][0], mqT, 0, 4, scale=1.0 / 16)
        residual("mem1 out", I["mem_wo"][0])
        transposes("ln2 transposed", h, hT)
        route_in = route[:, 0:TT * E1].rearrange("p (a b) -> p a b", a=TT)
        unit("router1", "tok", (hT, None, KT, E1, 0, E1), route_in, ACT.Sigmoid)
        unit("count1", "cum", (route_gate[:, :, 0:E1], E1), route_count)
        routed("moe1", E1, FF1 // COLS)
        transposes("mem2 transposed", mem_tok, memT)
        for i in range(2):
            project(f"xa{i} keys", "T", memT, I["xa_w_k_2"][i], mkT, 0, 2)
            project(f"xa{i} values", "tok", memT, I["xa_w_v_2"][i], mv, 0, 2)
            if i == 0:
                for j in range(16):
                    unit("bias tiles 0", "flip", (j,), biasT[:, j, :])
            transposes(f"ln{3 * i + 3} transposed", h, hT)
            if i == 0:
                w = I["ev_w_in_2"][0]
                c = chunk(kxn(w)[:, :, 512:640], w=128)
                unit("mix2", "tok", (hT, c, KT, 128, 0, 128), ckv)
                c = chunk(kxn(w)[:, :, 1152:1224], w=72)
                unit("mix2", "dup", (hT, c, KT, 72, 0, 1), kiT)
                unit("mix2", "tok", (hT, c, KT, 72, 64, 8), wi, ACT.Copy, 8.0 ** -0.5)
                project("mix2", "T", hT, w, qiT, 640, 2)
                for j in range(8):
                    unit("indexer", "idx", (j,), idx_act[:, j % 2], ACT.Relu, 0.125)
                project("mix2b", "T", hT, w, qaT, 0, 2)
                project("mix2b", "T", hT, w, qbT, 1224, 2, scale=0.125)
                c = chunk(kxn(w)[:, :, 1736:1992])
                unit("mix2b", "dup", (hT, c, KT, 256, 0, 2), kbT)
                unit("mix2b", "tok", (hT, c, KT, 256, 128, 128), vb)
                for j in (0, 4, 1, 5):
                    unit("latent queries", "uk", (j,), qlatT[:, j:j + 3:2, :], ACT.Copy, 0.125)
                unit("latent keys", "ctr", (), cT)
                for j in range(4):
                    unit("latent out", "uv", (j,), yT[:, j, :])
                residual("out2", I["ev_w_out_2"][0])
            else:
                w = I["od_w_in_2"][0]
                project("mix3", "T", hT, w, kvcT, 1024, 1)
                project("mix3", "T", hT, w, qcT, 0, 4, scale=0.125)
                for c0, kd, vd in ((1280, ksT, vs), (1536, kwT, vw)):
                    c = chunk(kxn(w)[:, :, c0:c0 + 256])
                    unit("mix3", "dup", (hT, c, KT, 256, 0, 2), kd)
                    unit("mix3", "tok", (hT, c, KT, 256, 128, 128), vd)
                c = chunk(kxn(w)[:, :, 1792:1840], w=48)
                unit("mix3", "tok", (hT, c, KT, 48, 0, 48), g3, ACT.Sigmoid)
                unit("compressed bias", "cb", (), bcmp)
                for br, name in enumerate(("od_w1_k_2", "od_w1_v_2")):
                    v = I[name][0].rearrange("(j d) c -> d j c", d=64)
                    cs = [chunk([(0, 64, v[:, 16 * a:16 * a + 16, :]), (64, 64, v[:, 16 * a:16 * a + 16, :])], 16, 128)
                          for a in range(2)]
                    for g in range(2):
                        unit("compress hidden", "hidden", (br, g, cs), geluT[:, br, g, 0:N_CMP])
                unit("compress out", "kc", (), kcT)
                unit("compress out", "vc", (), vc4)
                for par in range(2):
                    adds.append(("compressed logits", None, par, None))
                for par in range(2):
                    unit("compressed probs", "pctr", (par,), pcT[:, par])
                residual("out3", I["od_w_out_2"][0])
            transposes(f"ln{3 * i + 4} transposed", h, hT)
            project(f"xa{i} queries", "T", hT, I["xa_w_q_2"][i], mqT, 0, 2, scale=128.0 ** -0.5)
            residual(f"xa{i} out", I["xa_w_o_2"][i], 4)
            transposes(f"ln{3 * i + 5} transposed", h, hT)
            if i == 0:
                experts("dense", FF_DENSE // COLS)
                for j in range(8, 16):
                    unit("bias tiles 1", "flip", (j,), biasT[:, j, :])
            else:
                unit("router2", "tok", (hT, None, KT, E2, 0, E2), route[:, 0:TT * E2].rearrange(
                    "p (a b) -> p a b", a=TT))
                unit("count2", "cum", (route_gate[:, :, 0:E2], E2), route_count[:, :, 0:E2])
                routed("moe2", E2, FF2 // COLS)

        maps, groups, map_span = [], [], {}

        def attention(stage, items):
            m0, g0 = len(maps), len(groups)
            for members, dest in items:
                for n, mp in enumerate(members):
                    base = mp.setdefault("base", 0)
                    same = [i for i, o in enumerate(members) if o.get("base", 0) == base]
                    mp.update(group=len(groups), new=(n == 0), first=(n == same[0]), last=(n == same[-1]),
                              end=(n == len(members) - 1))
                    maps.append(mp)
                groups.append((len(maps) - 1, dest))
            map_span[stage] = (m0, len(maps), g0, len(groups))

        def half(j):
            return slice(64 * (j % 2), 64 * (j % 2) + 64)

        fox = [([dict(qk=[(fqT[half(j), j // 2, :], fkT[half(j), j // 2, :])], mask=causal, fox=j,
                      v=fv[:, :, 64 * j:64 * j + 64], base=64 * (j % 2)) for j in (2 * a, 2 * a + 1)],
                yT[:, a, :]) for a in range(2)]

        def diff_map(j, c):
            rows = slice(32 * (2 * (j % 2) + c), 32 * (2 * (j % 2) + c) + 32)
            return dict(qk=[(dqT[rows, j // 2, :], dkT[rows, j // 2, :])], mask=chunkmask,
                        coef=neglam if c else None, v=dv[:, :, 64 * j:64 * j + 64], base=64 * (j % 2))
        diff = [([diff_map(j, c) for j in (2 * a, 2 * a + 1) for c in range(2)], yT[:, 2 + a, :]) for a in range(2)]
        attention("mix1", fox + diff)
        attention("mem1", [([dict(qk=[(mqT[:, 2 * j + a, :], mkT[:, 2 * j + a, :]) for a in range(2)],
                                  v=mv[:, :, 256 * j:256 * j + 256])], yT[:, 2 * j:2 * j + 2, :]) for j in range(4)])

        def bias_of(j):
            v = biasT[:, j, P:P + T]
            return bass.AP(tensor=v.tensor, offset=v.offset, ap=[v.ap[0], [-P, TT], [1, T]])
        lat = [([dict(qk=[(qlatT[:, j, :], cT)], mask=bias_of(j), extra=work, v=ckv[:, :, 0:P])],
                olatT[:, j, :]) for j in range(8)]
        win = [([dict(qk=[(qbT[half(j), j // 2, :], kbT[half(j), j // 4, :])], mask=bias_of(8 + j), sink=j,
                      v=vb[:, :, 64 * (j // 4):64 * (j // 4) + 64], base=64 * (j % 2)) for j in (2 * a, 2 * a + 1)],
                yT[:, 4 + a, :]) for a in range(4)]
        attention("mix2", win + lat)
        cross = [([dict(qk=[(mqT[:, j, :], mkT[:, j, :])], v=mv[:, :, P * j:P * j + P])], yT[:, j, :])
                 for j in range(4)]
        attention("xa0", cross)

        def nsa_maps(j):
            g = j // 8
            out = []
            for branch, (k, v) in enumerate(((ksT, vs), (kwT, vw))):
                out.append(dict(qk=[(qcT[half(j), j // 2, :], k[half(j), g, :])], mask=bias_of(j),
                                coef=g3[:, :, 3 * j + 1 + branch], v=v[:, :, 64 * g:64 * g + 64], base=64 * (j % 2),
                                compressed=j if branch == 0 else None))
            return out
        attention("mix3", [(nsa_maps(2 * a) + nsa_maps(2 * a + 1), yT[:, a, :]) for a in range(8)])
        attention("xa1", [([dict(mp) for mp in members], dest) for members, dest in cross])

        def saved(stage):
            return span(stage)[1]

        def maps_end(stage):
            return map_span[stage][1]

        def groups_end(stage):
            return map_span[stage][3]

        N_PARAMS = len(SMALL_LOADS) + 4
        CREDIT = 4
        n_steps = steps_before[0]
        block = ctx.enter_context(nc.Block())

        @block.sync
        def _(sp):
            sp.dma_start(h[:], I["x"][0].rearrange("(t p) d -> p t d", p=P)).then_inc(x_in, 16)
            sp.dma_start(mem_tok, I["mem"][0].rearrange("(t p) d -> p t d", p=P)).then_inc(mem_in, 16)

            def load(c):
                pieces, kt, w = chunks[c]
                if c >= RING:
                    sp.wait_ge(*freed[c - RING])
                for row, n, src in pieces:
                    sp.dma_start(ring[row:row + n, c % RING, 0:kt * w].rearrange("p (a n) -> p a n", a=kt),
                                 src).then_inc(w_in[c % RING], 16)

            def expert_views(wg, wu, wd):
                return (wg.rearrange("e (a p) (c n) -> e c p a n", p=P, n=COLS),
                        wu.rearrange("e (a p) (c n) -> e c p a n", p=P, n=COLS),
                        wd.rearrange("e (c f p) n -> e c p f n", p=P, f=2))

            def load_part(w, e, c, part, slot, landed_):
                kt = KT if part < 2 else 2
                sp.dma_start(ring[:, slot, :].rearrange("p (a n) -> p a n", a=kt),
                             w[bass.ds(e, 1), bass.ds(c, 1)].rearrange("e c p a n -> p (e c a) n"))\
                    .then_inc(landed_[slot], 16)

            def load_dense(first, steps, before, views):
                def step(c, par, g, peeled):
                    for part, w in enumerate(views):
                        if peeled:
                            sp.wait_ge(*freed[first + 3 * par + part - RING])
                        elif part < 2:
                            sp.wait_ge(gu_ready, g * 2 - 2)
                        else:
                            sp.wait_ge(y_ready, g * 4 - 4)
                        load_part(w, 0, c, part, (first + 3 * par + part) % RING, w_in)

                for s in range(2):
                    step(s, s, before + s, True)
                with nc.sync.Fori(1, steps // 2) as b:
                    for s in range(2):
                        step(b * 2 + s, s, b * 2 + (before + s), False)
                if steps % 2:
                    step(steps - 1, 0, before + steps - 1, False)

            def load_routed(first, per, n_exp, views, q, landed_, rest):
                def step(e, s, par, where):
                    for part, w in enumerate(views):
                        if where == "start":
                            if not rest:
                                sp.wait_ge(*freed[first + 3 * par + part - RING])
                        elif part < 2:
                            sp.wait_ge(q["gu"], e * per + s - 1)
                        elif where == "turn":
                            sp.wait_ge(q["y_ready"], e * (per + 2) + s - 3)
                        else:
                            sp.wait_ge(q["y_ready"], e * (per + 2) + s - 1)
                        load_part(w, e, s, part, (first + 3 * par + part) % RING, landed_)

                def expert(e, where):
                    for s in range(2):
                        step(e, s, s, where)
                    if per > 2:
                        with nc.sync.Fori(1, per // 2) as b:
                            for s in range(2):
                                step(e, b * 2 + s, s, "in")
                expert(0, "start")
                with nc.sync.Fori(1, n_exp) as e:
                    expert(e, "turn")

            order = [("moe1", ("w1", "w3", "w2"), E1, FF1, True), ("dense", ("ff_w_gate_2", "ff_w_up_2", "ff_w_down_2"), 1,
                     FF_DENSE, False), ("moe2", ("moe_w_gate_2", "moe_w_up_2", "moe_w_down_2"), E2, FF2, True)]
            at = 0
            for name, ws, n_exp, ff, experts_dim in order:
                first, steps, _ = phases[name]
                for c in range(at, first):
                    load(c)
                wg, wu, wd = [I[x][0] if experts_dim else I[x] for x in ws]
                views = expert_views(wg, wu, wd)
                if name == "dense":
                    load_dense(first, steps, phases[name][2], views)
                    at = first + 3 * steps
                    continue
                per, n_exp = steps, phases[name][2]
                q, rest = rounds[name]
                load_routed(first, per, n_exp, views, q, w_in, False)
                at = first + 3 * per * n_exp
                sp.wait_ge(counted, 1 if name == "moe1" else 2)
                full = nc.sync.value_load(crowded[P - 1:P, 0:1] if name == "moe1" else crowded[P - 1:P, 1:2],
                                          min_val=0, max_val=1)
                with nc.sync.If(full > 0):
                    for c in range(at - RING, at):
                        sp.wait_ge(*freed[c])
                    load_routed(first, per, n_exp, views, rest, rest["w_in"], True)
                    sp.wait_ge(rest["y_ready"], n_exp * (per + 2))
            assert at == len(chunks)
            sp.wait_ge(ln_done, 10)
            sp.dma_start(out[0].rearrange("(t p) d -> p t d", p=P), h[:]).then_inc(out_stored, 16)
            sp.wait_ge(out_stored, 16)

        @block.gpsimd
        def _(pool):
            pool.dma_start(cw[:], I["const_wide"]).then_inc(consts_in, 16)
            pool.dma_start(ohot[:].rearrange("p a b -> p (a b)"), I["const_rows"]).then_inc(table_in, 16)
            pool.dma_start(tab[0:BUCKETS, :], I["rel_table_2"]).then_inc(table_in, 16)
            nc.gpsimd.memset(tab[BUCKETS:BUCKETS + 1, :], NEG).then_inc(set_up, 1)

            ln_params = [(I["ln_in_g"], I["ln_in_b"])] + [(I["ln_g"][0, i], I["ln_b"][0, i]) for i in range(3)] + \
                [(I["ln_g_2"][a, i], I["ln_b_2"][a, i]) for a in range(2) for i in range(3)]

            def load_gb(n):
                if n:
                    pool.wait_ge(ln_done, n)
                for k in range(2):
                    pool.dma_start(gb[:, k, :], across(ln_params[n][k])).then_inc(gb_in, 16)

            def across(row):
                return bass.AP(tensor=row.tensor, offset=row.offset, ap=[[0, P]] + list(row.ap))

            load_gb(0)
            small_loads = {
                "wff": (wff, kxn(I["w_in"][0])[:, :, 768:772]), "foxb": (foxb, across(I["fox_fb"][0])),
                "lam0": (lamv[:, 0], across(I["lam_q1"][0])), "lam1": (lamv[:, 1], across(I["lam_k1"][0])),
                "lam2": (lamv[:, 2], across(I["lam_q2"][0])), "lam3": (lamv[:, 3], across(I["lam_k2"][0])),
                "dng": (dng[0:64], I["diff_norm_g"][0].rearrange("(p a) -> p a", a=1)),
                "dng2": (dng[64:128], I["diff_norm_g"][0].rearrange("(p a) -> p a", a=1)),
                "hng": (hng, I["hgrn_norm_g"][0].rearrange("(p a) -> p a", a=1)),
                "rw1": (rw1, kxn(I["router_w"])), "rb1": (rb1, across(I["router_b"])),
                "rw2": (rw2, kxn(I["moe_w_router_2"][0])), "ckvg": (ckvg, across(I["ev_ckv_gain_2"][0])),
                "sinks": (sinks, across(I["ev_sinks_2"][0])),
                "wuk": (wuk[:], I["ev_w_uk_2"][0].rearrange("(a b) d c -> (b d) a c", b=2)),
                "wuv": (wuv[:], I["ev_w_uv_2"][0].rearrange("h c d -> c h d")),
                "w2k": (w2kv[:, 0], I["od_w2_k_2"][0]), "w2v": (w2kv[:, 1], I["od_w2_v_2"][0]),
            }
            assert list(small_loads) == SMALL_LOADS
            for dst, src in small_loads.values():
                pool.dma_start(dst, src, allow_slow_non_contiguous=True).then_inc(params_in, 16)
            for b in range(2):
                for k, name in enumerate(("od_pe_k_2", "od_pe_v_2")):
                    pool.dma_start(peT[64 * b:64 * b + 64, k], I[name][0].rearrange("j d -> d j"),
                                   allow_slow_non_contiguous=True).then_inc(params_in, 16)

            pool.wait_ge(proj_saved, saved("bias rows"))
            pool.dma_start(rows_dram, rowbuf).then_inc(rows_out, 16)

            def hankel_rows(heads, variant):
                src = bass.AP(tensor=rows_dram.tensor, offset=heads[0] * 2 * ROW_W + variant * ROW_W,
                              ap=[[1, P], [2 * ROW_W, len(heads)], [1, BIAS_W]])
                pool.dma_start(hankel[:, heads[0]:heads[0] + len(heads), :], src).then_inc(rows_back, 16)

            load_gb(1)
            for lv, b in enumerate(LEVELS):
                pool.wait_ge(hg_exp, lv + 1)
                if lv >= 2:
                    pool.wait_ge(hg_scores, 2 * (lv - 1) - 1)
                for side, src in enumerate((hkT, hqT)):
                    def view(x):
                        return x.rearrange("p h t -> p (h t)").rearrange("p (n a b) -> p n a b", a=2, b=b)[:, :, side, :]
                    ins = nc.gpsimd.tensor_tensor(view(Wlv[:, lv % 2]), view(decay[:, lv % 2]), view(src), ALU.mult)
                ins.then_inc(hg_w, 1)
            load_gb(2)
            load_gb(3)
            pool.dma_start(mem_tok, I["mem_2"][0].rearrange("(t p) d -> p t d", p=P)).then_inc(mem2_in, 16)
            pool.wait_ge(rows_out, 16)
            hankel_rows(list(range(8)), 0)
            hankel_rows(list(range(8, 16)), 1)
            for n in range(4, 7):
                load_gb(n)
            hankel_rows(list(range(8, 16)), 0)
            for n in range(7, 10):
                load_gb(n)

        def per_step_pair(fori, steps, head, tail):
            head(0, 0)
            with fori(0, (steps - 1) // 2) as i:
                head(i, 1)
                tail(i, 0)
                head(i + 1, 0)
                tail(i, 1)
            n = (steps - 1) // 2
            if steps % 2 == 0:
                head(n, 1)
            tail(n, 0)
            if steps % 2 == 0:
                tail(n, 1)

        @block.tensor
        def _(pe):
            mm = nc.tensor.matmul

            def weights(c):
                pe.wait_ge(w_in[c % RING], ready_at[c])
                _, kt, w = chunks[c]
                return wview(c, kt, w)

            def emit(u):
                stage, kind, args, dest, _, _ = units[u]
                bank = B[2 + u % 2]
                if u >= 2:
                    pe.wait_ge(proj_saved, u - 1)
                if kind == "T":
                    x, c, kt, w, _, _ = args
                    wt = weights(c)
                    for j in range(2):
                        for k in range(kt):
                            last = mm(bank[:, T * j:T * j + T], wt[:, k, P * j:P * j + P], x[:, k, :],
                                      start=(k == 0), stop=(k == kt - 1))
                elif kind == "tok":
                    x, c, kt, w, c0, n = args
                    wt = weights(c) if c is not None else {"mix1": wff, "router1": rw1, "router2": rw2}[stage]
                    for t in range(TT):
                        for k in range(kt):
                            last = mm(bank[:, n * t:n * t + n], x[:, k, P * t:P * t + P], wt[:, k, c0:c0 + n],
                                      start=(k == 0), stop=(k == kt - 1))
                elif kind == "dup":
                    x, c, kt, w, c0, groups_ = args
                    wt = weights(c)
                    for g in range(groups_):
                        for b in range(2):
                            for k in range(kt):
                                last = mm(bank[64 * b:64 * b + 64, T * g:T * g + T], wt[:, k, 64 * g:64 * g + 64],
                                          x[:, k, :], start=(k == 0), stop=(k == kt - 1))
                elif kind == "tr":
                    src, j0 = args
                    for j in range(2):
                        for t in range(TT):
                            last = nc.tensor.transpose(bank[:, T * j + P * t:T * j + P * t + P],
                                                       src[:, t, P * (j0 + j):P * (j0 + j) + P], eye)
                elif kind == "ctr":
                    for t in range(TT):
                        last = nc.tensor.transpose(bank[:, P * t:P * t + P], ckv[:, t, :], eye)
                elif kind == "pctr":
                    for a in range(2):
                        for t in range(TT):
                            blk = Pc[:, args[0], t, 4 * a:4 * a + 4, :].rearrange("p a b -> p (a b)")
                            last = nc.tensor.transpose(bank[:, T * a + P * t:T * a + P * t + P], blk, eye)
                elif kind == "row":
                    last = mm(bank[0:16, :], tab[:], ohot[:, args[0], :], start=True, stop=True)
                elif kind == "flip":
                    last = mm(bank[:, 0:BIAS_W], flip, hankel[:, args[0], :], start=True, stop=True)
                elif kind == "cum":
                    for t in range(TT):
                        for st in range(TT):
                            src, n = args
                            last = mm(bank[:, n * t:n * t + n], tri[:, st, P * t:P * t + P], src[:, st, :],
                                      start=(st == 0), stop=(st == TT - 1))
                elif kind == "sumsq":
                    lhs, sq, _ = args
                    last = mm(bank[:, :], lhs, sq.rearrange("p a b -> p (a b)"), start=True, stop=True)
                elif kind == "uk":
                    for a in range(2):
                        j = args[0] + 2 * a
                        last = mm(bank[:, T * a:T * a + T], wuk[half(j), j // 2, :], qaT[half(j), j // 2, :],
                                  start=True, stop=True)
                elif kind == "idx":
                    j = args[0]
                    for t in range(TT):
                        last = mm(bank[:, T * t:T * t + T], qiT[half(j), j // 2, P * t:P * t + P], kiT[half(j), :],
                                  start=True, stop=True)
                elif kind == "uv":
                    for a in range(2):
                        last = mm(bank[64 * a:64 * a + 64, 0:T], wuv[:, 2 * args[0] + a, :],
                                  olatT[:, 2 * args[0] + a, :], start=True, stop=True)
                elif kind == "cb":
                    for t in range(TT):
                        for n in range(N_CMP):
                            o = 255 + P * t - 16 * n - 31
                            last = mm(bank[:, 16 * (N_CMP * t + n):16 * (N_CMP * t + n) + 16], ohot[:, 2, o:o + P],
                                      tab[:], start=True, stop=True)
                elif kind == "hidden":
                    br, g, cs = args
                    rows = slice(64 * g, 64 * g + 64)
                    for j in range(32):
                        wt = weights(cs[j // 16]) if j % 16 == 0 else wt
                        last = mm(bank[:, 0:N_CMP], wt[rows, j % 16, :], kvcT[rows, br, j:j + 16 * (N_CMP - 1) + 1:16],
                                  start=(j == 0), stop=(j == 31))
                    for j in range(32):
                        wt = wview(cs[j // 16], 16, 128)
                        last = mm(bank[:, 16:17], wt[rows, j % 16, :], peT[rows, br, j:j + 1],
                                  start=(j == 0), stop=(j == 31))
                elif kind == "kc":
                    for g in range(2):
                        for b in range(2):
                            last = mm(bank[64 * b:64 * b + 64, 32 * g:32 * g + 32], w2kv[:, 0, :], geluT[:, 0, g, :],
                                      start=True, stop=True)
                elif kind == "vc":
                    for g in range(2):
                        for b in range(4):
                            last = mm(bank[32 * b:32 * b + 32, 64 * g:64 * g + 64], geluT[:, 1, g, :], w2kv[:, 1, :],
                                      start=True, stop=True)
                last.then_inc(proj_ready, 1)

            def run(stage):
                for u in range(*span(stage)):
                    emit(u)

            def add(stage, kt=KT):
                for a in range(*add_span(stage)):
                    _, c, kt, j = adds[a]
                    bank = F[a % 4]
                    if a >= 4:
                        pe.wait_ge(res_added, a - 3)
                    wt = weights(c)
                    for t in range(TT):
                        for k in range(kt):
                            last = mm(bank[:, COLS * t:COLS * t + COLS], yT[:, k, P * t:P * t + P], wt[:, k, :],
                                      start=(k == 0), stop=(k == kt - 1))
                    last.then_inc(res_ready, 1)

            def logits(m):
                mp, bank = maps[m], F[m % 2]
                if m >= 2:
                    pe.wait_ge(scored, m - 1)
                for t in range(TT):
                    n = len(mp["qk"]) + (TT if "fox" in mp else 0)
                    for i, (q, k) in enumerate(mp["qk"]):
                        last = mm(bank[:, T * t:T * t + T], q[:, P * t:P * t + P], k, start=(i == 0), stop=(i == n - 1))
                    if "fox" in mp:
                        for st in range(TT):
                            g = nlogf[:, st, mp["fox"]:mp["fox"] + 1].broadcast_to([P, P])
                            last = mm(bank[:, T * t:T * t + T], g, tri[:, st, :], start=False, stop=(st == TT - 1))
                last.then_inc(logits_ready, 1)

            def transpose_probs(m):
                pe.wait_ge(probs_ready, m + 1)
                if m >= 2:
                    pe.wait_ge(pt_saved, m - 1)
                for k in range(TT):
                    for t in range(TT):
                        last = nc.tensor.transpose(F[2 + m % 2][:, T * k + P * t:T * k + P * t + P],
                                                   S[:, m % NS, t, P * k:P * k + P], eye)
                last.then_inc(pt_ready, 1)

            def values(m):
                mp = maps[m]
                g = mp["group"]
                bank = B[g % 2]
                if mp["new"] and g >= 2:
                    pe.wait_ge(o_saved, g - 1)
                base, width = mp["base"], mp["v"].shape[2]
                first = mp["first"]
                if mp.get("compressed") is not None:
                    j = mp["compressed"]
                    rows = slice(32 * (j // 2 % 4), 32 * (j // 2 % 4) + N_CMP)
                    mm(bank[base:base + 64, 0:T], vc4[rows, j // 8, :], pcT[rows, j % 2, j // 8, :], start=True,
                       stop=False)
                    first = False
                pe.wait_ge(pt_saved, m + 1)
                for piece in range(0, width, P):
                    w = min(P, width - piece)
                    for k in range(TT):
                        last = mm(bank[base:base + w, 2 * piece:2 * piece + T], mp["v"][:, k, piece:piece + w],
                                  PT[:, m % 2, k, :], start=(first and k == 0), stop=(mp["last"] and k == TT - 1))
                last.then_inc(pv_done, 1)

            def attend(stage):
                m0, m1, _, _ = map_span[stage]
                for i in range(m0, m1 + 3):
                    if i < m1:
                        logits(i)
                    if m0 <= i - 2 < m1:
                        transpose_probs(i - 2)
                    if m0 <= i - 3:
                        values(i - 3)
                pe.wait_ge(o_saved, groups_end(stage))

            def hgrn():
                pend = []

                def level_values():
                    j, lv, hp = pend.pop(0)
                    pe.wait_ge(hg_masked, j + 1)
                    for n in range(4):
                        head = n if lv == 0 else 2 * hp + n // 2
                        i = 1 if lv == 0 else n % 2
                        s = 0 if lv == 0 else i
                        last = mm(B[head // 2][:, T * (head % 2) + P * i:T * (head % 2) + P * i + P],
                                  hi[:, s, P * head:P * head + P], SM[:, j % 3, P * n:P * n + P],
                                  start=(lv == 0 and n % 2 == 0), stop=(lv == len(LEVELS)), skip_group_check=True)
                    last.then_inc(hg_pv, 1)

                j = 0
                for lv in range(len(LEVELS) + 1):
                    if lv < len(LEVELS):
                        pe.wait_ge(hg_w, lv + 1)
                    key = Wlv[:, lv % 2] if lv < len(LEVELS) else hkT
                    query = Wlv[:, lv % 2] if lv < len(LEVELS) else hqT
                    for hp in range(1 if lv == 0 else 2):
                        if j >= 4:
                            pe.wait_ge(hg_masked, j - 3)
                        for n in range(4):
                            if lv == 0:
                                a, b = key[:, n, 0:P], query[:, n, P:T]
                            else:
                                head, i = 2 * hp + n // 2, n % 2
                                a, b = key[:, head, P * i:P * i + P], query[:, head, P * i:P * i + P]
                            last = mm(F[j % 4][:, P * n:P * n + P], a, b, start=True, stop=True)
                        last.then_inc(hg_scores, 1)
                        pend.append((j, lv, hp))
                        if len(pend) > 1:
                            level_values()
                        j += 1
                level_values()

            def expert_steps(name):
                first, steps, before = phases[name]

                def landed_(i, par, part):
                    c = first + 3 * par + part
                    pe.wait_ge(w_in[c % RING], i * 16 + ready_at[c])
                    return wview(c, KT if part < 2 else 2, COLS if part < 2 else D)

                def gate_up(i, par):
                    for f in range(2):
                        n = 2 * (before + par) + f
                        pe.wait_ge(hid_ready, i * 4 + (n + 1))
                        for part in range(2):
                            wt = landed_(i, par, part)
                            for k in range(KT):
                                last = mm(F[n % 4][:, T * part:T * part + T], wt[:, k, P * f:P * f + P], hT[:, k, :],
                                          start=(k == 0), stop=(k == KT - 1))
                        last.then_inc(gu_ready, 1)

                def down(i, par):
                    s = before + par
                    pe.wait_ge(hid_ready, i * 4 + (2 * s + 2 + CREDIT))
                    wt = landed_(i, par, 2)
                    for j in range(4):
                        t, c = j // 2, j % 2
                        pe.wait_ge(y_added, i * 8 + (4 * s + j + 1))
                        for f in range(2):
                            last = mm(B[j][:, :], hid[:, (2 * s + f) % 4, P * t:P * t + P],
                                      wt[:, f, 512 * c:512 * c + 512], start=(f == 0), stop=(f == 1))
                        last.then_inc(y_ready, 1)

                per_step_pair(nc.tensor.Fori, steps, gate_up, down)
                pe.wait_ge(y_added, 4 * (before + steps) + CREDIT)

            def routed_round(name, q, rest):
                first, per, n_exp = phases[name]
                zs, ys = per + 4, per + 2

                def small_bank(z, odd):
                    if not isinstance(z, int) or z >= 2:
                        pe.wait_ge(q["z_saved"], z - 1)
                    return F[2 + odd]

                def landed_(e, s, par, part, b=None):
                    c = first + 3 * par + part
                    use = e * (per // 2) + (b if b is not None else s // 2)
                    if rest:
                        pe.wait_ge(q["w_in"][c % RING], use * 16 + 16)
                    else:
                        pe.wait_ge(w_in[c % RING], use * 16 + ready_at[c])
                    return wview(c, KT if part < 2 else 2, COLS if part < 2 else D)

                def gather(e1, z, slots):
                    pe.wait_ge(q["slots"], slots)
                    for a in range(2):
                        bank = small_bank(z + a, a)
                        for k in range(4):
                            for t in range(TT):
                                last = mm(bank[:, SLOTS * k:SLOTS * k + SLOTS], h[:, t, P * (4 * a + k):P * (4 * a + k) + P],
                                          pick[:, t, :], start=(t == 0), stop=(t == TT - 1))
                        last.then_inc(q["z_ready"], 1)

                def gate_up(e, s, par, b=None, between=None):
                    g = e * per + s
                    pe.wait_ge(q["hid"], g + 1)
                    for part in range(2):
                        wt = landed_(e, s, par, part, b)
                        for k in range(KT):
                            last = mm(F[par][:, COLS * part:COLS * part + COLS], xgT[:, k, :], wt[:, k, :],
                                      start=(k == 0), stop=(k == KT - 1))
                        if part == 0 and between is not None:
                            between()
                    last.then_inc(q["gu"], 1)

                def turn(e, s, par):
                    bank = small_bank(e * zs + s + 2, par)
                    pe.wait_ge(q["hid"], e * per + s + 3)
                    for f in range(2):
                        last = nc.tensor.transpose(bank[:, SLOTS * f:SLOTS * f + SLOTS],
                                                   hidden_tok[:, par, P * f:P * f + P], eye)
                    last.then_inc(q["z_ready"], 1)

                def down(e, s, par, b=None):
                    y = e * ys + s
                    wt = landed_(e, s, par, 2, b)
                    pe.wait_ge(q["z_saved"], e * zs + s + 3)
                    pe.wait_ge(q["y_added"], y + 1)
                    for c in range(2):
                        for f in range(2):
                            last = mm(B[2 * par + c][:, :], hidden_T[:, par, f, :], wt[:, f, 512 * c:512 * c + 512],
                                      start=(f == 0), stop=(f == 1))
                    last.then_inc(q["y_ready"], 1)

                def expert(e):
                    pe.wait_ge(q["z_saved"], e * zs + 2)
                    gate_up(e, 0, 0)
                    if per > 2:
                        with nc.tensor.Fori(0, per // 2 - 1) as b:
                            gate_up(e, b * 2 + 1, 1, b, between=lambda: turn(e, b * 2, 0))
                            down(e, b * 2, 0, b)
                            gate_up(e, b * 2 + 2, 0, b + 1, between=lambda: turn(e, b * 2 + 1, 1))
                            down(e, b * 2 + 1, 1, b)
                    gate_up(e, per - 1, 1, between=lambda: turn(e, per - 2, 0))
                    down(e, per - 2, 0)
                    turn(e, per - 1, 1)
                    pe.wait_ge(q["slots"], e * 2 + 2)
                    for t in range(TT):
                        bank = small_bank(e * zs + per + 2 + t, t)
                        nc.tensor.transpose(bank[:, 0:P], gated[:, t, :], eye).then_inc(q["z_ready"], 1)
                    down(e, per - 1, 1)
                    gather(e + 1, e * zs + per + 4, e * 2 + 3)
                    for t in range(TT):
                        y = e * ys + per + t
                        pe.wait_ge(q["z_saved"], e * zs + per + 4)
                        pe.wait_ge(q["y_added"], y + 1)
                        if t == 0:
                            pe.wait_ge(q["y_added"], y + 2)
                        for c in range(2):
                            last = mm(B[2 * t + c][:, :], gatedT[:, t, :], y_slots[:, 512 * c:512 * c + 512], start=True,
                                      stop=True)
                        last.then_inc(q["y_ready"], 1)

                gather(0, 0, 1)
                with nc.tensor.Fori(0, n_exp) as e:
                    expert(e)
                pe.wait_ge(q["y_added"], n_exp * ys + 2)
                pe.wait_ge(q["z_saved"], n_exp * zs + 2)

            def routed_layer(name, n):
                routed_round(name, rounds[name][0], False)
                full = nc.tensor.value_load(crowded[P - 1:P, n:n + 1], min_val=0, max_val=1)
                with nc.tensor.If(full > 0):
                    routed_round(name, rounds[name][1], True)

            pe.wait_ge(consts_in, 16)
            pe.wait_ge(mem_in, 16)
            run("mem1 transposed")
            pe.wait_ge(proj_saved, saved("mem1 transposed"))
            run("mem1 keys")
            run("mem1 values")
            pe.wait_ge(table_in, 32)
            pe.wait_ge(set_up, 1)
            run("bias rows")
            pe.wait_ge(ln_done, 1)
            run("ln0 transposed")
            pe.wait_ge(proj_saved, saved("ln0 transposed"))
            pe.wait_ge(params_in, 16 * N_PARAMS)
            run("mix1")
            pe.wait_ge(logf_ready, 1)
            run("forget sums")
            pe.wait_ge(proj_saved, saved("forget sums"))
            attend("mix1")
            hgrn()
            pe.wait_ge(squares_ready, 2)
            run("mean squares")
            pe.wait_ge(y_normed, 2)
            add("out1")
            pe.wait_ge(ln_done, 2)
            run("ln1 transposed")
            pe.wait_ge(proj_saved, saved("ln1 transposed"))
            run("mem1 queries")
            pe.wait_ge(proj_saved, saved("mem1 queries"))
            attend("mem1")
            add("mem1 out")
            pe.wait_ge(ln_done, 3)
            run("ln2 transposed")
            pe.wait_ge(proj_saved, saved("ln2 transposed"))
            run("router1")
            pe.wait_ge(chosen_ready, 1)
            run("count1")
            pe.wait_ge(counted, 1)
            routed_layer("moe1", 0)
            pe.wait_ge(mem2_in, 16)
            run("mem2 transposed")
            pe.wait_ge(proj_saved, saved("mem2 transposed"))
            for i in range(2):
                if i == 1:
                    pe.wait_ge(rows_back, 48)
                    run("bias tiles 1")
                run(f"xa{i} keys")
                run(f"xa{i} values")
                pe.wait_ge(ln_done, 3 * i + 4)
                if i == 0:
                    pe.wait_ge(rows_back, 32)
                    run("bias tiles 0")
                run(f"ln{3 * i + 3} transposed")
                pe.wait_ge(proj_saved, saved(f"ln{3 * i + 3} transposed"))
                if i == 0:
                    run("mix2")
                    pe.wait_ge(proj_saved, saved("mix2"))
                    run("indexer")
                    run("mix2b")
                    pe.wait_ge(proj_saved, saved("mix2b"))
                    run("latent queries")
                    pe.wait_ge(latents_ready, 1)
                    run("latent keys")
                    pe.wait_ge(proj_saved, saved("latent keys"))
                    attend("mix2")
                    run("latent out")
                    pe.wait_ge(proj_saved, saved("latent out"))
                    add("out2")
                else:
                    run("mix3")
                    run("compressed bias")
                    pe.wait_ge(proj_saved, saved("mix3"))
                    run("compress hidden")
                    pe.wait_ge(proj_saved, saved("compress hidden"))
                    run("compress out")
                    pe.wait_ge(proj_saved, saved("compress out"))
                    for par in range(2):
                        a = add_span("compressed logits")[0] + par
                        pe.wait_ge(res_added, a - 3)
                        for t in range(TT):
                            for jj in range(8):
                                j = 2 * jj + par
                                o = 256 * t + 32 * jj
                                last = mm(F[a % 4][:, o:o + N_CMP], qcT[half(j), j // 2, P * t:P * t + P],
                                          kcT[half(j), j // 8, 0:N_CMP], start=True, stop=True)
                        last.then_inc(res_ready, 1)
                    pe.wait_ge(cmp_ready, 1)
                    run("compressed probs")
                    pe.wait_ge(proj_saved, saved("compressed probs"))
                    attend("mix3")
                    add("out3")
                pe.wait_ge(ln_done, 3 * i + 5)
                run(f"ln{3 * i + 4} transposed")
                pe.wait_ge(proj_saved, saved(f"ln{3 * i + 4} transposed"))
                run(f"xa{i} queries")
                pe.wait_ge(proj_saved, saved(f"xa{i} queries"))
                attend(f"xa{i}")
                add(f"xa{i} out")
                pe.wait_ge(ln_done, 3 * i + 6)
                run(f"ln{3 * i + 5} transposed")
                pe.wait_ge(proj_saved, saved(f"ln{3 * i + 5} transposed"))
                if i == 1:
                    run("router2")
                    pe.wait_ge(chosen_ready, 2)
                    run("count2")
                    pe.wait_ge(counted, 2)
                    routed_layer("moe2", 1)
                else:
                    expert_steps("dense")

        @block.scalar
        def _(act):
            step = Tally(act, act_step)
            asked = [0]
            ap_ = nc.scalar.activation

            def request():
                asked[0] += 1
                act.wait_ge(to_act, asked[0])

            def answer(ins):
                ins.then_inc(from_act, 1)

            def root():
                request()
                answer(ap_(std, veps, ACT.Sqrt))

            def save(stage):
                for u in range(*span(stage)):
                    _, kind, args, dest, func, scale = units[u]
                    bank = B[2 + u % 2]
                    act.wait_ge(proj_ready, u + 1)
                    if kind in ("T", "tr", "pctr", "uk"):
                        ins = ap_(dest, pair(bank), func, scale=scale)
                    elif kind == "tok":
                        ins = ap_(dest, pair(bank, args[5]), func, scale=scale)
                    elif kind == "dup":
                        ins = ap_(dest, pair(bank) if args[5] == 2 else bank[:, 0:T], func, scale=scale)
                    elif kind in ("ctr", "uv"):
                        ins = ap_(dest, bank[:, 0:T], func)
                    elif kind == "idx":
                        if args[0] >= 2:
                            act.wait_ge(idx_used, args[0] - 1)
                        ins = ap_(dest, pair(bank), func, scale=scale)
                    elif kind == "row":
                        ins = ap_(dest, bank[0:16, :], func)
                    elif kind == "flip":
                        ins = ap_(dest, bank[:, 0:BIAS_W], func)
                    elif kind == "cum":
                        ins = ap_(dest, pair(bank, args[1]), func, scale=scale)
                    elif kind == "sumsq":
                        step.did(ap_(dest, pair(bank), ACT.Ln, bias=pbias[:, 0:1], scale=args[2]))
                        step.wait()
                        ins = ap_(dest, dest, ACT.Exp, scale=-0.5)
                    elif kind == "cb":
                        for par in range(2):
                            for t in range(TT):
                                src = bank[:, 240 * t:240 * t + 240].rearrange("p (n j r) -> p r j n", r=2, j=8)[:, par]
                                ins = ap_(bcmp[:, par, t, :, 0:N_CMP], src, func)
                    elif kind == "hidden":
                        pe_col = pbias[:, 1 + 2 * args[0] + args[1]:2 + 2 * args[0] + args[1]]
                        step.did(ap_(pe_col, bank[:, 16:17], ACT.Copy))
                        step.wait()
                        ins = ap_(dest, bank[:, 0:N_CMP], ACT.Gelu_apprx_tanh, bias=pe_col)
                    elif kind == "kc":
                        ins = ap_(dest, bank[:, 0:64].rearrange("p (a b) -> p a b", a=2), func)
                    elif kind == "vc":
                        ins = ap_(dest, bank[:, 0:128].rearrange("p (a b) -> p a b", a=2), func)
                    ins.then_inc(proj_saved, 1)

            def exps(m):
                mp, s = maps[m], m % NS
                act.wait_ge(max_ready, m + 1)
                if "sink" in mp:
                    j = mp["sink"]
                    ap_(esink[:, s], nmx[:, s], ACT.Exp, bias=sinks[:, j:j + 1])
                for t in range(TT):
                    ins = ap_(S[:, s, t], S[:, s, t], ACT.Exp, bias=nmx[:, s, t:t + 1], accum_out=ssum[:, s, t:t + 1])
                ins.then_inc(exp_ready, 1)

            def save_probs(m):
                act.wait_ge(pt_ready, m + 1)
                if m >= 2:
                    act.wait_ge(pv_done, m - 1)
                ap_(PT[:, m % 2], pair(F[2 + m % 2]), ACT.Copy).then_inc(pt_saved, 1)

            def save_group(g):
                last, dest = groups[g]
                act.wait_ge(pv_done, last + 1)
                bank = B[g % 2]
                src = pair(bank) if len(dest.shape) == 3 else bank[:, 0:T]
                ap_(dest, src, ACT.Copy).then_inc(o_saved, 1)

            def attend(stage):
                m0, m1, _, _ = map_span[stage]
                for i in range(m0, m1 + 3):
                    if i < m1:
                        exps(i)
                    if m0 <= i - 2 < m1:
                        save_probs(i - 2)
                    if m0 <= i - 3 and maps[i - 3]["end"]:
                        save_group(maps[i - 3]["group"])

            def expert_steps(name):
                first, steps, before = phases[name]

                def one(i, par):
                    for f in range(2):
                        n = 2 * (before + par) + f
                        act.wait_ge(gu_ready, i * 4 + (n + 1))
                        act.wait_ge(hid_ready, i * 4 + (n - 1 + CREDIT))
                        ap_(sg[:, n % 2], F[n % 4][:, 0:T], ACT.Silu).then_inc(sg_ready, 1)
                with nc.scalar.Fori(0, steps // 2) as i:
                    one(i, 0)
                    one(i, 1)
                if steps % 2:
                    one(steps // 2, 0)

            def routed_round(name, q, rest):
                first, per, n_exp = phases[name]
                zs = per + 4

                def save_small(z, odd, dest, src):
                    act.wait_ge(q["z_ready"], z + 1)
                    ap_(dest, src(F[2 + odd]), ACT.Copy).then_inc(q["z_saved"], 1)

                def gathered(z):
                    for a in range(2):
                        save_small(z + a, a, xgT[:, 4 * a:4 * a + 4, :],
                                   lambda bank: bank[:, :].rearrange("p (k s) -> p k s", k=4))

                def silu(e, s, par):
                    act.wait_ge(q["gu"], e * per + s + 1)
                    ap_(hidden_sg[:, par], F[par][:, 0:COLS], ACT.Silu).then_inc(q["sg"], 1)

                def turned(e, s, par):
                    save_small(e * zs + s + 2, par, hidden_T[:, par], pair_of(SLOTS))

                def pair_of(w):
                    return lambda bank: pair(bank, w)

                gathered(0)
                with nc.scalar.Fori(0, n_exp) as e:
                    silu(e, 0, 0)
                    if per > 2:
                        with nc.scalar.Fori(0, per // 2 - 1) as b:
                            turned(e, b * 2, 0)
                            silu(e, b * 2 + 1, 1)
                            turned(e, b * 2 + 1, 1)
                            silu(e, b * 2 + 2, 0)
                    turned(e, per - 2, 0)
                    silu(e, per - 1, 1)
                    turned(e, per - 1, 1)
                    for t in range(TT):
                        save_small(e * zs + per + 2 + t, t, gatedT[:, t, :], lambda bank: bank[:, 0:P])
                    gathered(e * zs + per + 4)

            def routed_layer(name, n):
                routed_round(name, rounds[name][0], False)
                full = nc.scalar.value_load(crowded[P - 1:P, n:n + 1], min_val=0, max_val=1)
                with nc.scalar.If(full > 0):
                    routed_round(name, rounds[name][1], True)

            root()
            request()
            answer(ap_(lame, lams, ACT.Exp))
            save("mem1 transposed")
            save("mem1 keys")
            save("mem1 values")
            save("bias rows")
            save("ln0 transposed")
            save("mix1")
            request()
            step.did(ap_(ffe, ffa, ACT.Exp, scale=-1.0))
            step.wait()
            answer(ap_(ffe, ffe, ACT.Ln, bias=1.0))
            request()
            step.did(ap_(hkT, bcT, ACT.Exp, scale=-1.0))
            step.wait()
            step.did(ap_(bcT, hkT, ACT.Ln, bias=1.0))
            step.wait()
            answer(ap_(hkT, hfT, ACT.Sigmoid, scale=-1.0))
            save("forget sums")
            act.wait_ge(rows_out, 16)
            attend("mix1")
            for lv in range(len(LEVELS)):
                act.wait_ge(hg_arg, lv + 1)
                ap_(decay[:, lv % 2], decay[:, lv % 2], ACT.Exp).then_inc(hg_exp, 1)
            act.wait_ge(hg_pv, 2 * len(LEVELS) + 1)
            for a in range(2):
                ins = ap_(oT[:, 2 * a:2 * a + 2, :], pair(B[a]), ACT.Copy)
            answer(ins)
            save("mean squares")
            root()
            save("ln1 transposed")
            save("mem1 queries")
            attend("mem1")
            root()
            save("ln2 transposed")
            save("router1")
            save("count1")
            act.wait_ge(counted, 1)
            routed_layer("moe1", 0)
            root()
            save("mem2 transposed")
            for i in range(2):
                if i == 1:
                    root()
                    save("bias tiles 1")
                save(f"xa{i} keys")
                save(f"xa{i} values")
                if i == 0:
                    save("bias tiles 0")
                save(f"ln{3 * i + 3} transposed")
                if i == 0:
                    save("mix2")
                    request()
                    answer(ap_(cstd, css, ACT.Sqrt))
                    save("indexer")
                    save("mix2b")
                    save("latent queries")
                    save("latent keys")
                    attend("mix2")
                    save("latent out")
                else:
                    save("mix3")
                    save("compressed bias")
                    act.wait_ge(cmp_cleared, 1)
                    save("compress hidden")
                    save("compress out")
                    request()
                    pc = Pc.rearrange("p r t j n -> p (r t j) n")[:, :, 0:N_CMP]
                    answer(ap_(pc, pc, ACT.Exp))
                    save("compressed probs")
                    attend("mix3")
                root()
                save(f"ln{3 * i + 4} transposed")
                save(f"xa{i} queries")
                attend(f"xa{i}")
                root()
                save(f"ln{3 * i + 5} transposed")
                if i == 1:
                    save("router2")
                    request()
                    e = route[:, 16:32]
                    answer(ap_(e, e, ACT.Exp))
                    save("count2")
                    act.wait_ge(counted, 2)
                    routed_layer("moe2", 1)
                else:
                    expert_steps("dense")
            root()

        @block.vector
        def _(dve):
            V = nc.vector
            step = Tally(dve, dve_step)
            answered = [0]

            def ask(ins):
                ins.then_inc(to_act, 1)
                answered[0] += 1

            def answer():
                dve.wait_ge(from_act, answered[0])

            def do(ins):
                step.did(ins)
                step.wait()

            norms = [0]

            def layer_norm(src=None):
                src = h if src is None else src
                n = norms[0]
                norms[0] += 1
                for t in range(TT):
                    for a in range(2):
                        ins = V.bn_stats(stats[:, t, a, :], src[:, t, 512 * a:512 * a + 512])
                do(ins)
                for t in range(TT):
                    ins = V.bn_aggr(mvar[:, t, :], stats[:, t])
                do(ins)
                ask(V.tensor_scalar(veps, mvar[:, :, 1], EPS, None, ALU.add))
                answer()
                do(V.reciprocal(rstd, std))
                for t in range(TT):
                    ins = V.tensor_scalar(h[:, t], src[:, t], mvar[:, t, 0:1], rstd[:, t:t + 1], ALU.subtract, ALU.mult)
                do(ins)
                dve.wait_ge(gb_in, 32 * (n + 1))
                for t in range(TT):
                    ins = V.tensor_tensor(h[:, t], h[:, t], gb[:, 0], ALU.mult)
                do(ins)
                for t in range(TT):
                    ins = V.tensor_tensor(h[:, t], h[:, t], gb[:, 1], ALU.add)
                ins.then_inc(ln_done, 1)
                dve.wait_ge(ln_done, n + 1)

            def add(stage, alpha):
                for a in range(*add_span(stage)):
                    j = adds[a][3]
                    hs = h[:, :, COLS * j:COLS * j + COLS]
                    dve.wait_ge(res_ready, a + 1)
                    V.scalar_tensor_tensor(out=hs, in0=hs, scalar=alpha, in1=pair(F[a % 4]), op0=ALU.mult,
                                           op1=ALU.add).then_inc(res_added, 1)
                dve.wait_ge(res_added, add_span(stage)[1])

            def score_map(m):
                mp, s = maps[m], m % NS
                bank = pair(F[m % 2])
                dve.wait_ge(logits_ready, m + 1)
                if m >= NS:
                    dve.wait_ge(pt_ready, m - NS + 1)
                if "fox" in mp:
                    j = mp["fox"]
                    for t in range(TT):
                        ins = V.scalar_tensor_tensor(out=S[:, s, t], in0=bank[:, t], scalar=cumq[:, t, j:j + 1],
                                                     in1=mp["mask"][:, t], op0=ALU.add, op1=ALU.add)
                elif "mask" in mp:
                    ins = V.tensor_tensor(S[:, s], bank, mp["mask"], ALU.add)
                else:
                    ins = V.tensor_copy(S[:, s], bank)
                ins.then_inc(scored, 1)
                dve.wait_ge(scored, m + 1)
                if "extra" in mp:
                    do(V.tensor_tensor(S[:, s], S[:, s], mp["extra"], ALU.add))
                ins = V.tensor_reduce(nmx[:, s], S[:, s], AX.X, ALU.max, negate=True)
                if "sink" in mp:
                    do(ins)
                    j = mp["sink"]
                    ins = V.tensor_scalar(nmx[:, s], nmx[:, s], nsinks[:, j:j + 1], None, ALU.min)
                ins.then_inc(max_ready, 1)

            def normalise(m):
                mp, s = maps[m], m % NS
                dve.wait_ge(exp_ready, m + 1)
                if "sink" in mp:
                    do(V.tensor_tensor(ssum[:, s], ssum[:, s], esink[:, s], ALU.add))
                do(V.reciprocal(rsum[:, s], ssum[:, s]))
                if mp.get("coef") is not None:
                    do(V.tensor_tensor(rsum[:, s], rsum[:, s], mp["coef"], ALU.mult))
                for t in range(TT):
                    ins = V.tensor_scalar(S[:, s, t], S[:, s, t], rsum[:, s, t:t + 1], None, ALU.mult)
                ins.then_inc(probs_ready, 1)

            def attend(stage):
                m0, m1, _, _ = map_span[stage]
                for i in range(m0, m1 + 1):
                    if i < m1:
                        score_map(i)
                    if m0 <= i - 1:
                        normalise(i - 1)

            def chosen(src, groups_, n, k, lower, rank, sel):
                shape = [P, groups_, n, n]
                gt = route[:, 400:400 + groups_ * n * n].rearrange("p (g j i) -> p g j i", j=n, i=n)
                ge = route[:, 600:600 + groups_ * n * n].rearrange("p (g j i) -> p g j i", j=n, i=n)
                low = lower.rearrange("p (j i) -> p j i", j=n)
                other = src.unsqueeze(2).broadcast_to(shape)
                own = src.unsqueeze(3).broadcast_to(shape)
                V.tensor_tensor(gt, other, own, ALU.is_gt)
                do(V.tensor_tensor(ge, other, own, ALU.is_ge))
                for g in range(groups_):
                    ins = V.tensor_tensor(ge[:, g], ge[:, g], low, ALU.mult)
                do(ins)
                do(V.tensor_tensor(gt, gt, ge, ALU.max))
                do(V.tensor_reduce(rank, gt, AX.X, ALU.add))
                do(V.tensor_scalar(sel, rank, k - 0.5, None, ALU.is_lt))

            def place(sel, gates, n_exp, n):
                gate = route_gate[:, :, 0:n_exp]
                V.tensor_copy(gate, sel).then_inc(chosen_ready, 1)
                V.memset(route_slot, -1.0)
                V.memset(route_gate[:, :, n_exp:n_exp + 1], 0.0)
                dve.wait_ge(proj_saved, saved(f"count{n}"))
                count = route_count[:, :, 0:n_exp]
                slot = route_slot[:, :, 0:n_exp]
                top = route[:, 380:381]
                do(V.tensor_reduce(top, count[:, 1], AX.X, ALU.max))
                do(V.tensor_tensor(slot, count, sel, ALU.mult))
                do(V.tensor_scalar(slot, slot, -1.0, None, ALU.add))
                do(V.tensor_copy(gate, gates))
                V.tensor_scalar(crowded[:, n - 1:n], top, CROWD + 0.5, None, ALU.is_gt).then_inc(counted, 1)
                dve.wait_ge(counted, n)

            def route1():
                r_ = Slots(route, TT * E1)
                sc = route[:, 0:32].rearrange("p (a b) -> p a b", a=TT)
                biased, sel, gates, rank = (r_.get(32) for _ in range(4))
                gs, grank, gsel, tot = r_.get(8), r_.get(8), r_.get(8), r_.get(2)
                dve.wait_ge(proj_saved, saved("router1"))
                v3 = lambda x: x.rearrange("p (a b) -> p a b", a=TT)
                v8 = lambda x: x.rearrange("p (g n) -> p g n", n=4)
                do(V.tensor_tensor(v3(biased), sc, rb1.unsqueeze(1).broadcast_to([P, TT, E1]), ALU.add))
                chosen(v8(biased), 8, 4, 2, const("lower4"), v8(rank), v8(sel))
                do(V.tensor_tensor(gates, biased, sel, ALU.mult))
                do(V.tensor_reduce(gs, v8(gates), AX.X, ALU.add))
                g2 = lambda x: x.rearrange("p (a b) -> p a b", a=TT)
                chosen(g2(gs), 2, 4, 1, const("lower4"), g2(grank), g2(gsel))
                do(V.tensor_tensor(v8(sel), v8(sel), gsel.unsqueeze(2).broadcast_to([P, 8, 4]), ALU.mult))
                do(V.tensor_tensor(gates, route[:, 0:32], sel, ALU.mult))
                do(V.tensor_reduce(tot, v3(gates), AX.X, ALU.add))
                do(V.reciprocal(tot, tot))
                do(V.tensor_tensor(v3(gates), v3(gates), tot.unsqueeze(2).broadcast_to([P, TT, E1]), ALU.mult))
                place(v3(sel), v3(gates), E1, 1)

            def route2():
                lg = route[:, 0:16]
                e = route[:, 16:32]
                r_ = Slots(route, 32)
                sel, rank, mx, tot = r_.get(16), r_.get(16), r_.get(2), r_.get(2)
                v3 = lambda x: x.rearrange("p (a b) -> p a b", a=TT)
                dve.wait_ge(proj_saved, saved("router2"))
                chosen(v3(lg), 2, 8, 2, const("lower8"), v3(rank), v3(sel))
                do(V.tensor_reduce(mx, v3(lg), AX.X, ALU.max))
                ask(V.tensor_tensor(v3(e), v3(lg), mx.unsqueeze(2).broadcast_to([P, TT, E2]), ALU.subtract))
                answer()
                do(V.tensor_tensor(e, e, sel, ALU.mult))
                do(V.tensor_reduce(tot, v3(e), AX.X, ALU.add))
                do(V.reciprocal(tot, tot))
                do(V.tensor_tensor(v3(e), v3(e), tot.unsqueeze(2).broadcast_to([P, TT, E2]), ALU.mult))
                place(v3(sel), v3(e), E2, 2)

            def expert_steps(name, alpha):
                first, steps, before = phases[name]
                do(V.tensor_scalar(h[:], h[:], alpha, None, ALU.mult))

                def hidden(i, par):
                    for f in range(2):
                        n = 2 * (before + par) + f
                        dve.wait_ge(sg_ready, i * 4 + (n + 1))
                        V.tensor_tensor(hid[:, n % 4], sg[:, n % 2], F[n % 4][:, T:2 * T], ALU.mult)\
                            .then_inc(hid_ready, 1)

                def gather(i, par):
                    s = before + par
                    for j in range(4):
                        t, c = j // 2, j % 2
                        dve.wait_ge(y_ready, i * 8 + (4 * s + j + 1))
                        dve.wait_ge(y_added, i * 8 + (4 * s + j + 1))
                        hs = h[:, t, 512 * c:512 * c + 512]
                        V.scalar_tensor_tensor(out=hs, in0=B[j][:, :], scalar=1.0, in1=hs, op0=ALU.mult,
                                               op1=ALU.add).then_inc(y_added, 1)

                per_step_pair(nc.vector.Fori, steps, hidden, gather)
                dve.wait_ge(y_added, 4 * (before + steps) + CREDIT)

            def routed_round(name, q, rest):
                first, per, n_exp = phases[name]
                ys = per + 2
                iota = const("iota")

                def make_pick(e):
                    for t in range(TT):
                        ins = V.tensor_scalar(pick[:, t], iota, route_slot[:, t, bass.ds(e, 1)], None, ALU.is_equal)
                    ins.then_inc(q["slots"], 1)

                def make_gated(e):
                    for t in range(TT):
                        ins = V.tensor_scalar(gated[:, t], iota, route_slot[:, t, bass.ds(e, 1)],
                                              route_gate[:, t, bass.ds(e, 1)], ALU.is_equal, ALU.mult)
                    ins.then_inc(q["slots"], 1)

                def hidden(e, s, par):
                    dve.wait_ge(q["sg"], e * per + s + 1)
                    V.tensor_tensor(hidden_tok[:, par], hidden_sg[:, par], F[par][:, COLS:2 * COLS], ALU.mult)\
                        .then_inc(q["hid"], 1)

                def gather_y(e, s, par, first_=False):
                    y = e * ys + s
                    dve.wait_ge(q["y_ready"], y + 1)
                    dve.wait_ge(q["y_added"], y + 2)
                    for c in range(2):
                        part = y_slots[:, 512 * c:512 * c + 512]
                        if first_:
                            ins = V.tensor_copy(part, B[2 * par + c][:, :])
                        else:
                            ins = V.tensor_tensor(part, part, B[2 * par + c][:, :], ALU.add)
                    ins.then_inc(q["y_added"], 1)

                V.memset(pick, 0.0).then_inc(q["hid"], 2)
                V.memset(gated, 0.0).then_inc(q["y_added"], 1)
                V.tensor_scalar(route_slot, route_slot, -1.0 * SLOTS if rest else 0.0, None, ALU.add)\
                    .then_inc(q["y_added"], 1)
                dve.wait_ge(q["y_added"], 2)
                dve.wait_ge(q["hid"], 2)
                make_pick(0)
                with nc.vector.Fori(0, n_exp) as e:
                    make_gated(e)
                    dve.wait_ge(q["z_ready"], e * (per + 4) + 2)
                    make_pick(e + 1)
                    hidden(e, 0, 0)
                    hidden(e, 1, 1)
                    gather_y(e, 0, 0, True)
                    if per > 2:
                        with nc.vector.Fori(0, per // 2 - 1) as b:
                            hidden(e, b * 2 + 2, 0)
                            gather_y(e, b * 2 + 1, 1)
                            hidden(e, b * 2 + 3, 1)
                            gather_y(e, b * 2 + 2, 0)
                    gather_y(e, per - 1, 1)
                    for t in range(TT):
                        y = e * ys + per + t
                        dve.wait_ge(q["y_ready"], y + 1)
                        dve.wait_ge(q["y_added"], y + 2)
                        for c in range(2):
                            part = acc[:, t, 512 * c:512 * c + 512]
                            ins = V.tensor_tensor(part, part, B[2 * t + c][:, :], ALU.add)
                        ins.then_inc(q["y_added"], 1)
                dve.wait_ge(q["y_added"], n_exp * ys + 2)

            def routed_layer(name, n, alpha):
                do(V.tensor_scalar(acc, h, alpha, None, ALU.mult))
                routed_round(name, rounds[name][0], False)
                full = V.value_load(crowded[P - 1:P, n:n + 1], min_val=0, max_val=1)
                with V.If(full > 0):
                    routed_round(name, rounds[name][1], True)

            V.memset(ones[:], 1.0).then_inc(hid_ready, CREDIT)
            V.memset(pbias[:, 0:1], EPS).then_inc(y_added, CREDIT)
            dve.wait_ge(x_in, 16)
            layer_norm()
            dve.wait_ge(params_in, 16 * N_PARAMS)
            for a in range(2):
                ins = V.tensor_tensor(lamp[:, a], lamv[:, 2 * a], lamv[:, 2 * a + 1], ALU.mult)
            do(ins)
            ask(V.tensor_reduce(lams, lamp, AX.X, ALU.add))
            answer()
            for a in range(2):
                ins = V.tensor_scalar(neglam[:, a:a + 1], lame[:, 1:2], lame[:, 0:1], -LAM_INIT, ALU.subtract, ALU.add)
            V.tensor_scalar(dng, dng, 1.0 - LAM_INIT, None, ALU.mult)
            do(V.tensor_scalar(nsinks, sinks, -1.0, None, ALU.mult))
            dve.wait_ge(proj_saved, saved("mix1"))
            do(V.tensor_tensor(ffx, ffx, foxb.unsqueeze(1).broadcast_to([P, TT, FOX_H]), ALU.add))
            flat = lambda x: x.rearrange("p a b -> p (a b)")
            ask(V.scalar_tensor_tensor(out=flat(ffa), in0=flat(ffx), scalar=-1.0, in1=flat(ffx), op0=ALU.mult,
                                       op1=ALU.max))
            ask(V.scalar_tensor_tensor(out=flat(bcT), in0=flat(hfT), scalar=-1.0, in1=flat(hfT), op0=ALU.mult,
                                       op1=ALU.max))
            answer()
            do(V.scalar_tensor_tensor(out=flat(ffx), in0=flat(ffx), scalar=0.0, in1=flat(ffe), op0=ALU.min,
                                      op1=ALU.subtract))
            V.tensor_scalar(nlogf, ffx, -1.0, None, ALU.mult).then_inc(logf_ready, 1)
            do(V.scalar_tensor_tensor(out=flat(bcT), in0=flat(hfT), scalar=0.0, in1=flat(bcT), op0=ALU.min,
                                      op1=ALU.subtract))
            for j in range(HGRN_H):
                ins = V.tensor_tensor_scan(hfT[:, j], ones[:], bcT[:, j], 0.0, ALU.mult, ALU.add)
            do(ins)
            dve.wait_ge(proj_saved, saved("forget sums"))
            attend("mix1")
            dve.wait_ge(o_saved, groups_end("mix1"))
            V.tensor_tensor(dsq, yT[:, 2:4], yT[:, 2:4], ALU.mult).then_inc(squares_ready, 1)

            def level_argument(lv):
                b = LEVELS[lv]
                cut = lambda x: x.rearrange("p h t -> p (h t)").rearrange("p (n a b) -> p n a b", a=2, b=b)
                src, dst = cut(hfT), cut(decay[:, lv % 2])
                ref = src[:, :, 0, b - 1:b].broadcast_to([P, HGRN_H * T // (2 * b), b])
                if lv >= 2:
                    dve.wait_ge(hg_w, lv - 1)
                V.tensor_tensor(dst[:, :, 0, :], ref, src[:, :, 0, :], ALU.subtract)
                V.tensor_tensor(dst[:, :, 1, :], src[:, :, 1, :], ref, ALU.subtract).then_inc(hg_arg, 1)

            j = 0
            level_argument(0)
            for lv in range(len(LEVELS) + 1):
                if lv + 1 < len(LEVELS):
                    level_argument(lv + 1)
                for hp in range(1 if lv == 0 else 2):
                    dve.wait_ge(hg_scores, j + 1)
                    if j >= 3:
                        dve.wait_ge(hg_pv, j - 2)
                    if lv == 0:
                        ins = V.tensor_copy(SM[:, j % 3], F[j % 4][:, :])
                    else:
                        ins = V.tensor_tensor(SM[:, j % 3].rearrange("p (a b) -> p a b", a=4),
                                              F[j % 4][:, :].rearrange("p (a b) -> p a b", a=4),
                                              levelmask[:, lv - 1:lv, :].broadcast_to([P, 4, P]), ALU.mult)
                    ins.then_inc(hg_masked, 1)
                    j += 1
            answered[0] += 1
            answer()
            V.tensor_tensor(sqT, oT, oT, ALU.mult).then_inc(squares_ready, 1)
            dve.wait_ge(proj_saved, saved("mean squares"))
            V.scalar_tensor_tensor(out=yT[:, 2:4], in0=yT[:, 2:4], scalar=dng[:, 0:1], in1=drs, op0=ALU.mult,
                                   op1=ALU.mult).then_inc(y_normed, 1)
            do(V.scalar_tensor_tensor(out=oT, in0=oT, scalar=hng[:, 0:1], in1=decay[:, 0], op0=ALU.mult, op1=ALU.mult))
            V.tensor_tensor(yT[:, 4:8], oT, hgT, ALU.mult).then_inc(y_normed, 1)
            add("out1", ALPHA1)
            layer_norm()
            attend("mem1")
            add("mem1 out", ALPHA1)
            layer_norm()
            route1()
            routed_layer("moe1", 0, ALPHA1)
            layer_norm(acc)
            for i in range(2):
                if i == 0:
                    dve.wait_ge(proj_saved, saved("mix2"))
                    for t in range(TT):
                        do(V.tensor_tensor_reduce(out=work[:, t, 0:P], in0=ckv[:, t], in1=ckv[:, t], scale=1.0,
                                                  scalar=0.0, op0=ALU.mult, op1=ALU.add, accum_out=css[:, t:t + 1]))
                    ask(V.tensor_scalar(css, css, 1.0 / P, EPS, ALU.mult, ALU.add))
                    answer()
                    do(V.reciprocal(crstd, cstd))
                    for t in range(TT):
                        ins = V.scalar_tensor_tensor(out=ckv[:, t], in0=ckv[:, t], scalar=crstd[:, t:t + 1],
                                                     in1=ckvg, op0=ALU.mult, op1=ALU.mult)
                    ins.then_inc(latents_ready, 1)
                    for j in range(8):
                        dve.wait_ge(proj_saved, span("indexer")[0] + j + 1)
                        for t in range(TT):
                            ins = V.scalar_tensor_tensor(out=score[:, t], in0=idx_act[:, j % 2, t],
                                                         scalar=wi[:, t, j:j + 1],
                                                         in1=causal[:, t] if j == 0 else score[:, t],
                                                         op0=ALU.mult, op1=ALU.add)
                        ins.then_inc(idx_used, 1)
                        dve.wait_ge(idx_used, j + 1)
                    for rnd in range(TOPK // 8):
                        src = score if rnd == 0 else work
                        for t in range(TT):
                            ins = V.max(m8[:, t], src[:, t])
                        do(ins)
                        for t in range(TT):
                            ins = V.match_replace(work[:, t], m8[:, t], src[:, t], TAKEN)
                        do(ins)
                    do(V.tensor_scalar(work, work, TAKEN / 2, NEG, ALU.is_gt, ALU.mult))
                    attend("mix2")
                    add("out2", ALPHA2)
                else:
                    dve.wait_ge(proj_saved, saved("mix3"))
                    V.memset(Pc, 0.0)
                    V.memset(geluT, 0.0).then_inc(cmp_cleared, 1)
                    dve.wait_ge(cmp_cleared, 1)
                    dve.wait_ge(proj_saved, saved("compressed bias"))
                    pc = Pc.rearrange("p r t j n -> p (r t j) n")
                    for par in range(2):
                        a = add_span("compressed logits")[0] + par
                        dve.wait_ge(res_ready, a + 1)
                        V.tensor_tensor(pc[:, 16 * par:16 * par + 16, 0:N_CMP],
                                        F[a % 4][:, :].rearrange("p (a n) -> p a n", n=32)[:, :, 0:N_CMP],
                                        bcmp[:, par].rearrange("p t j n -> p (t j) n")[:, :, 0:N_CMP],
                                        ALU.add).then_inc(res_added, 1)
                    dve.wait_ge(res_added, add_span("compressed logits")[1])
                    pn = pc[:, :, 0:N_CMP]
                    do(V.tensor_reduce(cmx, pn, AX.X, ALU.max, negate=True))
                    ask(V.tensor_tensor(pn, pn, cmx.unsqueeze(2).broadcast_to([P, 32, N_CMP]), ALU.add))
                    answer()
                    do(V.tensor_reduce(csum, pn, AX.X, ALU.add))
                    do(V.reciprocal(csum, csum))
                    for par in range(2):
                        c2 = csum[:, 16 * par:16 * par + 16].rearrange("p (t j) -> p t j", t=TT)
                        gate = g3[:].rearrange("p t (j r c) -> p r c t j", r=2, c=3)[:, par, 0]
                        ins = V.tensor_tensor(c2, c2, gate, ALU.mult)
                    do(ins)
                    do(V.tensor_tensor(pn, pn, csum.unsqueeze(2).broadcast_to([P, 32, N_CMP]), ALU.mult))
                    for par in range(2):
                        for t in range(TT):
                            x = Pc[:, par, t, :, 0:N_CMP]
                            ins = V.tensor_tensor(x, x, valid[:, t:t + 1, :].broadcast_to([P, 8, N_CMP]), ALU.mult)
                    ins.then_inc(cmp_ready, 1)
                    attend("mix3")
                    add("out3", ALPHA2)
                layer_norm()
                attend(f"xa{i}")
                add(f"xa{i} out", ALPHA2)
                layer_norm()
                if i == 1:
                    route2()
                    routed_layer("moe2", 1, ALPHA2)
                    layer_norm(acc)
                else:
                    dve.wait_ge(proj_saved, saved("ln5 transposed"))
                    expert_steps("dense", ALPHA2)
                    layer_norm()


SMALL_LOADS = ["wff", "foxb", "lam0", "lam1", "lam2", "lam3", "dng", "dng2", "hng", "rw1", "rb1", "rw2", "ckvg", "sinks",
               "wuk", "wuv", "w2k", "w2v"]


class Slots:

    def __init__(self, tensor, at):
        self.tensor, self.at = tensor, at

    def get(self, n):
        self.at += n
        assert self.at <= 400
        return self.tensor[:, self.at - n:self.at]


def kernel(**inputs):
    import concourse.bacc as _bacc
    from concourse.bass_utils import run_bass_kernel_spmd as _run

    nc = _bacc.Bacc("TRN2", target_bir_lowering=False, num_devices=1)
    arrays, args = {}, {}
    named = dict(inputs)
    named["const_wide"], named["const_rows"] = CONST_WIDE, CONST_ROWS
    for name, a in named.items():
        a = np.ascontiguousarray(a)
        arrays[f"in_{name}_dram"] = a
        args[name] = nc.dram_tensor(f"in_{name}_dram", a.shape, mybir.dt.from_np(a.dtype), kind="ExternalInput").ap()
    out = nc.dram_tensor("out_0_dram", (1, T, D), F32, kind="ExternalOutput").ap()
    two_block_kernel(nc, args, out)
    r = _run(nc, [arrays], core_ids=[0])
    return r.results[0]["out_0_dram"]
```

```python
import math
from contextlib import ExitStack

import numpy as np

import concourse.bass as bass
from concourse import mybir

ALU = mybir.AluOpType
ACT = mybir.ActivationFunctionType
AX = mybir.AxisListType
F32 = mybir.dt.float32
R32 = mybir.dt.float32r

P = 128
T = 256
TT = T // P
D = 1024
KT = D // P
COLS = 256
RING = 6
SLOT = KT * COLS
CROWD = 128
SLOTS = 128
EPS = 1e-5
NEG = -1e30
TAKEN = -3e38

ALPHA1 = 2.0 ** 0.25
ALPHA2 = 4.0 ** 0.25
FOX_H, DIFF_H, HGRN_H, MEM_H = 4, 4, 4, 4
LAM_INIT = 0.8 - 0.6 * math.exp(0.0)
E1, FF1 = 16, 512
E2, FF2 = 8, 3584
FF_DENSE = 2816
TOPK = T // 4
N_CMP = 15
BUCKETS = 32
LEVELS = [128, 64, 32, 16, 8, 4, 2, 1]
BIAS_W = 384
ROW_W = 512


def shape_constants():
    p = np.arange(P)
    q = np.arange(T)
    eye = np.eye(P)
    flip = np.eye(P)[::-1]
    tri = np.stack([(p[:, None] + P * t <= q[None, :]) for t in range(TT)], 1).reshape(P, -1)
    causal = np.stack([np.where(q[None, :] <= p[:, None] + P * t, 0.0, NEG) for t in range(TT)], 1).reshape(P, -1)
    chunk = np.stack([np.where(q[None, :] // 64 <= (p[:, None] + P * t) // 64, 0.0, NEG) for t in range(TT)],
                     1).reshape(P, -1)
    levels = []
    for b in LEVELS[1:]:
        s, t = p[:, None], p[None, :]
        levels.append((s // (2 * b) == t // (2 * b)) & (s % (2 * b) < b) & (t % (2 * b) >= b))
    levels.append(p[:, None] == p[None, :])
    levels = np.stack(levels, 1).reshape(P, -1)
    halves = (p[:, None] // 64 == p[None, :] // 64)
    ends = 16 * np.arange(N_CMP) + 31
    valid = np.stack([(p[:, None] + P * t >= ends[None, :]) for t in range(TT)], 1).reshape(P, -1)
    lower = lambda n: np.broadcast_to((np.arange(n)[None, :] < np.arange(n)[:, None]).reshape(1, -1), (P, n * n))
    iota = np.broadcast_to(np.arange(SLOTS)[None, :], (P, SLOTS))
    parts = [("iota", iota), ("eye", eye), ("flip", flip), ("tri", tri), ("causal", causal), ("chunk", chunk), ("levels", levels),
             ("halves", halves), ("valid", valid), ("lower4", lower(4)), ("lower8", lower(8))]
    at, off = {}, 0
    for name, a in parts:
        at[name] = (off, a.shape[1])
        off += a.shape[1]
    wide = np.concatenate([np.asarray(a, np.float32) for _, a in parts], 1)

    def bucket(dist):
        n = np.maximum(dist, 1)
        log_b = 16 + (np.log(n / 16.0) / math.log(8.0) * 16).astype(np.int64)
        return np.where(dist < 16, np.maximum(dist, 0), np.minimum(log_b, BUCKETS - 1))

    def onehot(dist, ok):
        m = np.zeros((BUCKETS + 1, len(dist)))
        m[bucket(dist), np.arange(len(dist))] = ok
        m[BUCKETS] = ~ok
        return m
    j = np.arange(ROW_W)
    dist = 255 - j
    fwd = j - 255
    rows = np.stack([onehot(dist, dist >= 0), onehot(dist, (dist >= 0) & (dist < 128)), onehot(fwd, fwd >= 0)], 1)
    return at, np.ascontiguousarray(wide), rows.reshape(BUCKETS + 1, -1).astype(np.float32)


CONST_AT, CONST_WIDE, CONST_ROWS = shape_constants()


class Tally:

    def __init__(self, eng, sem):
        self.eng, self.sem, self.n = eng, sem, 0

    def did(self, ins):
        ins.then_inc(self.sem, 1)
        self.n += 1

    def wait(self):
        self.eng.wait_ge(self.sem, self.n)


def two_block_kernel(nc, I, out):
    ctx = ExitStack()
    with ctx:
        def sb(name, shape):
            return ctx.enter_context(nc.sbuf_tensor(name, shape, F32))[tuple(slice(None) for _ in shape)]

        def sb_rounded(name, shape):
            everything = tuple(slice(None) for _ in shape)
            with nc.sbuf_tensor(name + "_rounded", shape, F32) as same:
                rounded = same[everything]
            return sb(name, shape), rounded

        def sem(name):
            return ctx.enter_context(nc.semaphore(name))

        ring, ring_r = sb_rounded("ring", [P, RING, SLOT])
        h = sb("h", [P, TT, D])
        hT, hT_r = sb_rounded("hT", [P, KT, T])
        yT, yT_r = sb_rounded("yT", [P, KT, T])
        memT = sb("memT", [P, KT, T])
        mkT, mkT_r = sb_rounded("mkT", [P, KT, T])
        mv, mv_r = sb_rounded("mv", [P, TT, D])
        gb = sb("gb", [P, 2, D])
        cw = sb("cw", [P, CONST_WIDE.shape[1]])
        NS = 3
        S = sb("S", [P, NS, TT, T])
        PT, PT_r = sb_rounded("PT", [P, 2, TT, T])
        small = sb("small", [P, 1500])
        arena, arena_r = sb_rounded("arena", [P, 15872])

        def const(name):
            o, n = CONST_AT[name]
            return cw[:, o:o + n]
        eye, flip, halves = const("eye"), const("flip"), const("halves")
        tri = const("tri").rearrange("p (a k) -> p a k", a=TT)
        causal = const("causal").rearrange("p (a k) -> p a k", a=TT)
        chunkmask = const("chunk").rearrange("p (a k) -> p a k", a=TT)
        levelmask = const("levels").rearrange("p (a k) -> p a k", a=len(LEVELS))
        valid = const("valid").rearrange("p (t n) -> p t n", t=TT)

        small_used = [0]

        def tiny(*shape):
            n = int(np.prod(shape))
            o = small_used[0]
            small_used[0] += n
            assert small_used[0] <= 1500, small_used
            v = small[:, o:o + n]
            names = " ".join("abcd"[:len(shape)])
            return v if len(shape) == 1 else v.rearrange(f"p ({names}) -> p {names}",
                                                         **{c: s for c, s in zip("abcd", shape)})

        class Region:

            def __init__(self, start=0, memory=arena):
                self.at, self.memory = start, memory

            def get(self, *shape):
                n = int(np.prod(shape))
                v = self.memory[:, self.at:self.at + n]
                self.at += n
                assert self.at <= 15872, self.at
                names = " ".join("abcd"[:len(shape)])
                return v if len(shape) == 1 else v.rearrange(f"p ({names}) -> p {names}",
                                                             **{c: s for c, s in zip("abcd", shape)})

        r = Region()
        fqT, fkT, fv = r.get(2, T), r.get(2, T), r.get(TT, 256)
        dqT, dkT, dv = r.get(2, T), r.get(2, T), r.get(TT, 256)
        hqT, hfT, hi, hgT = r.get(4, T), r.get(4, T), r.get(TT, 512), r.get(4, T)
        hkT, bcT = r.get(4, T), r.get(4, T)
        decay = r.get(2, 4, T)
        Wlv = r.get(2, 4, T)
        SM = r.get(3, 512)
        oT, sqT = hqT, hfT
        dsq, drs = r.get(2, T), r.get(2, T)
        r = Region()
        hidden_sg = r.get(2, COLS)
        hidden_tok = r.get(2, COLS)
        hiddenT_hi = Region(r.at, arena_r).get(2, 2, SLOTS)
        hiddenT_lo = PT_r[:].rearrange("p a b c -> p (a b c)")[:, 0:512].rearrange("p (a b c) -> p a b c", a=2, b=2)
        r = Region(r.at + 512, arena_r)
        w_hi = [r.get(SLOT) for _ in range(4)] + [mkT_r[:].rearrange("p a b -> p (a b)"),
                                                  mv_r[:].rearrange("p a b -> p (a b)")]
        assert r.at <= 9728
        r = Region(9728)
        acc = r.get(TT, D)
        rr = Region(r.at, arena_r)
        xgT_hi, xgT_lo = rr.get(KT, SLOTS), rr.get(KT, SLOTS)
        r = Region(rr.at)
        y_slots = r.get(D)
        pick, gated = r.get(TT, SLOTS), r.get(TT, SLOTS)
        gatedT = r.get(TT, P)
        mem_tok = yT[:].rearrange("p a b -> p (a b)").rearrange("p (a b) -> p a b", a=TT)
        hankel = Region(3584).get(16, BIAS_W)
        mqT = Region().get(KT, T)
        r = Region()
        sg = r.get(2, T)
        hid_hi = Region(r.at, arena_r).get(4, T)
        hid_lo = PT_r[:].rearrange("p a b c -> p (a b) c")
        hid_all = S[:].rearrange("p a b c -> p (a b) c")
        x_hi, x_lo = yT_r, hT_r
        assert r.at + 4 * T <= 1536
        biasT = Region(15872 - 16 * BIAS_W).get(16, BIAS_W)
        r = Region()
        qaT, qiT, qbT = r.get(4, T), r.get(4, T), r.get(4, T)
        kiT, kbT, vb = r.get(T), r.get(2, T), r.get(TT, P)
        ckv, cT, qlatT = r.get(TT, P), r.get(T), r.get(8, T)
        olatT = qlatT
        idx_act = r.get(2, TT, T)
        score = r.get(TT, T)
        work = r.get(TT, T)
        assert r.at <= 15872 - 16 * BIAS_W, r.at
        r = Region()
        qcT = r.get(8, T)
        kvcT = r.get(2, T)
        ksT, vs, kwT, vw = r.get(2, T), r.get(TT, P), r.get(2, T), r.get(TT, P)
        Pc = r.get(2, TT, 8, 32)
        bcmp = r.get(2, TT, 8, 16)
        pcT = r.get(2, 2, T)
        geluT = r.get(2, 2, 32)
        windows = r.get(2, 32, N_CMP)
        gelu_tok = r.get(2, 2, P)
        kcT = r.get(2, 32)
        vc4 = r.get(2, 64)
        assert r.at <= 15872 - 16 * BIAS_W, r.at

        wff = tiny(KT, FOX_H)
        foxb = tiny(FOX_H)
        lamv = tiny(4, 32)
        dng, hng = tiny(1), tiny(1)
        rw1, rb1, rw2 = tiny(KT, E1), tiny(E1), tiny(KT, E2)
        ckvg = tiny(P)
        sinks = tiny(8)
        peT = tiny(2, 32)
        gain_T, bias_T = tiny(9, KT), tiny(9, KT)
        stats, mvar, veps, std, rstd = tiny(TT, 4, 6), tiny(TT, 2), tiny(TT), tiny(TT), tiny(TT)
        ffx = tiny(TT, FOX_H)
        ffa, ffe, nlogf, cumq = tiny(TT, FOX_H), tiny(TT, FOX_H), tiny(TT, FOX_H), tiny(TT, FOX_H)
        lamp, lams, lame, neglam = tiny(2, 32), tiny(2), tiny(2), tiny(2)
        nmx, ssum, rsum, esink = tiny(NS, TT), tiny(NS, TT), tiny(NS, TT), tiny(NS, TT)
        nsinks = tiny(8)
        wi = tiny(TT, 8)
        css, cstd, crstd = tiny(TT), tiny(TT), tiny(TT)
        m8 = tiny(TT, 8)
        eps = tiny(1)
        csum, cmx = tiny(32), tiny(32)

        wuk, wuv, w2kv = sb("wuk", [P, 4, P]), sb("wuv", [P, 8, 64]), sb("w2kv", [P, 2, 64])
        tab = sb("tab", [BUCKETS + 1, 16])
        ohot = sb("ohot", [BUCKETS + 1, 3, ROW_W])
        rowbuf = PT[0:16].rearrange("p a b c -> p a (b c)")
        rows_dram = nc.dram_tensor("bias_rows", (16, 2, ROW_W), F32, kind="Internal").ap()
        ones = sb("ones", [P, T])
        route = S[:].rearrange("p a b c -> p (a b c)")[:, 0:1000]
        route_slot, route_gate = tiny(TT, E1 + 1), tiny(TT, E1 + 1)
        route_count = tiny(TT, E1)
        crowded = ctx.enter_context(nc.sbuf_tensor("crowded", [P, 2], mybir.dt.int32))
        g3 = sb("g3", [P, TT, 48])

        F = [ctx.enter_context(nc.psum_tensor(f"psF{i}", [P, 512], F32)) for i in range(4)]
        B = [ctx.enter_context(nc.psum_tensor(f"psB{i}", [P, 512], F32)) for i in range(4)]

        def pair(bank, w=T):
            return bank[:, 0:2 * w].rearrange("p (a b) -> p a b", a=2)

        x_in, mem_in, mem2_in = sem("x_in"), sem("mem_in"), sem("mem2_in")
        consts_in, params_in, table_in = sem("consts_in"), sem("params_in"), sem("table_in")
        gb_in = sem("gb_in")
        w_in = [sem(f"weights_in{i}") for i in range(RING)]
        out_stored = sem("out_stored")
        rows_out, rows_back = sem("bias_rows_out"), sem("bias_rows_back")
        set_up = sem("set_up")
        ln_done, normed_half = sem("ln_done"), sem("normed_half_ready")
        proj_ready, proj_saved = sem("proj_ready"), sem("proj_saved")
        res_ready, res_added = sem("res_ready"), sem("res_added")
        logits_ready, scored, max_ready = sem("logits_ready"), sem("scored"), sem("max_ready")
        exp_ready, probs_ready = sem("exp_ready"), sem("probs_ready")
        pt_ready, pt_saved, pv_done, o_saved = sem("pt_ready"), sem("pt_saved"), sem("pv_done"), sem("o_saved")
        dve_step, act_step, pool_step = sem("dve_step"), sem("act_step"), sem("pool_step")
        gu_ready, sg_ready, hid_ready = sem("gate_up_ready"), sem("silu_ready"), sem("hidden_ready")
        y_ready, y_added = sem("y_ready"), sem("y_added")
        to_act, from_act = sem("dve_to_act"), sem("act_to_dve")
        logf_ready = sem("log_forget_ready")
        squares_ready, y_normed = sem("squares_ready"), sem("y_normed")
        latents_ready, penalty_ready = sem("latents_ready"), sem("penalty_ready")
        dense_hi, dense_lo = sem("dense_high"), sem("dense_low")
        dense_hi_down, dense_lo_down = sem("dense_high_down"), sem("dense_low_down")
        tokens_hi, tokens_lo, hid_parted = sem("tokens_high"), sem("tokens_low"), sem("hidden_parted")
        windows_ready, cmp_ready = sem("windows_ready"), sem("compressed_probs_ready")
        idx_used = sem("indexer_product_used")
        hg_arg, hg_exp, hg_w = sem("level_argument"), sem("level_decay"), sem("level_operands")
        hg_scores, hg_masked, hg_pv = sem("level_scores"), sem("level_masked"), sem("level_pv")

        def pass_sems(name, ring_too):
            d = {k: sem(f"{name}_{k}") for k in (
                "slots", "z_ready", "z_hi", "z_saved", "gate", "gu", "sg", "hid", "y_ready", "y_added", "hi", "hi_down", "lo",
                "lo_down")}
            if ring_too:
                d["w_in"] = [sem(f"{name}_weights_in{i}") for i in range(RING)]
            return d
        rounds = {name: [pass_sems(name, False), pass_sems(name + "_rest", True)] for name in ("moe1", "moe2")}
        chosen_ready, counted = sem("experts_chosen"), sem("experts_counted")

        chunks = []
        freed = {}
        landed = [0] * RING
        ready_at = {}

        def chunk(src, kt=KT, w=COLS):
            c = len(chunks)
            pieces = src if isinstance(src, list) else [(0, P, src)]
            chunks.append((pieces, kt, w))
            landed[c % RING] += 16 * len(pieces)
            ready_at[c] = landed[c % RING]
            return c

        def wview(c, kt, w):
            return ring[:, c % RING, 0:kt * w].rearrange("p (a n) -> p a n", a=kt)

        def kxn(ap):
            return ap.rearrange("(a p) n -> p a n", p=P)

        units = []
        adds = []

        def unit(stage, kind, args, dest, func=ACT.Copy, scale=1.0):
            units.append((stage, kind, args, dest, func, scale))
            if kind in ("T", "tok", "dup") and args[1] is not None:
                freed[args[1]] = (proj_ready, len(units))
            if kind == "hidden":
                for c in args[2]:
                    freed[c] = (proj_ready, len(units))

        def span(stage):
            n = [i for i, u in enumerate(units) if u[0] == stage]
            return n[0], n[-1] + 1

        def add_span(stage):
            n = [i for i, u in enumerate(adds) if u[0] == stage]
            return n[0], n[-1] + 1

        def transposes(stage, src, dst, norm=None):
            for j in range(0, KT, 2):
                unit(stage, "tr", (src, j, norm), dst[:, j:j + 2, :])

        def project(stage, kind, x, src, dest, c0, n, func=ACT.Copy, scale=1.0, dstT=True):
            for j in range(n):
                c = chunk(kxn(src)[:, :, c0 + j * COLS:c0 + (j + 1) * COLS])
                d = dest[:, 2 * j:2 * j + 2, :] if kind == "T" else dest[:, :, j * COLS:(j + 1) * COLS]
                unit(stage, kind, (x, c, KT, COLS, 0, COLS), d, func, scale)

        def residual(stage, src, kt=KT):
            for j in range(D // COLS):
                c = chunk(kxn(src)[:, :, j * COLS:(j + 1) * COLS], kt)
                adds.append((stage, c, kt, j))
                freed[c] = (res_ready, len(adds))

        phases = {}
        steps_before = [0]

        def experts(name, steps):
            phases[name] = (len(chunks), steps, steps_before[0])
            for s in range(steps):
                g = steps_before[0] + s
                for part in range(3):
                    c = len(chunks)
                    chunks.append((None, 0, 0))
                    landed[c % RING] += 16
                    ready_at[c] = landed[c % RING]
                    freed[c] = (gu_ready, 2 * g + 2) if part < 2 else (y_ready, 4 * g + 4)
            steps_before[0] += steps

        def routed(name, n_exp, per):
            q = rounds[name][0]
            phases[name] = (len(chunks), per, n_exp)
            for e in range(n_exp):
                for s in range(per):
                    for part in range(3):
                        c = len(chunks)
                        chunks.append((None, 0, 0))
                        landed[c % RING] += 16
                        ready_at[c] = landed[c % RING]
                        freed[c] = (q[("gate", "gu")[part]], e * per + s + 1) if part < 2 else (q["y_ready"], e * (per + 2) + s + 1)

        transposes("mem1 transposed", mem_tok, memT)
        project("mem1 keys", "T", memT, I["mem_wk"][0], mkT, 0, 4)
        project("mem1 values", "tok", memT, I["mem_wv"][0], mv, 0, 4)
        for a in range(2):
            unit("bias rows", "row", (a,), rowbuf[:, a, :])
        transposes("ln0 transposed", h, hT, 0)
        w = I["w_in"][0]
        project("mix1", "T", hT, w, hfT, 2052, 2)
        unit("mix1", "tok", (hT, None, KT, FOX_H, 0, FOX_H), ffx)
        project("mix1", "T", hT, w, fqT, 0, 1, scale=0.125)
        project("mix1", "T", hT, w, fkT, 256, 1)
        project("mix1", "tok", hT, w, fv, 512, 1)
        project("mix1", "T", hT, w, dqT, 772, 1, scale=32.0 ** -0.5)
        project("mix1", "T", hT, w, dkT, 1028, 1)
        project("mix1", "tok", hT, w, dv, 1284, 1)
        project("mix1", "tok", hT, w, hi, 2564, 2)
        project("mix1", "T", hT, w, hqT, 1540, 2, func=ACT.Silu)
        project("mix1", "T", hT, w, hgT, 3076, 2, func=ACT.Silu)
        unit("forget sums", "cum", (nlogf, FOX_H), cumq, ACT.Copy, -1.0)
        unit("mean squares", "sumsq", (halves, dsq, 1.0 / 64), drs)
        for a in range(2):
            unit("mean squares", "sumsq", (ones[:, 0:P], sqT[:, 2 * a:2 * a + 2, :], 1.0 / P),
                 decay[:, 0, 2 * a:2 * a + 2, :])
        residual("out1", I["w_out"][0])
        transposes("ln1 transposed", h, hT, 1)
        project("mem1 queries", "T", hT, I["mem_wq"][0], mqT, 0, 4, scale=1.0 / 16)
        residual("mem1 out", I["mem_wo"][0])
        transposes("ln2 transposed", h, hT, 2)
        route_in = route[:, 0:TT * E1].rearrange("p (a b) -> p a b", a=TT)
        unit("router1", "tok", (hT, None, KT, E1, 0, E1), route_in, ACT.Sigmoid)
        unit("count1", "cum", (route_gate[:, :, 0:E1], E1), route_count)
        routed("moe1", E1, FF1 // COLS)
        transposes("mem2 transposed", mem_tok, memT)
        for i in range(2):
            project(f"xa{i} keys", "T", memT, I["xa_w_k_2"][i], mkT, 0, 2)
            project(f"xa{i} values", "tok", memT, I["xa_w_v_2"][i], mv, 0, 2)
            for j in range(8 * i, 16):
                unit(f"bias tiles {i}", "flip", (j,), biasT[:, j, :])
            transposes(f"ln{3 * i + 3} transposed", h, hT, 3 * i + 3)
            if i == 0:
                w = I["ev_w_in_2"][0]
                c = chunk(kxn(w)[:, :, 512:640], w=128)
                unit("mix2", "tok", (hT, c, KT, 128, 0, 128), ckv)
                c = chunk(kxn(w)[:, :, 1152:1224], w=72)
                unit("mix2", "dup", (hT, c, KT, 72, 0, 1), kiT)
                unit("mix2", "tok", (hT, c, KT, 72, 64, 8), wi, ACT.Copy, 8.0 ** -0.5)
                project("mix2", "T", hT, w, qiT, 640, 2)
                for j in range(8):
                    unit("indexer", "idx", (j,), idx_act[:, j % 2], ACT.Relu, 0.125)
                project("mix2b", "T", hT, w, qaT, 0, 2)
                project("mix2b", "T", hT, w, qbT, 1224, 2, scale=0.125)
                c = chunk(kxn(w)[:, :, 1736:1992])
                unit("mix2b", "dup", (hT, c, KT, 256, 0, 2), kbT)
                unit("mix2b", "tok", (hT, c, KT, 256, 128, 128), vb)
                for j in (0, 4, 1, 5):
                    unit("latent queries", "uk", (j,), qlatT[:, j:j + 3:2, :], ACT.Copy, 0.125)
                unit("latent keys", "ctr", (), cT)
                for j in range(4):
                    unit("latent out", "uv", (j,), yT[:, j, :])
                residual("out2", I["ev_w_out_2"][0])
            else:
                w = I["od_w_in_2"][0]
                project("mix3", "T", hT, w, kvcT, 1024, 1)
                project("mix3", "T", hT, w, qcT, 0, 4, scale=0.125)
                for c0, kd, vd in ((1280, ksT, vs), (1536, kwT, vw)):
                    c = chunk(kxn(w)[:, :, c0:c0 + 256])
                    unit("mix3", "dup", (hT, c, KT, 256, 0, 2), kd)
                    unit("mix3", "tok", (hT, c, KT, 256, 128, 128), vd)
                c = chunk(kxn(w)[:, :, 1792:1840], w=48)
                unit("mix3", "tok", (hT, c, KT, 48, 0, 48), g3, ACT.Sigmoid)
                unit("compressed bias", "cb", (), bcmp)
                for br, name in enumerate(("od_w1_k_2", "od_w1_v_2")):
                    v = I[name][0].rearrange("(j d) c -> d j c", d=64)
                    cs = [chunk([(0, 64, v[:, 16 * a:16 * a + 16, :]), (64, 64, v[:, 16 * a:16 * a + 16, :])], 16, 128)
                          for a in range(2)]
                    for g in range(2):
                        unit("compress hidden", "hidden", (br, g, cs), gelu_tok[0:N_CMP, br, g, :],
                             ACT.Gelu_apprx_tanh)
                unit("compress turned", "gtr", (), geluT[:, :, :, 0:N_CMP])
                unit("compress out", "kc", (), kcT)
                unit("compress out", "vc", (), vc4)
                for par in range(2):
                    adds.append(("compressed logits", None, par, None))
                for par in range(2):
                    unit("compressed probs", "pctr", (par,), pcT[:, par])
                residual("out3", I["od_w_out_2"][0])
            transposes(f"ln{3 * i + 4} transposed", h, hT, 3 * i + 4)
            project(f"xa{i} queries", "T", hT, I["xa_w_q_2"][i], mqT, 0, 2, scale=128.0 ** -0.5)
            residual(f"xa{i} out", I["xa_w_o_2"][i], 4)
            transposes(f"ln{3 * i + 5} transposed", h, hT, 3 * i + 5)
            if i == 0:
                experts("dense", FF_DENSE // COLS)
            else:
                unit("router2", "tok", (hT, None, KT, E2, 0, E2), route[:, 0:TT * E2].rearrange(
                    "p (a b) -> p a b", a=TT))
                unit("count2", "cum", (route_gate[:, :, 0:E2], E2), route_count[:, :, 0:E2])
                routed("moe2", E2, FF2 // COLS)

        maps, groups, map_span = [], [], {}

        def attention(stage, items):
            m0, g0 = len(maps), len(groups)
            for members, dest in items:
                for n, mp in enumerate(members):
                    base = mp.setdefault("base", 0)
                    same = [i for i, o in enumerate(members) if o.get("base", 0) == base]
                    mp.update(group=len(groups), new=(n == 0), first=(n == same[0]), last=(n == same[-1]),
                              end=(n == len(members) - 1))
                    maps.append(mp)
                groups.append((len(maps) - 1, dest))
            map_span[stage] = (m0, len(maps), g0, len(groups))

        def half(j):
            return slice(64 * (j % 2), 64 * (j % 2) + 64)

        fox = [([dict(qk=[(fqT[half(j), j // 2, :], fkT[half(j), j // 2, :])], mask=causal, fox=j,
                      v=fv[:, :, 64 * j:64 * j + 64], base=64 * (j % 2)) for j in (2 * a, 2 * a + 1)],
                yT[:, a, :]) for a in range(2)]

        def diff_map(j, c):
            rows = slice(32 * (2 * (j % 2) + c), 32 * (2 * (j % 2) + c) + 32)
            return dict(qk=[(dqT[rows, j // 2, :], dkT[rows, j // 2, :])], mask=chunkmask,
                        coef=neglam if c else None, v=dv[:, :, 64 * j:64 * j + 64], base=64 * (j % 2))
        diff = [([diff_map(j, c) for j in (2 * a, 2 * a + 1) for c in range(2)], yT[:, 2 + a, :]) for a in range(2)]
        attention("mix1", fox + diff)
        attention("mem1", [([dict(qk=[(mqT[:, 2 * j + a, :], mkT[:, 2 * j + a, :]) for a in range(2)],
                                  v=mv[:, :, 256 * j:256 * j + 256])], yT[:, 2 * j:2 * j + 2, :]) for j in range(4)])

        def bias_of(j):
            v = biasT[:, j, P:P + T]
            return bass.AP(tensor=v.tensor, offset=v.offset, ap=[v.ap[0], [-P, TT], [1, T]])
        lat = [([dict(qk=[(qlatT[:, j, :], cT)], mask=bias_of(j), extra=work, v=ckv[:, :, 0:P])],
                olatT[:, j, :]) for j in range(8)]
        win = [([dict(qk=[(qbT[half(j), j // 2, :], kbT[half(j), j // 4, :])], mask=bias_of(8 + j), sink=j,
                      v=vb[:, :, 64 * (j // 4):64 * (j // 4) + 64], base=64 * (j % 2)) for j in (2 * a, 2 * a + 1)],
                yT[:, 4 + a, :]) for a in range(4)]
        attention("mix2", win + lat)
        cross = [([dict(qk=[(mqT[:, j, :], mkT[:, j, :])], v=mv[:, :, P * j:P * j + P])], yT[:, j, :])
                 for j in range(4)]
        attention("xa0", cross)

        def nsa_maps(j):
            g = j // 8
            out = []
            for branch, (k, v) in enumerate(((ksT, vs), (kwT, vw))):
                out.append(dict(qk=[(qcT[half(j), j // 2, :], k[half(j), g, :])], mask=bias_of(j),
                                coef=g3[:, :, 3 * j + 1 + branch], v=v[:, :, 64 * g:64 * g + 64], base=64 * (j % 2),
                                compressed=j if branch == 0 else None))
            return out
        attention("mix3", [(nsa_maps(2 * a) + nsa_maps(2 * a + 1), yT[:, a, :]) for a in range(8)])
        attention("xa1", [([dict(mp) for mp in members], dest) for members, dest in cross])

        def saved(stage):
            return span(stage)[1]

        def maps_end(stage):
            return map_span[stage][1]

        def groups_end(stage):
            return map_span[stage][3]

        N_PARAMS = len(SMALL_LOADS) + 4 + 6
        CREDIT = 4
        n_steps = steps_before[0]
        block = ctx.enter_context(nc.Block())

        @block.sync
        def _(sp):
            sp.dma_start(h[:], I["x"][0].rearrange("(t p) d -> p t d", p=P)).then_inc(x_in, 16)
            sp.dma_start(mem_tok, I["mem"][0].rearrange("(t p) d -> p t d", p=P)).then_inc(mem_in, 16)

            def load(c):
                pieces, kt, w = chunks[c]
                if c >= RING:
                    sp.wait_ge(*freed[c - RING])
                for row, n, src in pieces:
                    sp.dma_start(ring[row:row + n, c % RING, 0:kt * w].rearrange("p (a n) -> p a n", a=kt),
                                 src).then_inc(w_in[c % RING], 16)

            def expert_views(wg, wu, wd):
                return (wg.rearrange("e (a p) (c n) -> e c p a n", p=P, n=COLS),
                        wu.rearrange("e (a p) (c n) -> e c p a n", p=P, n=COLS),
                        wd.rearrange("e (c f p) n -> e c p f n", p=P, f=2))

            def load_part(w, e, c, part, slot, landed_):
                kt = KT if part < 2 else 2
                sp.dma_start(ring[:, slot, :].rearrange("p (a n) -> p a n", a=kt),
                             w[bass.ds(e, 1), bass.ds(c, 1)].rearrange("e c p a n -> p (e c a) n"))\
                    .then_inc(landed_[slot], 16)

            def load_dense(first, steps, before, views):
                def step(c, par, g, peeled):
                    for part, w in enumerate(views):
                        if peeled:
                            sp.wait_ge(*freed[first + 3 * par + part - RING])
                        elif part < 2:
                            sp.wait_ge(gu_ready, g * 2 - 2)
                        else:
                            sp.wait_ge(y_ready, g * 4 - 4)
                        load_part(w, 0, c, part, (first + 3 * par + part) % RING, w_in)

                for s in range(2):
                    step(s, s, before + s, True)
                with nc.sync.Fori(1, steps // 2) as b:
                    for s in range(2):
                        step(b * 2 + s, s, b * 2 + (before + s), False)
                if steps % 2:
                    step(steps - 1, 0, before + steps - 1, False)

            def load_routed(first, per, n_exp, views, q, landed_, rest):
                def part_of(e, s, par, part, where):
                    if where == "start":
                        if not rest:
                            sp.wait_ge(*freed[first + 3 * par + part - RING])
                    elif part < 2:
                        sp.wait_ge(q[("gate", "gu")[part]], e * per + s - 1)
                    elif where == "turn":
                        sp.wait_ge(q["y_ready"], e * (per + 2) + s - 3)
                    else:
                        sp.wait_ge(q["y_ready"], e * (per + 2) + s - 1)
                    load_part(views[part], e, s, part, (first + 3 * par + part) % RING, landed_)

                def step(e, s, par, where, where_before):
                    part_of(e, s, par, 0, where)
                    part_of(e, s, par, 1, where)
                    if where_before is not None:
                        part_of(e, s - 1, 1 - par, 2, where_before)

                def expert(e, where):
                    step(e, 0, 0, where, None)
                    step(e, 1, 1, where, where)
                    if per > 2:
                        step(e, 2, 0, "in", where)
                        step(e, 3, 1, "in", "in")
                        with nc.sync.Fori(2, per // 2) as b:
                            step(e, b * 2, 0, "in", "in")
                            step(e, b * 2 + 1, 1, "in", "in")
                    part_of(e, per - 1, 1, 2, where if per == 2 else "in")
                expert(0, "start")
                with nc.sync.Fori(1, n_exp) as e:
                    expert(e, "turn")

            order = [("moe1", ("w1", "w3", "w2"), E1, FF1, True), ("dense", ("ff_w_gate_2", "ff_w_up_2", "ff_w_down_2"), 1,
                     FF_DENSE, False), ("moe2", ("moe_w_gate_2", "moe_w_up_2", "moe_w_down_2"), E2, FF2, True)]
            at = 0
            for name, ws, n_exp, ff, experts_dim in order:
                first, steps, _ = phases[name]
                for c in range(at, first):
                    load(c)
                wg, wu, wd = [I[x][0] if experts_dim else I[x] for x in ws]
                views = expert_views(wg, wu, wd)
                if name == "dense":
                    load_dense(first, steps, phases[name][2], views)
                    at = first + 3 * steps
                    continue
                per, n_exp = steps, phases[name][2]
                q, rest = rounds[name]
                load_routed(first, per, n_exp, views, q, w_in, False)
                at = first + 3 * per * n_exp
                sp.wait_ge(counted, 1 if name == "moe1" else 2)
                full = nc.sync.value_load(crowded[P - 1:P, 0:1] if name == "moe1" else crowded[P - 1:P, 1:2],
                                          min_val=0, max_val=1)
                with nc.sync.If(full > 0):
                    for c in range(at - RING, at):
                        sp.wait_ge(*freed[c])
                    load_routed(first, per, n_exp, views, rest, rest["w_in"], True)
                    sp.wait_ge(rest["y_ready"], n_exp * (per + 2))
            assert at == len(chunks)
            sp.wait_ge(ln_done, 10)
            sp.dma_start(out[0].rearrange("(t p) d -> p t d", p=P), h[:]).then_inc(out_stored, 16)
            sp.wait_ge(out_stored, 16)

        @block.gpsimd
        def _(pool):
            pool.dma_start(cw[:], I["const_wide"]).then_inc(consts_in, 16)
            pool.dma_start(ohot[:].rearrange("p a b -> p (a b)"), I["const_rows"]).then_inc(table_in, 16)
            pool.dma_start(tab[0:BUCKETS, :], I["rel_table_2"]).then_inc(table_in, 16)
            nc.gpsimd.memset(tab[BUCKETS:BUCKETS + 1, :], NEG).then_inc(set_up, 1)

            ln_params = [(I["ln_in_g"], I["ln_in_b"])] + [(I["ln_g"][0, i], I["ln_b"][0, i]) for i in range(3)] + \
                [(I["ln_g_2"][a, i], I["ln_b_2"][a, i]) for a in range(2) for i in range(3)]

            def load_gb(n):
                if n:
                    pool.wait_ge(ln_done, n)
                for k in range(2):
                    pool.dma_start(gb[:, k, :], across(ln_params[n][k])).then_inc(gb_in, 16)

            def across(row):
                return bass.AP(tensor=row.tensor, offset=row.offset, ap=[[0, P]] + list(row.ap))

            load_gb(0)
            small_loads = {
                "wff": (wff, kxn(I["w_in"][0])[:, :, 768:772]), "foxb": (foxb, across(I["fox_fb"][0])),
                "lam0": (lamv[:, 0], across(I["lam_q1"][0])), "lam1": (lamv[:, 1], across(I["lam_k1"][0])),
                "lam2": (lamv[:, 2], across(I["lam_q2"][0])), "lam3": (lamv[:, 3], across(I["lam_k2"][0])),
                "dng": (dng[0:64], I["diff_norm_g"][0].rearrange("(p a) -> p a", a=1)),
                "dng2": (dng[64:128], I["diff_norm_g"][0].rearrange("(p a) -> p a", a=1)),
                "hng": (hng, I["hgrn_norm_g"][0].rearrange("(p a) -> p a", a=1)),
                "rw1": (rw1, kxn(I["router_w"])), "rb1": (rb1, across(I["router_b"])),
                "rw2": (rw2, kxn(I["moe_w_router_2"][0])), "ckvg": (ckvg, across(I["ev_ckv_gain_2"][0])),
                "sinks": (sinks, across(I["ev_sinks_2"][0])),
                "wuk": (wuk[:], I["ev_w_uk_2"][0].rearrange("(a b) d c -> (b d) a c", b=2)),
                "wuv": (wuv[:], I["ev_w_uv_2"][0].rearrange("h c d -> c h d")),
                "w2k": (w2kv[:, 0], I["od_w2_k_2"][0]), "w2v": (w2kv[:, 1], I["od_w2_v_2"][0]),
            }
            assert list(small_loads) == SMALL_LOADS
            for dst, src in small_loads.values():
                pool.dma_start(dst, src, allow_slow_non_contiguous=True).then_inc(params_in, 16)
            for b in range(2):
                for k, name in enumerate(("od_pe_k_2", "od_pe_v_2")):
                    pool.dma_start(peT[64 * b:64 * b + 64, k], I[name][0].rearrange("j d -> d j"),
                                   allow_slow_non_contiguous=True).then_inc(params_in, 16)

            columns = lambda x: x.rearrange("n (k p) -> p n k", p=P)
            for dst, first_, last_, layers in ((gain_T, "ln_in_g", "ln_g", "ln_g_2"), (bias_T, "ln_in_b", "ln_b", "ln_b_2")):
                pool.dma_start(dst[:, 0], I[first_].rearrange("(k p) -> p k", p=P), allow_slow_non_contiguous=True)\
                    .then_inc(params_in, 16)
                pool.dma_start(dst[:, 1:4], columns(I[last_][0]), allow_slow_non_contiguous=True).then_inc(params_in, 16)
                pool.dma_start(dst[:, 4:9], columns(I[layers].rearrange("a b c -> (a b) c"))[:, 0:5],
                               allow_slow_non_contiguous=True).then_inc(params_in, 16)

            pool.wait_ge(proj_saved, saved("bias rows"))
            pool.dma_start(rows_dram, rowbuf).then_inc(rows_out, 16)

            def hankel_rows(heads, variant):
                src = bass.AP(tensor=rows_dram.tensor, offset=heads[0] * 2 * ROW_W + variant * ROW_W,
                              ap=[[1, P], [2 * ROW_W, len(heads)], [1, BIAS_W]])
                pool.dma_start(hankel[:, heads[0]:heads[0] + len(heads), :], src).then_inc(rows_back, 16)

            load_gb(1)
            for lv, b in enumerate(LEVELS):
                pool.wait_ge(hg_exp, lv + 1)
                if lv >= 2:
                    pool.wait_ge(hg_scores, 2 * (lv - 1) - 1)
                for side, src in enumerate((hkT, hqT)):
                    def view(x):
                        return x.rearrange("p h t -> p (h t)").rearrange("p (n a b) -> p n a b", a=2, b=b)[:, :, side, :]
                    ins = nc.gpsimd.tensor_tensor(view(Wlv[:, lv % 2]), view(decay[:, lv % 2]), view(src), ALU.mult)
                ins.then_inc(hg_w, 1)
            load_gb(2)
            load_gb(3)
            pool.dma_start(mem_tok, I["mem_2"][0].rearrange("(t p) d -> p t d", p=P)).then_inc(mem2_in, 16)
            def routed_round(name, q):
                first, per, n_exp = phases[name]

                def low(e, s, par):
                    pool.wait_ge(q["hi_down"], e * per + s + 1)
                    slot = (first + 3 * par + 2) % RING
                    nc.gpsimd.tensor_tensor(ring_r[:, slot].bitcast(R32), ring[:, slot], w_hi[slot], ALU.subtract)\
                        .then_inc(q["lo_down"], 1)

                with nc.gpsimd.Fori(0, n_exp) as e:
                    with nc.gpsimd.Fori(0, per // 2) as b:
                        for par in range(2):
                            low(e, b * 2 + par, par)

            def routed_layer(name, n):
                routed_round(name, rounds[name][0])
                pool.wait_ge(counted, n + 1)
                full = nc.gpsimd.value_load(crowded[P - 1:P, n:n + 1], min_val=0, max_val=1)
                with nc.gpsimd.If(full > 0):
                    routed_round(name, rounds[name][1])

            routed_layer("moe1", 0)
            pool.wait_ge(normed_half, 8)
            pool.wait_ge(rows_out, 16)
            hankel_rows(list(range(8)), 0)
            hankel_rows(list(range(8, 16)), 1)
            for n in range(4, 6):
                load_gb(n)
            first, steps, _ = phases["dense"]

            def low_down(i, par):
                pool.wait_ge(dense_hi_down, i * 2 + (par + 1))
                slot = (first + 3 * par + 2) % RING
                nc.gpsimd.tensor_tensor(ring_r[:, slot].bitcast(R32), ring[:, slot], w_hi[slot], ALU.subtract)\
                    .then_inc(dense_lo_down, 1)

            with nc.gpsimd.Fori(0, steps // 2) as i:
                for par in range(2):
                    low_down(i, par)
            low_down(steps // 2, 0)
            load_gb(6)
            pool.wait_ge(normed_half, 14)
            hankel_rows(list(range(8, 16)), 0)
            for n in range(7, 10):
                load_gb(n)
            routed_layer("moe2", 1)

        def per_step_pair(fori, steps, head, tail):
            assert steps % 2
            def turn(i, more):
                head(i, 1, True)
                tail(i, 0)
                head(i + 1, 0, more)
                tail(i, 1)

            head(0, 0, True)
            n = (steps - 1) // 2
            with fori(0, n - 1) as i:
                turn(i, True)
            turn(n - 1, False)
            tail(n, 0)

        @block.tensor
        def _(pe):
            mm = nc.tensor.matmul

            def weights(c):
                pe.wait_ge(w_in[c % RING], ready_at[c])
                _, kt, w = chunks[c]
                return wview(c, kt, w)

            def parts(first, par, part):
                slot = (first + 3 * par + part) % RING
                return (x.rearrange("p (a n) -> p a n", a=KT if part < 2 else 2) for x in (w_hi[slot], ring_r[:, slot]))

            def product(bank, x_hi_, x_lo_, w_hi_, w_lo_, start, stop):
                x1, x2, w1, w2 = (v.bitcast(R32) for v in (x_hi_, x_lo_, w_hi_, w_lo_))
                mm(bank, x1, w1, start=start, stop=False)
                mm(bank, x1, w2, start=False, stop=False)
                return mm(bank, x2, w1, start=False, stop=stop)

            def emit(u):
                stage, kind, args, dest, _, _ = units[u]
                bank = B[2 + u % 2]
                if u >= 2:
                    pe.wait_ge(proj_saved, u - 1)
                if kind == "T":
                    x, c, kt, w, _, _ = args
                    wt = weights(c)
                    for j in range(2):
                        for k in range(kt):
                            last = mm(bank[:, T * j:T * j + T], wt[:, k, P * j:P * j + P], x[:, k, :],
                                      start=(k == 0), stop=(k == kt - 1))
                elif kind == "tok":
                    x, c, kt, w, c0, n = args
                    wt = weights(c) if c is not None else {"mix1": wff, "router1": rw1, "router2": rw2}[stage]
                    for t in range(TT):
                        for k in range(kt):
                            last = mm(bank[:, n * t:n * t + n], x[:, k, P * t:P * t + P], wt[:, k, c0:c0 + n],
                                      start=(k == 0), stop=(k == kt - 1))
                elif kind == "dup":
                    x, c, kt, w, c0, groups_ = args
                    wt = weights(c)
                    for g in range(groups_):
                        for b in range(2):
                            for k in range(kt):
                                last = mm(bank[64 * b:64 * b + 64, T * g:T * g + T], wt[:, k, 64 * g:64 * g + 64],
                                          x[:, k, :], start=(k == 0), stop=(k == kt - 1))
                elif kind == "tr":
                    src, j0, norm = args
                    if norm is not None:
                        pe.wait_ge(normed_half, 2 * norm + 1 + j0 // 4)
                    for j in range(2):
                        for t in range(TT):
                            last = nc.tensor.transpose(bank[:, T * j + P * t:T * j + P * t + P],
                                                       src[:, t, P * (j0 + j):P * (j0 + j) + P], eye)
                elif kind == "ctr":
                    for t in range(TT):
                        last = nc.tensor.transpose(bank[:, P * t:P * t + P], ckv[:, t, :], eye)
                elif kind == "pctr":
                    for a in range(2):
                        for t in range(TT):
                            blk = Pc[:, args[0], t, 4 * a:4 * a + 4, :].rearrange("p a b -> p (a b)")
                            last = nc.tensor.transpose(bank[:, T * a + P * t:T * a + P * t + P], blk, eye)
                elif kind == "row":
                    last = mm(bank[0:16, :], tab[:], ohot[:, args[0], :], start=True, stop=True)
                elif kind == "flip":
                    last = mm(bank[:, 0:BIAS_W], flip, hankel[:, args[0], :], start=True, stop=True)
                elif kind == "cum":
                    for t in range(TT):
                        for st in range(TT):
                            src, n = args
                            last = mm(bank[:, n * t:n * t + n], tri[:, st, P * t:P * t + P], src[:, st, :],
                                      start=(st == 0), stop=(st == TT - 1))
                elif kind == "sumsq":
                    lhs, sq, _ = args
                    last = mm(bank[:, :], lhs, sq.rearrange("p a b -> p (a b)"), start=True, stop=True)
                elif kind == "uk":
                    for a in range(2):
                        j = args[0] + 2 * a
                        last = mm(bank[:, T * a:T * a + T], wuk[half(j), j // 2, :], qaT[half(j), j // 2, :],
                                  start=True, stop=True)
                elif kind == "idx":
                    j = args[0]
                    for t in range(TT):
                        last = mm(bank[:, T * t:T * t + T], qiT[half(j), j // 2, P * t:P * t + P], kiT[half(j), :],
                                  start=True, stop=True)
                elif kind == "uv":
                    for a in range(2):
                        last = mm(bank[64 * a:64 * a + 64, 0:T], wuv[:, 2 * args[0] + a, :],
                                  olatT[:, 2 * args[0] + a, :], start=True, stop=True)
                elif kind == "cb":
                    for t in range(TT):
                        for n in range(N_CMP):
                            o = 255 + P * t - 16 * n - 31
                            last = mm(bank[:, 16 * (N_CMP * t + n):16 * (N_CMP * t + n) + 16], ohot[:, 2, o:o + P],
                                      tab[:], start=True, stop=True)
                elif kind == "hidden":
                    br, g, cs = args
                    rows = slice(64 * g, 64 * g + 64)
                    for j in range(32):
                        wt = weights(cs[j // 16]) if j % 16 == 0 else wt
                        last = mm(bank[0:N_CMP, 0:P], windows[rows, br, j, :], wt[rows, j % 16, :], start=(j == 0),
                                  stop=(j == 31))
                elif kind == "gtr":
                    for g in range(4):
                        last = nc.tensor.transpose(bank[:, 32 * g:32 * g + N_CMP], gelu_tok[0:N_CMP, g // 2, g % 2, :],
                                                   eye[0:N_CMP, 0:N_CMP])
                elif kind == "kc":
                    for g in range(2):
                        for b in range(2):
                            last = mm(bank[64 * b:64 * b + 64, 32 * g:32 * g + 32], w2kv[:, 0, :], geluT[:, 0, g, :],
                                      start=True, stop=True)
                elif kind == "vc":
                    for g in range(2):
                        for b in range(4):
                            last = mm(bank[32 * b:32 * b + 32, 64 * g:64 * g + 64], geluT[:, 1, g, :], w2kv[:, 1, :],
                                      start=True, stop=True)
                last.then_inc(proj_ready, 1)

            def run(stage):
                for u in range(*span(stage)):
                    emit(u)

            def add(stage, kt=KT):
                for a in range(*add_span(stage)):
                    _, c, kt, j = adds[a]
                    bank = F[a % 4]
                    if a >= 4:
                        pe.wait_ge(res_added, a - 3)
                    wt = weights(c)
                    for t in range(TT):
                        for k in range(kt):
                            last = mm(bank[:, COLS * t:COLS * t + COLS], yT[:, k, P * t:P * t + P], wt[:, k, :],
                                      start=(k == 0), stop=(k == kt - 1))
                    last.then_inc(res_ready, 1)

            def logits(m):
                mp, bank = maps[m], F[m % 2]
                if m >= 2:
                    pe.wait_ge(scored, m - 1)
                for t in range(TT):
                    n = len(mp["qk"]) + (TT if "fox" in mp else 0)
                    for i, (q, k) in enumerate(mp["qk"]):
                        last = mm(bank[:, T * t:T * t + T], q[:, P * t:P * t + P], k, start=(i == 0), stop=(i == n - 1))
                    if "fox" in mp:
                        for st in range(TT):
                            g = nlogf[:, st, mp["fox"]:mp["fox"] + 1].broadcast_to([P, P])
                            last = mm(bank[:, T * t:T * t + T], g, tri[:, st, :], start=False, stop=(st == TT - 1))
                last.then_inc(logits_ready, 1)

            def transpose_probs(m):
                pe.wait_ge(probs_ready, m + 1)
                if m >= 2:
                    pe.wait_ge(pt_saved, m - 1)
                for k in range(TT):
                    for t in range(TT):
                        last = nc.tensor.transpose(F[2 + m % 2][:, T * k + P * t:T * k + P * t + P],
                                                   S[:, m % NS, t, P * k:P * k + P], eye)
                last.then_inc(pt_ready, 1)

            def values(m):
                mp = maps[m]
                g = mp["group"]
                bank = B[g % 2]
                if mp["new"] and g >= 2:
                    pe.wait_ge(o_saved, g - 1)
                base, width = mp["base"], mp["v"].shape[2]
                first = mp["first"]
                if mp.get("compressed") is not None:
                    j = mp["compressed"]
                    rows = slice(32 * (j // 2 % 4), 32 * (j // 2 % 4) + N_CMP)
                    mm(bank[base:base + 64, 0:T], vc4[rows, j // 8, :], pcT[rows, j % 2, j // 8, :], start=True,
                       stop=False)
                    first = False
                pe.wait_ge(pt_saved, m + 1)
                for piece in range(0, width, P):
                    w = min(P, width - piece)
                    for k in range(TT):
                        last = mm(bank[base:base + w, 2 * piece:2 * piece + T], mp["v"][:, k, piece:piece + w],
                                  PT[:, m % 2, k, :], start=(first and k == 0), stop=(mp["last"] and k == TT - 1))
                last.then_inc(pv_done, 1)

            def attend(stage):
                m0, m1, _, _ = map_span[stage]
                for i in range(m0, m1 + 3):
                    if i < m1:
                        logits(i)
                    if m0 <= i - 2 < m1:
                        transpose_probs(i - 2)
                    if m0 <= i - 3:
                        values(i - 3)
                pe.wait_ge(o_saved, groups_end(stage))

            def hgrn():
                pend = []

                def level_values():
                    j, lv, hp = pend.pop(0)
                    pe.wait_ge(hg_masked, j + 1)
                    for n in range(4):
                        head = n if lv == 0 else 2 * hp + n // 2
                        i = 1 if lv == 0 else n % 2
                        s = 0 if lv == 0 else i
                        last = mm(B[head // 2][:, T * (head % 2) + P * i:T * (head % 2) + P * i + P],
                                  hi[:, s, P * head:P * head + P], SM[:, j % 3, P * n:P * n + P],
                                  start=(lv == 0 and n % 2 == 0), stop=(lv == len(LEVELS)), skip_group_check=True)
                    last.then_inc(hg_pv, 1)

                j = 0
                for lv in range(len(LEVELS) + 1):
                    if lv < len(LEVELS):
                        pe.wait_ge(hg_w, lv + 1)
                    key = Wlv[:, lv % 2] if lv < len(LEVELS) else hkT
                    query = Wlv[:, lv % 2] if lv < len(LEVELS) else hqT
                    for hp in range(1 if lv == 0 else 2):
                        if j >= 4:
                            pe.wait_ge(hg_masked, j - 3)
                        for n in range(4):
                            if lv == 0:
                                a, b = key[:, n, 0:P], query[:, n, P:T]
                            else:
                                head, i = 2 * hp + n // 2, n % 2
                                a, b = key[:, head, P * i:P * i + P], query[:, head, P * i:P * i + P]
                            last = mm(F[j % 4][:, P * n:P * n + P], a, b, start=True, stop=True)
                        last.then_inc(hg_scores, 1)
                        pend.append((j, lv, hp))
                        if len(pend) > 1:
                            level_values()
                        j += 1
                level_values()

            def expert_steps(name):
                first, steps, before = phases[name]

                pe.wait_ge(tokens_lo, 2)

                def gate_up(i, par, more):
                    for f in range(2):
                        n = 2 * (before + par) + f
                        pe.wait_ge(hid_ready, i * 4 + (n + 1))
                        for part in range(2):
                            hi, lo = parts(first, par, part)
                            if f == 0:
                                pe.wait_ge(dense_lo, i * 4 + (2 * par + part + 1))
                            for k in range(KT):
                                cols = slice(P * f, P * f + P)
                                last = product(F[n % 4][:, T * part:T * part + T], hi[:, k, cols], lo[:, k, cols],
                                               x_hi[:, k, :], x_lo[:, k, :], k == 0, k == KT - 1)
                        last.then_inc(gu_ready, 1)

                def down(i, par):
                    s = before + par
                    pe.wait_ge(hid_ready, i * 4 + (2 * s + 2 + CREDIT))
                    hi, lo = parts(first, par, 2)
                    pe.wait_ge(dense_lo_down, i * 2 + (par + 1))
                    for j in range(4):
                        t, c = j // 2, j % 2
                        pe.wait_ge(y_added, i * 8 + (4 * s + j + 1))
                        for f in range(2):
                            n, rows, cols = (2 * s + f) % 4, slice(P * t, P * t + P), slice(512 * c, 512 * c + 512)
                            last = product(B[j][:, :], hid_hi[:, n, rows], hid_lo[:, n, rows], hi[:, f, cols],
                                           lo[:, f, cols], f == 0, f == 1)
                        last.then_inc(y_ready, 1)

                per_step_pair(nc.tensor.Fori, steps, gate_up, down)
                pe.wait_ge(y_added, 4 * (before + steps) + CREDIT)

            def routed_round(name, q, rest):
                first, per, n_exp = phases[name]
                zs, ys = per + 4, per + 2

                def small_bank(z, odd):
                    if not isinstance(z, int) or z >= 2:
                        pe.wait_ge(q["z_saved"], z - 1)
                    return F[2 + odd]

                def base(e):
                    return e * zs + 2

                def gather(z, odd, slots):
                    pe.wait_ge(q["slots"], slots)
                    for a in range(2):
                        bank = small_bank(z + a, (a + odd) % 2)
                        for k in range(4):
                            for t in range(TT):
                                last = mm(bank[:, SLOTS * k:SLOTS * k + SLOTS], h[:, t, P * (4 * a + k):P * (4 * a + k) + P],
                                          pick[:, t, :], start=(t == 0), stop=(t == TT - 1))
                        last.then_inc(q["z_ready"], 1)

                def gate_up(e, s, par, between=None):
                    g = e * per + s
                    pe.wait_ge(q["hid"], g + 1)
                    for part, done in enumerate(("gate", "gu")):
                        hi, lo = parts(first, par, part)
                        pe.wait_ge(q["lo"], g * 2 + (part + 1))
                        for k in range(KT):
                            last = product(F[par][:, COLS * part:COLS * part + COLS], xgT_hi[:, k, :], xgT_lo[:, k, :],
                                           hi[:, k, :], lo[:, k, :], k == 0, k == KT - 1)
                        last.then_inc(q[done], 1)
                        if part == 0 and between is not None:
                            between()

                def turn(e, s, par, z=None):
                    bank = small_bank(base(e) + s if z is None else z, par)
                    pe.wait_ge(q["hid"], e * per + s + 3)
                    for f in range(2):
                        last = nc.tensor.transpose(bank[:, SLOTS * f:SLOTS * f + SLOTS],
                                                   hidden_tok[:, par, P * f:P * f + P], eye)
                    last.then_inc(q["z_ready"], 1)

                def down(e, s, par, z=None):
                    y = e * ys + s
                    hi, lo = parts(first, par, 2)
                    pe.wait_ge(q["lo_down"], e * per + s + 1)
                    pe.wait_ge(q["z_saved"], (base(e) + s if z is None else z) + 1)
                    pe.wait_ge(q["y_added"], y + 1)
                    for c in range(2):
                        cols = slice(512 * c, 512 * c + 512)
                        for f in range(2):
                            last = product(B[2 * par + c][:, :], hiddenT_hi[:, par, f, :], hiddenT_lo[:, par, f, :],
                                           hi[:, f, cols], lo[:, f, cols], f == 0, f == 1)
                    last.then_inc(q["y_ready"], 1)

                def scatter(e, saved_):
                    for t in range(TT):
                        y = e * ys + per + t
                        pe.wait_ge(q["z_saved"], saved_)
                        pe.wait_ge(q["y_added"], y + 1)
                        if t == 0:
                            pe.wait_ge(q["y_added"], y + 2)
                        for c in range(2):
                            last = mm(B[2 * t + c][:, :], gatedT[:, t, :], y_slots[:, 512 * c:512 * c + 512], start=True,
                                      stop=True)
                        last.then_inc(q["y_ready"], 1)

                def expert(e, more):
                    if per > 2:
                        with nc.tensor.Fori(0, per // 2 - 1) as b:
                            gate_up(e, b * 2 + 1, 1, between=lambda: turn(e, b * 2, 0))
                            down(e, b * 2, 0)
                            gate_up(e, b * 2 + 2, 0, between=lambda: turn(e, b * 2 + 1, 1))
                            down(e, b * 2 + 1, 1)
                    gate_up(e, per - 1, 1, between=lambda: turn(e, per - 2, 0))
                    z = base(e) + per - 1
                    if more:
                        gather(z, 1, e * 2 + 3)
                        z = z + 2
                    down(e, per - 2, 0)
                    turn(e, per - 1, 1, z)
                    pe.wait_ge(q["slots"], e * 2 + 2)
                    for t in range(TT):
                        bank = small_bank(z + 1 + t, t)
                        nc.tensor.transpose(bank[:, 0:P], gated[:, t, :], eye).then_inc(q["z_ready"], 1)
                    down(e, per - 1, 1, z)
                    if more:
                        pe.wait_ge(q["z_saved"], z)
                        gate_up(e + 1, 0, 0, between=lambda: scatter(e, z + 3))
                    else:
                        scatter(e, z + 3)

                gather(0, 0, 1)
                pe.wait_ge(q["z_saved"], 2)
                gate_up(0, 0, 0)
                with nc.tensor.Fori(0, n_exp - 1) as e:
                    expert(e, True)
                expert(n_exp - 1, False)
                pe.wait_ge(q["y_added"], n_exp * ys + 2)
                pe.wait_ge(q["z_saved"], n_exp * zs)

            def routed_layer(name, n):
                routed_round(name, rounds[name][0], False)
                full = nc.tensor.value_load(crowded[P - 1:P, n:n + 1], min_val=0, max_val=1)
                with nc.tensor.If(full > 0):
                    routed_round(name, rounds[name][1], True)

            pe.wait_ge(consts_in, 16)
            pe.wait_ge(mem_in, 16)
            run("mem1 transposed")
            pe.wait_ge(proj_saved, saved("mem1 transposed"))
            run("mem1 keys")
            run("mem1 values")
            pe.wait_ge(table_in, 32)
            pe.wait_ge(set_up, 1)
            run("bias rows")
            run("ln0 transposed")
            pe.wait_ge(proj_saved, saved("ln0 transposed"))
            pe.wait_ge(params_in, 16 * N_PARAMS)
            run("mix1")
            pe.wait_ge(logf_ready, 1)
            run("forget sums")
            pe.wait_ge(proj_saved, saved("forget sums"))
            attend("mix1")
            hgrn()
            pe.wait_ge(squares_ready, 2)
            run("mean squares")
            pe.wait_ge(y_normed, 2)
            add("out1")
            run("ln1 transposed")
            pe.wait_ge(proj_saved, saved("ln1 transposed"))
            run("mem1 queries")
            pe.wait_ge(proj_saved, saved("mem1 queries"))
            attend("mem1")
            add("mem1 out")
            run("ln2 transposed")
            pe.wait_ge(proj_saved, saved("ln2 transposed"))
            run("router1")
            pe.wait_ge(chosen_ready, 1)
            run("count1")
            pe.wait_ge(counted, 1)
            routed_layer("moe1", 0)
            pe.wait_ge(mem2_in, 16)
            run("mem2 transposed")
            pe.wait_ge(proj_saved, saved("mem2 transposed"))
            for i in range(2):
                run(f"xa{i} keys")
                run(f"xa{i} values")
                pe.wait_ge(rows_back, 32 + 16 * i)
                run(f"bias tiles {i}")
                run(f"ln{3 * i + 3} transposed")
                pe.wait_ge(proj_saved, saved(f"ln{3 * i + 3} transposed"))
                if i == 0:
                    run("mix2")
                    pe.wait_ge(proj_saved, saved("mix2"))
                    run("indexer")
                    run("mix2b")
                    pe.wait_ge(proj_saved, saved("mix2b"))
                    run("latent queries")
                    pe.wait_ge(latents_ready, 1)
                    run("latent keys")
                    pe.wait_ge(proj_saved, saved("latent keys"))
                    attend("mix2")
                    run("latent out")
                    pe.wait_ge(proj_saved, saved("latent out"))
                    add("out2")
                else:
                    run("mix3")
                    run("compressed bias")
                    pe.wait_ge(proj_saved, saved("mix3"))
                    pe.wait_ge(windows_ready, 1)
                    run("compress hidden")
                    pe.wait_ge(proj_saved, saved("compress hidden"))
                    run("compress turned")
                    pe.wait_ge(proj_saved, saved("compress turned"))
                    run("compress out")
                    pe.wait_ge(proj_saved, saved("compress out"))
                    for par in range(2):
                        a = add_span("compressed logits")[0] + par
                        pe.wait_ge(res_added, a - 3)
                        for t in range(TT):
                            for jj in range(8):
                                j = 2 * jj + par
                                o = 256 * t + 32 * jj
                                last = mm(F[a % 4][:, o:o + N_CMP], qcT[half(j), j // 2, P * t:P * t + P],
                                          kcT[half(j), j // 8, 0:N_CMP], start=True, stop=True)
                        last.then_inc(res_ready, 1)
                    pe.wait_ge(cmp_ready, 1)
                    run("compressed probs")
                    pe.wait_ge(proj_saved, saved("compressed probs"))
                    attend("mix3")
                    add("out3")
                run(f"ln{3 * i + 4} transposed")
                pe.wait_ge(proj_saved, saved(f"ln{3 * i + 4} transposed"))
                run(f"xa{i} queries")
                pe.wait_ge(proj_saved, saved(f"xa{i} queries"))
                attend(f"xa{i}")
                add(f"xa{i} out")
                run(f"ln{3 * i + 5} transposed")
                pe.wait_ge(proj_saved, saved(f"ln{3 * i + 5} transposed"))
                if i == 1:
                    run("router2")
                    pe.wait_ge(chosen_ready, 2)
                    run("count2")
                    pe.wait_ge(counted, 2)
                    routed_layer("moe2", 1)
                else:
                    expert_steps("dense")

        @block.scalar
        def _(act):
            step = Tally(act, act_step)
            asked = [0]
            ap_ = nc.scalar.activation

            def request():
                asked[0] += 1
                act.wait_ge(to_act, asked[0])

            def answer(ins):
                ins.then_inc(from_act, 1)

            def root():
                request()
                answer(ap_(std, veps, ACT.Sqrt))

            def save(stage):
                for u in range(*span(stage)):
                    _, kind, args, dest, func, scale = units[u]
                    bank = B[2 + u % 2]
                    act.wait_ge(proj_ready, u + 1)
                    if kind == "tr" and args[2] is not None:
                        for j in range(2):
                            col = slice(args[1] + j, args[1] + j + 1)
                            ins = ap_(dest[:, j, :], bank[:, T * j:T * j + T], ACT.Identity,
                                      bias=bias_T[:, args[2], col], scale=gain_T[:, args[2], col])
                    elif kind in ("T", "tr", "pctr", "uk"):
                        ins = ap_(dest, pair(bank), func, scale=scale)
                    elif kind == "tok":
                        ins = ap_(dest, pair(bank, args[5]), func, scale=scale)
                    elif kind == "dup":
                        ins = ap_(dest, pair(bank) if args[5] == 2 else bank[:, 0:T], func, scale=scale)
                    elif kind in ("ctr", "uv"):
                        ins = ap_(dest, bank[:, 0:T], func)
                    elif kind == "idx":
                        if args[0] >= 2:
                            act.wait_ge(idx_used, args[0] - 1)
                        ins = ap_(dest, pair(bank), func, scale=scale)
                    elif kind == "row":
                        ins = ap_(dest, bank[0:16, :], func)
                    elif kind == "flip":
                        ins = ap_(dest, bank[:, 0:BIAS_W], func)
                    elif kind == "cum":
                        ins = ap_(dest, pair(bank, args[1]), func, scale=scale)
                    elif kind == "sumsq":
                        step.did(ap_(dest, pair(bank), ACT.Ln, bias=eps, scale=args[2]))
                        step.wait()
                        ins = ap_(dest, dest, ACT.Exp, scale=-0.5)
                    elif kind == "cb":
                        for par in range(2):
                            for t in range(TT):
                                src = bank[:, 240 * t:240 * t + 240].rearrange("p (n j r) -> p r j n", r=2, j=8)[:, par]
                                ins = ap_(bcmp[:, par, t, :, 0:N_CMP], src, func)
                    elif kind == "hidden":
                        ins = ap_(dest, bank[0:N_CMP, 0:P], func)
                    elif kind == "gtr":
                        ins = ap_(dest, bank[:, 0:P].rearrange("p (a b c) -> p a b c", a=2, b=2)[:, :, :, 0:N_CMP], func)
                    elif kind == "kc":
                        ins = ap_(dest, bank[:, 0:64].rearrange("p (a b) -> p a b", a=2), func)
                    elif kind == "vc":
                        ins = ap_(dest, bank[:, 0:128].rearrange("p (a b) -> p a b", a=2), func)
                    ins.then_inc(proj_saved, 1)

            def exps(m):
                mp, s = maps[m], m % NS
                act.wait_ge(max_ready, m + 1)
                if "sink" in mp:
                    j = mp["sink"]
                    ap_(esink[:, s], nmx[:, s], ACT.Exp, bias=sinks[:, j:j + 1])
                for t in range(TT):
                    ins = ap_(S[:, s, t], S[:, s, t], ACT.Exp, bias=nmx[:, s, t:t + 1], accum_out=ssum[:, s, t:t + 1])
                ins.then_inc(exp_ready, 1)

            def save_probs(m):
                act.wait_ge(pt_ready, m + 1)
                if m >= 2:
                    act.wait_ge(pv_done, m - 1)
                ap_(PT[:, m % 2], pair(F[2 + m % 2]), ACT.Copy).then_inc(pt_saved, 1)

            def save_group(g):
                last, dest = groups[g]
                act.wait_ge(pv_done, last + 1)
                bank = B[g % 2]
                src = pair(bank) if len(dest.shape) == 3 else bank[:, 0:T]
                ap_(dest, src, ACT.Copy).then_inc(o_saved, 1)

            def attend(stage):
                m0, m1, _, _ = map_span[stage]
                for i in range(m0, m1 + 3):
                    if i < m1:
                        exps(i)
                    if m0 <= i - 2 < m1:
                        save_probs(i - 2)
                    if m0 <= i - 3 and maps[i - 3]["end"]:
                        save_group(maps[i - 3]["group"])

            def expert_steps(name):
                first, steps, before = phases[name]

                def one(i, par, more):
                    dense_high(i, par, 2)
                    for f in range(2):
                        n = 2 * (before + par) + f
                        act.wait_ge(gu_ready, i * 4 + (n + 1))
                        act.wait_ge(hid_ready, i * 4 + (n - 1 + CREDIT))
                        ap_(sg[:, n % 2], F[n % 4][:, 0:T], ACT.Silu).then_inc(sg_ready, 1)
                        if more:
                            dense_high(i + par, 1 - par, f)
                act.wait_ge(proj_saved, saved("ln5 transposed"))
                for a in range(2):
                    cut = slice(4 * a, 4 * a + 4)
                    ap_(x_hi[:, cut].bitcast(R32), hT[:, cut], ACT.Copy).then_inc(tokens_hi, 1)
                with nc.scalar.Fori(0, steps // 2) as i:
                    one(i, 0, True)
                    one(i, 1, True)
                one(steps // 2, 0, False)

            def dense_high(i, par, part):
                c = phases["dense"][0] + 3 * par + part
                act.wait_ge(w_in[c % RING], i * 16 + ready_at[c])
                ap_(w_hi[c % RING].bitcast(R32), ring[:, c % RING], ACT.Copy)\
                    .then_inc(dense_hi if part < 2 else dense_hi_down, 1)

            def routed_round(name, q, rest):
                first, per, n_exp = phases[name]
                zs = per + 4

                def high(e, s, par, b, part):
                    c = first + 3 * par + part
                    use = e * (per // 2) + b
                    if rest:
                        act.wait_ge(q["w_in"][c % RING], use * 16 + 16)
                    else:
                        act.wait_ge(w_in[c % RING], use * 16 + ready_at[c])
                    ap_(w_hi[c % RING].bitcast(R32), ring[:, c % RING], ACT.Copy)\
                        .then_inc(q["hi" if part < 2 else "hi_down"], 1)

                def save_small(z, odd, dest, src):
                    act.wait_ge(q["z_ready"], z + 1)
                    ap_(dest.bitcast(R32), src(F[2 + odd]), ACT.Copy).then_inc(q["z_hi"], 1)

                def gathered(z, odd):
                    for a in range(2):
                        save_small(z + a, (a + odd) % 2, xgT_hi[:, 4 * a:4 * a + 4, :],
                                   lambda bank: bank[:, :].rearrange("p (k s) -> p k s", k=4))

                def silu(e, s, par):
                    act.wait_ge(q["gu"], e * per + s + 1)
                    ap_(hidden_sg[:, par], F[par][:, 0:COLS], ACT.Silu).then_inc(q["sg"], 1)

                def turned(e, s, par, ahead=0):
                    save_small(e * zs + s + (2 + ahead), par, hiddenT_hi[:, par], lambda bank: pair(bank, SLOTS))

                def step(e, s, par, b, following):
                    silu(e, s - 1, 1 - par)
                    if following is not None:
                        high(*following, 0)
                    turned(e, s - 1, 1 - par)
                    if following is not None:
                        high(*following, 1)
                    high(e, s, par, b, 2)

                def expert(e, more):
                    for part in range(2):
                        high(e, 1, 1, 0, part)
                    high(e, 0, 0, 0, 2)
                    if per > 2:
                        with nc.scalar.Fori(0, per // 2 - 1) as b:
                            step(e, b * 2 + 1, 1, b, (e, b * 2 + 2, 0, b + 1))
                            step(e, b * 2 + 2, 0, b + 1, (e, b * 2 + 3, 1, b + 1))
                    step(e, per - 1, 1, per // 2 - 1, (e + 1, 0, 0, 0) if more else None)
                    silu(e, per - 1, 1)
                    if more:
                        gathered(e * zs + (per + 1), 1)
                    turned(e, per - 1, 1, 2 if more else 0)

                for part in range(2):
                    high(0, 0, 0, 0, part)
                gathered(0, 0)
                with nc.scalar.Fori(0, n_exp - 1) as e:
                    expert(e, True)
                expert(n_exp - 1, False)

            def routed_layer(name, n):
                routed_round(name, rounds[name][0], False)
                full = nc.scalar.value_load(crowded[P - 1:P, n:n + 1], min_val=0, max_val=1)
                with nc.scalar.If(full > 0):
                    routed_round(name, rounds[name][1], True)

            save("mem1 transposed")
            root()
            save("mem1 keys")
            save("mem1 values")
            save("bias rows")
            act.wait_ge(params_in, 16 * N_PARAMS)
            save("ln0 transposed")
            request()
            answer(ap_(lame, lams, ACT.Exp))
            save("mix1")
            request()
            step.did(ap_(ffe, ffa, ACT.Exp, scale=-1.0))
            step.wait()
            answer(ap_(ffe, ffe, ACT.Ln, bias=1.0))
            request()
            step.did(ap_(hkT, bcT, ACT.Exp, scale=-1.0))
            step.wait()
            step.did(ap_(bcT, hkT, ACT.Ln, bias=1.0))
            step.wait()
            answer(ap_(hkT, hfT, ACT.Sigmoid, scale=-1.0))
            save("forget sums")
            act.wait_ge(rows_out, 16)
            attend("mix1")
            for lv in range(len(LEVELS)):
                act.wait_ge(hg_arg, lv + 1)
                ap_(decay[:, lv % 2], decay[:, lv % 2], ACT.Exp).then_inc(hg_exp, 1)
            act.wait_ge(hg_pv, 2 * len(LEVELS) + 1)
            for a in range(2):
                ins = ap_(oT[:, 2 * a:2 * a + 2, :], pair(B[a]), ACT.Copy)
            answer(ins)
            save("mean squares")
            root()
            save("ln1 transposed")
            save("mem1 queries")
            attend("mem1")
            root()
            save("ln2 transposed")
            save("router1")
            save("count1")
            act.wait_ge(counted, 1)
            routed_layer("moe1", 0)
            root()
            save("mem2 transposed")
            for i in range(2):
                if i == 1:
                    root()
                save(f"xa{i} keys")
                save(f"xa{i} values")
                save(f"bias tiles {i}")
                save(f"ln{3 * i + 3} transposed")
                if i == 0:
                    save("mix2")
                    request()
                    answer(ap_(cstd, css, ACT.Sqrt))
                    save("indexer")
                    save("mix2b")
                    save("latent queries")
                    save("latent keys")
                    attend("mix2")
                    save("latent out")
                else:
                    save("mix3")
                    save("compressed bias")
                    act.wait_ge(windows_ready, 1)
                    save("compress hidden")
                    save("compress turned")
                    save("compress out")
                    request()
                    pc = Pc.rearrange("p r t j n -> p (r t j) n")[:, :, 0:N_CMP]
                    answer(ap_(pc, pc, ACT.Exp))
                    save("compressed probs")
                    attend("mix3")
                root()
                save(f"ln{3 * i + 4} transposed")
                save(f"xa{i} queries")
                attend(f"xa{i}")
                if i == 0:
                    for part in range(2):
                        dense_high(0, 0, part)
                root()
                save(f"ln{3 * i + 5} transposed")
                if i == 1:
                    save("router2")
                    request()
                    e = route[:, 16:32]
                    answer(ap_(e, e, ACT.Exp))
                    save("count2")
                    act.wait_ge(counted, 2)
                    routed_layer("moe2", 1)
                else:
                    expert_steps("dense")
            root()

        @block.vector
        def _(dve):
            V = nc.vector
            step = Tally(dve, dve_step)
            answered = [0]

            def ask(ins):
                ins.then_inc(to_act, 1)
                answered[0] += 1

            def answer():
                dve.wait_ge(from_act, answered[0])

            def do(ins):
                step.did(ins)
                step.wait()

            norms = [0]

            def sums(src, j):
                for t in range(TT):
                    ins = V.bn_stats(stats[:, t, j, :], src[:, t, COLS * j:COLS * j + COLS])
                return ins

            def layer_norm(src=None, counted=True, last=False):
                src = h if src is None else src
                n = norms[0]
                norms[0] += 1
                if not counted:
                    for j in range(D // COLS):
                        ins = sums(src, j)
                    do(ins)
                for t in range(TT):
                    ins = V.bn_aggr(mvar[:, t, :], stats[:, t].rearrange("p a b -> p (a b)"))
                do(ins)
                ask(V.tensor_scalar(veps, mvar[:, :, 1], EPS, None, ALU.add))
                answer()
                do(V.reciprocal(rstd, std))
                for a in range(2):
                    cut = slice(512 * a, 512 * a + 512)
                    for t in range(TT):
                        ins = V.tensor_scalar(h[:, t, cut], src[:, t, cut], mvar[:, t, 0:1], rstd[:, t:t + 1],
                                              ALU.subtract, ALU.mult)
                    ins.then_inc(normed_half, 1)
                dve.wait_ge(gb_in, 32 * (n + 1))
                dve.wait_ge(normed_half, 2 * n + 2)
                if not last:
                    dve.wait_ge(proj_saved, saved(f"ln{n} transposed"))
                if n == 5:
                    tokens_low()
                for t in range(TT):
                    ins = V.tensor_tensor(h[:, t], h[:, t], gb[:, 0], ALU.mult)
                do(ins)
                for t in range(TT):
                    ins = V.tensor_tensor(h[:, t], h[:, t], gb[:, 1], ALU.add)
                ins.then_inc(ln_done, 1)
                dve.wait_ge(ln_done, n + 1)

            def add(stage, alpha):
                for a in range(*add_span(stage)):
                    j = adds[a][3]
                    hs = h[:, :, COLS * j:COLS * j + COLS]
                    dve.wait_ge(res_ready, a + 1)
                    V.scalar_tensor_tensor(out=hs, in0=hs, scalar=alpha, in1=pair(F[a % 4]), op0=ALU.mult,
                                           op1=ALU.add).then_inc(res_added, 1)
                    dve.wait_ge(res_added, a + 1)
                    ins = sums(h, j)
                do(ins)

            def score_map(m):
                mp, s = maps[m], m % NS
                bank = pair(F[m % 2])
                dve.wait_ge(logits_ready, m + 1)
                if m >= NS:
                    dve.wait_ge(pt_ready, m - NS + 1)
                if "fox" in mp:
                    j = mp["fox"]
                    for t in range(TT):
                        ins = V.scalar_tensor_tensor(out=S[:, s, t], in0=bank[:, t], scalar=cumq[:, t, j:j + 1],
                                                     in1=mp["mask"][:, t], op0=ALU.add, op1=ALU.add)
                elif "mask" in mp:
                    ins = V.tensor_tensor(S[:, s], bank, mp["mask"], ALU.add)
                else:
                    ins = V.tensor_copy(S[:, s], bank)
                ins.then_inc(scored, 1)
                dve.wait_ge(scored, m + 1)
                if "extra" in mp:
                    do(V.tensor_tensor(S[:, s], S[:, s], mp["extra"], ALU.add))
                ins = V.tensor_reduce(nmx[:, s], S[:, s], AX.X, ALU.max, negate=True)
                if "sink" in mp:
                    do(ins)
                    j = mp["sink"]
                    ins = V.tensor_scalar(nmx[:, s], nmx[:, s], nsinks[:, j:j + 1], None, ALU.min)
                ins.then_inc(max_ready, 1)

            def normalise(m):
                mp, s = maps[m], m % NS
                dve.wait_ge(exp_ready, m + 1)
                if "sink" in mp:
                    do(V.tensor_tensor(ssum[:, s], ssum[:, s], esink[:, s], ALU.add))
                do(V.reciprocal(rsum[:, s], ssum[:, s]))
                if mp.get("coef") is not None:
                    do(V.tensor_tensor(rsum[:, s], rsum[:, s], mp["coef"], ALU.mult))
                for t in range(TT):
                    ins = V.tensor_scalar(S[:, s, t], S[:, s, t], rsum[:, s, t:t + 1], None, ALU.mult)
                ins.then_inc(probs_ready, 1)

            def attend(stage):
                m0, m1, _, _ = map_span[stage]
                for i in range(m0, m1 + 1):
                    if i < m1:
                        score_map(i)
                    if m0 <= i - 1:
                        normalise(i - 1)

            def chosen(src, groups_, n, k, lower, rank, sel):
                shape = [P, groups_, n, n]
                gt = route[:, 400:400 + groups_ * n * n].rearrange("p (g j i) -> p g j i", j=n, i=n)
                ge = route[:, 600:600 + groups_ * n * n].rearrange("p (g j i) -> p g j i", j=n, i=n)
                low = lower.rearrange("p (j i) -> p j i", j=n)
                other = src.unsqueeze(2).broadcast_to(shape)
                own = src.unsqueeze(3).broadcast_to(shape)
                V.tensor_tensor(gt, other, own, ALU.is_gt)
                do(V.tensor_tensor(ge, other, own, ALU.is_ge))
                for g in range(groups_):
                    ins = V.tensor_tensor(ge[:, g], ge[:, g], low, ALU.mult)
                do(ins)
                do(V.tensor_tensor(gt, gt, ge, ALU.max))
                do(V.tensor_reduce(rank, gt, AX.X, ALU.add))
                do(V.tensor_scalar(sel, rank, k - 0.5, None, ALU.is_lt))

            def place(sel, gates, n_exp, n):
                gate = route_gate[:, :, 0:n_exp]
                V.tensor_copy(gate, sel).then_inc(chosen_ready, 1)
                V.memset(route_slot, -1.0)
                V.memset(route_gate[:, :, n_exp:n_exp + 1], 0.0)
                dve.wait_ge(proj_saved, saved(f"count{n}"))
                count = route_count[:, :, 0:n_exp]
                slot = route_slot[:, :, 0:n_exp]
                top = route[:, 380:381]
                do(V.tensor_reduce(top, count[:, 1], AX.X, ALU.max))
                do(V.tensor_tensor(slot, count, sel, ALU.mult))
                do(V.tensor_scalar(slot, slot, -1.0, None, ALU.add))
                do(V.tensor_copy(gate, gates))
                V.tensor_scalar(crowded[:, n - 1:n], top, CROWD + 0.5, None, ALU.is_gt).then_inc(counted, 1)
                dve.wait_ge(counted, n)

            def route1():
                r_ = Slots(route, TT * E1)
                sc = route[:, 0:32].rearrange("p (a b) -> p a b", a=TT)
                biased, sel, gates, rank = (r_.get(32) for _ in range(4))
                gs, grank, gsel, tot = r_.get(8), r_.get(8), r_.get(8), r_.get(2)
                dve.wait_ge(proj_saved, saved("router1"))
                v3 = lambda x: x.rearrange("p (a b) -> p a b", a=TT)
                v8 = lambda x: x.rearrange("p (g n) -> p g n", n=4)
                do(V.tensor_tensor(v3(biased), sc, rb1.unsqueeze(1).broadcast_to([P, TT, E1]), ALU.add))
                chosen(v8(biased), 8, 4, 2, const("lower4"), v8(rank), v8(sel))
                do(V.tensor_tensor(gates, biased, sel, ALU.mult))
                do(V.tensor_reduce(gs, v8(gates), AX.X, ALU.add))
                g2 = lambda x: x.rearrange("p (a b) -> p a b", a=TT)
                chosen(g2(gs), 2, 4, 1, const("lower4"), g2(grank), g2(gsel))
                do(V.tensor_tensor(v8(sel), v8(sel), gsel.unsqueeze(2).broadcast_to([P, 8, 4]), ALU.mult))
                do(V.tensor_tensor(gates, route[:, 0:32], sel, ALU.mult))
                do(V.tensor_reduce(tot, v3(gates), AX.X, ALU.add))
                do(V.reciprocal(tot, tot))
                do(V.tensor_tensor(v3(gates), v3(gates), tot.unsqueeze(2).broadcast_to([P, TT, E1]), ALU.mult))
                place(v3(sel), v3(gates), E1, 1)

            def route2():
                lg = route[:, 0:16]
                e = route[:, 16:32]
                r_ = Slots(route, 32)
                sel, rank, mx, tot = r_.get(16), r_.get(16), r_.get(2), r_.get(2)
                v3 = lambda x: x.rearrange("p (a b) -> p a b", a=TT)
                dve.wait_ge(proj_saved, saved("router2"))
                chosen(v3(lg), 2, 8, 2, const("lower8"), v3(rank), v3(sel))
                do(V.tensor_reduce(mx, v3(lg), AX.X, ALU.max))
                ask(V.tensor_tensor(v3(e), v3(lg), mx.unsqueeze(2).broadcast_to([P, TT, E2]), ALU.subtract))
                answer()
                do(V.tensor_tensor(e, e, sel, ALU.mult))
                do(V.tensor_reduce(tot, v3(e), AX.X, ALU.add))
                do(V.reciprocal(tot, tot))
                do(V.tensor_tensor(v3(e), v3(e), tot.unsqueeze(2).broadcast_to([P, TT, E2]), ALU.mult))
                place(v3(sel), v3(e), E2, 2)

            def dense_low(i, par, part):
                slot = (phases["dense"][0] + 3 * par + part) % RING
                dve.wait_ge(dense_hi, i * 4 + (2 * par + part + 1))
                V.tensor_tensor(ring_r[:, slot].bitcast(R32), ring[:, slot], w_hi[slot], ALU.subtract)\
                    .then_inc(dense_lo, 1)

            def tokens_low():
                for a in range(2):
                    cut = slice(4 * a, 4 * a + 4)
                    dve.wait_ge(tokens_hi, a + 1)
                    V.tensor_tensor(x_lo[:, cut].bitcast(R32), hT[:, cut], x_hi[:, cut], ALU.subtract)\
                        .then_inc(tokens_lo, 1)

            def expert_steps(name, alpha):
                first, steps, before = phases[name]
                do(V.tensor_scalar(h[:], h[:], alpha, None, ALU.mult))

                def hidden(i, par, more):
                    for f in range(2):
                        n = 2 * (before + par) + f
                        dve.wait_ge(sg_ready, i * 4 + (n + 1))
                        V.tensor_tensor(hid_all[:, n % 2], sg[:, n % 2], F[n % 4][:, T:2 * T], ALU.mult)\
                            .then_inc(hid_parted, 1)
                        dve.wait_ge(hid_parted, i * 8 + (2 * n + 1))
                        V.tensor_copy(hid_hi[:, n % 4].bitcast(R32), hid_all[:, n % 2]).then_inc(hid_parted, 1)
                        dve.wait_ge(hid_parted, i * 8 + (2 * n + 2))
                        V.tensor_tensor(hid_lo[:, n % 4].bitcast(R32), hid_all[:, n % 2], hid_hi[:, n % 4], ALU.subtract)\
                            .then_inc(hid_ready, 1)
                        if more:
                            dense_low(i + par, 1 - par, f)

                def gather(i, par):
                    s = before + par
                    for j in range(4):
                        t, c = j // 2, j % 2
                        dve.wait_ge(y_ready, i * 8 + (4 * s + j + 1))
                        dve.wait_ge(y_added, i * 8 + (4 * s + j + 1))
                        hs = h[:, t, 512 * c:512 * c + 512]
                        V.scalar_tensor_tensor(out=hs, in0=B[j][:, :], scalar=1.0, in1=hs, op0=ALU.mult,
                                               op1=ALU.add).then_inc(y_added, 1)

                per_step_pair(nc.vector.Fori, steps, hidden, gather)
                dve.wait_ge(y_added, 4 * (before + steps) + CREDIT)

            def routed_round(name, q, rest):
                first, per, n_exp = phases[name]
                ys = per + 2
                iota = const("iota")

                def make_pick(e):
                    for t in range(TT):
                        ins = V.tensor_scalar(pick[:, t], iota, route_slot[:, t, bass.ds(e, 1)], None, ALU.is_equal)
                    ins.then_inc(q["slots"], 1)

                def make_gated(e):
                    for t in range(TT):
                        ins = V.tensor_scalar(gated[:, t], iota, route_slot[:, t, bass.ds(e, 1)],
                                              route_gate[:, t, bass.ds(e, 1)], ALU.is_equal, ALU.mult)
                    ins.then_inc(q["slots"], 1)

                def hidden(e, s, par):
                    dve.wait_ge(q["sg"], e * per + s + 1)
                    V.tensor_tensor(hidden_tok[:, par], hidden_sg[:, par], F[par][:, COLS:2 * COLS], ALU.mult)\
                        .then_inc(q["hid"], 1)

                def gather_y(e, s, par, first_=False):
                    y = e * ys + s
                    dve.wait_ge(q["y_ready"], y + 1)
                    dve.wait_ge(q["y_added"], y + 2)
                    for c in range(2):
                        part = y_slots[:, 512 * c:512 * c + 512]
                        if first_:
                            ins = V.tensor_copy(part, B[2 * par + c][:, :])
                        else:
                            ins = V.tensor_tensor(part, part, B[2 * par + c][:, :], ALU.add)
                    ins.then_inc(q["y_added"], 1)

                def low(e, s, par, part):
                    slot = (first + 3 * par + part) % RING
                    dve.wait_ge(q["hi"], (e * per + s) * 2 + (part + 1))
                    V.tensor_tensor(ring_r[:, slot].bitcast(R32), ring[:, slot], w_hi[slot], ALU.subtract)\
                        .then_inc(q["lo"], 1)

                def low_small(zh, odd, dest, hi, src):
                    dve.wait_ge(q["z_hi"], zh + 1)
                    V.tensor_tensor(dest.bitcast(R32), src(F[2 + odd]), hi, ALU.subtract).then_inc(q["z_saved"], 1)

                def gathered(zh, odd):
                    for a in range(2):
                        cut = slice(4 * a, 4 * a + 4)
                        low_small(zh + a, (a + odd) % 2, xgT_lo[:, cut, :], xgT_hi[:, cut, :],
                                  lambda bank: bank[:, :].rearrange("p (k s) -> p k s", k=4))

                def turned(e, s, par, ahead=0):
                    low_small(e * (per + 2) + s + (2 + ahead), par, hiddenT_lo[:, par], hiddenT_hi[:, par],
                              lambda bank: pair(bank, SLOTS))

                def scattered(e):
                    for t in range(TT):
                        y = e * ys + per + t
                        dve.wait_ge(q["y_ready"], y + 1)
                        dve.wait_ge(q["y_added"], y + 2)
                        for c in range(2):
                            part = acc[:, t, 512 * c:512 * c + 512]
                            ins = V.tensor_tensor(part, part, B[2 * t + c][:, :], ALU.add)
                        ins.then_inc(q["y_added"], 1)

                def step(e, s, par, following, before):
                    hidden(e, s - 1, 1 - par)
                    if following is not None:
                        low(*following, 0)
                    turned(e, s - 1, 1 - par)
                    if following is not None:
                        low(*following, 1)
                    if before is not None:
                        gather_y(*before)

                def expert(e, more):
                    make_gated(e)
                    if more:
                        dve.wait_ge(q["z_ready"], e * (per + 4) + 2)
                        make_pick(e + 1)
                    if per > 2:
                        step(e, 1, 1, (e, 2, 0), None)
                        step(e, 2, 0, (e, 3, 1), (e, 0, 0, True))
                        with nc.vector.Fori(1, per // 2 - 1) as b:
                            step(e, b * 2 + 1, 1, (e, b * 2 + 2, 0), (e, b * 2 - 1, 1))
                            step(e, b * 2 + 2, 0, (e, b * 2 + 3, 1), (e, b * 2, 0))
                        step(e, per - 1, 1, (e + 1, 0, 0) if more else None, (e, per - 3, 1))
                    else:
                        step(e, 1, 1, (e + 1, 0, 0) if more else None, None)
                    hidden(e, per - 1, 1)
                    ahead = 2 if more else 0
                    if more:
                        gathered(e * (per + 2) + (per + 1), 1)
                    turned(e, per - 1, 1, ahead)
                    for t in range(TT):
                        dve.wait_ge(q["z_ready"], e * (per + 4) + (per + 3 + ahead + t))
                        V.tensor_copy(gatedT[:, t, :], F[2 + t][:, 0:P]).then_inc(q["z_saved"], 1)
                    gather_y(e, per - 2, 0, per == 2)
                    gather_y(e, per - 1, 1)
                    if more:
                        for part in range(2):
                            low(e + 1, 1, 1, part)
                    scattered(e)

                V.memset(pick, 0.0).then_inc(q["hid"], 2)
                V.memset(gated, 0.0).then_inc(q["y_added"], 1)
                V.tensor_scalar(route_slot, route_slot, -1.0 * SLOTS if rest else 0.0, None, ALU.add)\
                    .then_inc(q["y_added"], 1)
                dve.wait_ge(q["y_added"], 2)
                dve.wait_ge(q["hid"], 2)
                make_pick(0)
                for part in range(2):
                    low(0, 0, 0, part)
                gathered(0, 0)
                for part in range(2):
                    low(0, 1, 1, part)
                with nc.vector.Fori(0, n_exp - 1) as e:
                    expert(e, True)
                expert(n_exp - 1, False)
                dve.wait_ge(q["y_added"], n_exp * ys + 2)

            def routed_layer(name, n, alpha):
                do(V.tensor_scalar(acc, h, alpha, None, ALU.mult))
                routed_round(name, rounds[name][0], False)
                full = V.value_load(crowded[P - 1:P, n:n + 1], min_val=0, max_val=1)
                with V.If(full > 0):
                    routed_round(name, rounds[name][1], True)

            V.memset(ones[:], 1.0).then_inc(hid_ready, CREDIT)
            V.memset(eps, EPS).then_inc(y_added, CREDIT)
            dve.wait_ge(x_in, 16)
            layer_norm(counted=False)
            dve.wait_ge(params_in, 16 * N_PARAMS)
            for a in range(2):
                ins = V.tensor_tensor(lamp[:, a], lamv[:, 2 * a], lamv[:, 2 * a + 1], ALU.mult)
            do(ins)
            ask(V.tensor_reduce(lams, lamp, AX.X, ALU.add))
            answer()
            for a in range(2):
                ins = V.tensor_scalar(neglam[:, a:a + 1], lame[:, 1:2], lame[:, 0:1], -LAM_INIT, ALU.subtract, ALU.add)
            V.tensor_scalar(dng, dng, 1.0 - LAM_INIT, None, ALU.mult)
            do(V.tensor_scalar(nsinks, sinks, -1.0, None, ALU.mult))
            dve.wait_ge(proj_saved, saved("mix1"))
            do(V.tensor_tensor(ffx, ffx, foxb.unsqueeze(1).broadcast_to([P, TT, FOX_H]), ALU.add))
            flat = lambda x: x.rearrange("p a b -> p (a b)")
            ask(V.scalar_tensor_tensor(out=flat(ffa), in0=flat(ffx), scalar=-1.0, in1=flat(ffx), op0=ALU.mult,
                                       op1=ALU.max))
            ask(V.scalar_tensor_tensor(out=flat(bcT), in0=flat(hfT), scalar=-1.0, in1=flat(hfT), op0=ALU.mult,
                                       op1=ALU.max))
            answer()
            do(V.scalar_tensor_tensor(out=flat(ffx), in0=flat(ffx), scalar=0.0, in1=flat(ffe), op0=ALU.min,
                                      op1=ALU.subtract))
            V.tensor_scalar(nlogf, ffx, -1.0, None, ALU.mult).then_inc(logf_ready, 1)
            do(V.scalar_tensor_tensor(out=flat(bcT), in0=flat(hfT), scalar=0.0, in1=flat(bcT), op0=ALU.min,
                                      op1=ALU.subtract))
            for j in range(HGRN_H):
                ins = V.tensor_tensor_scan(hfT[:, j], ones[:], bcT[:, j], 0.0, ALU.mult, ALU.add)
            do(ins)
            dve.wait_ge(proj_saved, saved("forget sums"))
            attend("mix1")
            dve.wait_ge(o_saved, groups_end("mix1"))
            V.tensor_tensor(dsq, yT[:, 2:4], yT[:, 2:4], ALU.mult).then_inc(squares_ready, 1)

            def level_argument(lv):
                b = LEVELS[lv]
                cut = lambda x: x.rearrange("p h t -> p (h t)").rearrange("p (n a b) -> p n a b", a=2, b=b)
                src, dst = cut(hfT), cut(decay[:, lv % 2])
                ref = src[:, :, 0, b - 1:b].broadcast_to([P, HGRN_H * T // (2 * b), b])
                if lv >= 2:
                    dve.wait_ge(hg_w, lv - 1)
                V.tensor_tensor(dst[:, :, 0, :], ref, src[:, :, 0, :], ALU.subtract)
                V.tensor_tensor(dst[:, :, 1, :], src[:, :, 1, :], ref, ALU.subtract).then_inc(hg_arg, 1)

            j = 0
            level_argument(0)
            for lv in range(len(LEVELS) + 1):
                if lv + 1 < len(LEVELS):
                    level_argument(lv + 1)
                for hp in range(1 if lv == 0 else 2):
                    dve.wait_ge(hg_scores, j + 1)
                    if j >= 3:
                        dve.wait_ge(hg_pv, j - 2)
                    if lv == 0:
                        ins = V.tensor_copy(SM[:, j % 3], F[j % 4][:, :])
                    else:
                        ins = V.tensor_tensor(SM[:, j % 3].rearrange("p (a b) -> p a b", a=4),
                                              F[j % 4][:, :].rearrange("p (a b) -> p a b", a=4),
                                              levelmask[:, lv - 1:lv, :].broadcast_to([P, 4, P]), ALU.mult)
                    ins.then_inc(hg_masked, 1)
                    j += 1
            answered[0] += 1
            answer()
            V.tensor_tensor(sqT, oT, oT, ALU.mult).then_inc(squares_ready, 1)
            dve.wait_ge(proj_saved, saved("mean squares"))
            V.scalar_tensor_tensor(out=yT[:, 2:4], in0=yT[:, 2:4], scalar=dng[:, 0:1], in1=drs, op0=ALU.mult,
                                   op1=ALU.mult).then_inc(y_normed, 1)
            do(V.scalar_tensor_tensor(out=oT, in0=oT, scalar=hng[:, 0:1], in1=decay[:, 0], op0=ALU.mult, op1=ALU.mult))
            V.tensor_tensor(yT[:, 4:8], oT, hgT, ALU.mult).then_inc(y_normed, 1)
            add("out1", ALPHA1)
            layer_norm()
            attend("mem1")
            add("mem1 out", ALPHA1)
            layer_norm()
            route1()
            routed_layer("moe1", 0, ALPHA1)
            layer_norm(acc, counted=False)
            for i in range(2):
                if i == 0:
                    dve.wait_ge(proj_saved, saved("mix2"))
                    for t in range(TT):
                        do(V.tensor_tensor_reduce(out=work[:, t, 0:P], in0=ckv[:, t], in1=ckv[:, t], scale=1.0,
                                                  scalar=0.0, op0=ALU.mult, op1=ALU.add, accum_out=css[:, t:t + 1]))
                    ask(V.tensor_scalar(css, css, 1.0 / P, EPS, ALU.mult, ALU.add))
                    answer()
                    do(V.reciprocal(crstd, cstd))
                    for t in range(TT):
                        ins = V.scalar_tensor_tensor(out=ckv[:, t], in0=ckv[:, t], scalar=crstd[:, t:t + 1],
                                                     in1=ckvg, op0=ALU.mult, op1=ALU.mult)
                    ins.then_inc(latents_ready, 1)
                    for j in range(8):
                        dve.wait_ge(proj_saved, span("indexer")[0] + j + 1)
                        for t in range(TT):
                            ins = V.scalar_tensor_tensor(out=score[:, t], in0=idx_act[:, j % 2, t],
                                                         scalar=wi[:, t, j:j + 1],
                                                         in1=causal[:, t] if j == 0 else score[:, t],
                                                         op0=ALU.mult, op1=ALU.add)
                        ins.then_inc(idx_used, 1)
                        dve.wait_ge(idx_used, j + 1)
                    for rnd in range(TOPK // 8):
                        src = score if rnd == 0 else work
                        for t in range(TT):
                            ins = V.max(m8[:, t], src[:, t])
                        do(ins)
                        for t in range(TT):
                            ins = V.match_replace(work[:, t], m8[:, t], src[:, t], TAKEN)
                        do(ins)
                    do(V.tensor_scalar(work, work, TAKEN / 2, NEG, ALU.is_gt, ALU.mult))
                    attend("mix2")
                    add("out2", ALPHA2)
                else:
                    dve.wait_ge(proj_saved, saved("mix3"))
                    V.memset(Pc, 0.0)
                    V.memset(geluT, 0.0)
                    for br in range(2):
                        kv = kvcT[:, br]
                        tokens = bass.AP(tensor=kv.tensor, offset=kv.offset, ap=[list(kv.ap[0]), [1, 32], [16, N_CMP]])
                        ins = V.tensor_tensor(windows[:, br], tokens, peT[:, br].unsqueeze(2).broadcast_to([P, 32, N_CMP]),
                                              ALU.add)
                    ins.then_inc(windows_ready, 1)
                    dve.wait_ge(windows_ready, 1)
                    dve.wait_ge(proj_saved, saved("compressed bias"))
                    pc = Pc.rearrange("p r t j n -> p (r t j) n")
                    for par in range(2):
                        a = add_span("compressed logits")[0] + par
                        dve.wait_ge(res_ready, a + 1)
                        V.tensor_tensor(pc[:, 16 * par:16 * par + 16, 0:N_CMP],
                                        F[a % 4][:, :].rearrange("p (a n) -> p a n", n=32)[:, :, 0:N_CMP],
                                        bcmp[:, par].rearrange("p t j n -> p (t j) n")[:, :, 0:N_CMP],
                                        ALU.add).then_inc(res_added, 1)
                    dve.wait_ge(res_added, add_span("compressed logits")[1])
                    pn = pc[:, :, 0:N_CMP]
                    do(V.tensor_reduce(cmx, pn, AX.X, ALU.max, negate=True))
                    ask(V.tensor_tensor(pn, pn, cmx.unsqueeze(2).broadcast_to([P, 32, N_CMP]), ALU.add))
                    answer()
                    do(V.tensor_reduce(csum, pn, AX.X, ALU.add))
                    do(V.reciprocal(csum, csum))
                    for par in range(2):
                        c2 = csum[:, 16 * par:16 * par + 16].rearrange("p (t j) -> p t j", t=TT)
                        gate = g3[:].rearrange("p t (j r c) -> p r c t j", r=2, c=3)[:, par, 0]
                        ins = V.tensor_tensor(c2, c2, gate, ALU.mult)
                    do(ins)
                    do(V.tensor_tensor(pn, pn, csum.unsqueeze(2).broadcast_to([P, 32, N_CMP]), ALU.mult))
                    for par in range(2):
                        for t in range(TT):
                            x = Pc[:, par, t, :, 0:N_CMP]
                            ins = V.tensor_tensor(x, x, valid[:, t:t + 1, :].broadcast_to([P, 8, N_CMP]), ALU.mult)
                    ins.then_inc(cmp_ready, 1)
                    attend("mix3")
                    add("out3", ALPHA2)
                layer_norm()
                attend(f"xa{i}")
                if i == 0:
                    for part in range(2):
                        dense_low(0, 0, part)
                add(f"xa{i} out", ALPHA2)
                layer_norm()
                if i == 1:
                    route2()
                    routed_layer("moe2", 1, ALPHA2)
                    layer_norm(acc, counted=False, last=True)
                else:
                    dve.wait_ge(proj_saved, saved("ln5 transposed"))
                    expert_steps("dense", ALPHA2)
                    layer_norm(counted=False)


SMALL_LOADS = ["wff", "foxb", "lam0", "lam1", "lam2", "lam3", "dng", "dng2", "hng", "rw1", "rb1", "rw2", "ckvg", "sinks",
               "wuk", "wuv", "w2k", "w2v"]


class Slots:

    def __init__(self, tensor, at):
        self.tensor, self.at = tensor, at

    def get(self, n):
        self.at += n
        assert self.at <= 400
        return self.tensor[:, self.at - n:self.at]


def kernel(**inputs):
    import concourse.bacc as _bacc
    from concourse.bass_utils import run_bass_kernel_spmd as _run

    nc = _bacc.Bacc("TRN2", target_bir_lowering=False, num_devices=1)
    arrays, args = {}, {}
    named = dict(inputs)
    named["const_wide"], named["const_rows"] = CONST_WIDE, CONST_ROWS
    for name, a in named.items():
        a = np.ascontiguousarray(a)
        arrays[f"in_{name}_dram"] = a
        args[name] = nc.dram_tensor(f"in_{name}_dram", a.shape, mybir.dt.from_np(a.dtype), kind="ExternalInput").ap()
    out = nc.dram_tensor("out_0_dram", (1, T, D), F32, kind="ExternalOutput").ap()
    two_block_kernel(nc, args, out)
    r = _run(nc, [arrays], core_ids=[0])
    return r.results[0]["out_0_dram"]
```
